# Optimizing a Trainium2 kernel written in Bass

```python
import jax, jax.numpy as jnp
from jax import lax
import numpy as np

D_MODEL = 1024
BATCH = 1
SEQ = 256
DEPTH = 1

GRID_W = 64
CTX_LEN = 256
MIX_WIDTH = D_MODEL // 2
HEAD_DIM = 64
GQA_HEADS = MIX_WIDTH // HEAD_DIM
GQA_KV_HEADS = GQA_HEADS // 4
NA_HEADS = MIX_WIDTH // HEAD_DIM
NA_WIN_ROWS = 8
NA_WIN_COLS = 16
FOURIER_WIDTH = MIX_WIDTH
FOURIER_GROUPS = 4
FOURIER_GROUP_DIM = FOURIER_WIDTH // FOURIER_GROUPS
CONV_WIDTH = MIX_WIDTH
CONV_KERNEL = 31
N_BRANCHES = 4
N_EXPERTS = 16
N_EXPERT_GROUPS = 4
EXPERTS_PER_GROUP = N_EXPERTS // N_EXPERT_GROUPS
TOP_K = 2
EXPERT_FF = D_MODEL // 2
Q_BLOCK = 128
ROPE_THETA = 10000.0
EPS = 1e-6
ATTN_SCALE = HEAD_DIM ** -0.5

GQA_Q_WIDTH = GQA_HEADS * HEAD_DIM
GQA_KV_WIDTH = GQA_KV_HEADS * HEAD_DIM
NA_WIDTH = NA_HEADS * HEAD_DIM
PROJ_SIZES = (GQA_Q_WIDTH, GQA_KV_WIDTH, GQA_KV_WIDTH, NA_WIDTH, NA_WIDTH, NA_WIDTH,
              FOURIER_WIDTH, 2 * CONV_WIDTH, N_BRANCHES * D_MODEL)
PROJ_SPLITS = tuple(int(v) for v in np.cumsum(PROJ_SIZES)[:-1])
IN_WIDTH = sum(PROJ_SIZES)


def rms_norm(x, g):
    xf = x.astype(jnp.float32)
    y = xf * lax.rsqrt(jnp.mean(xf * xf, axis=-1, keepdims=True) + EPS)
    return (y * g.astype(jnp.float32)).astype(x.dtype)

def axial_rope(n_tokens):
    t = jnp.arange(n_tokens, dtype=jnp.int32)
    row = (t // GRID_W).astype(jnp.float32)
    col = (t % GRID_W).astype(jnp.float32)
    n_pairs = HEAD_DIM // 4
    inv_freq = ROPE_THETA ** (-jnp.arange(n_pairs, dtype=jnp.float32) / n_pairs)
    ang = jnp.concatenate([row[:, None] * inv_freq, col[:, None] * inv_freq], axis=-1)
    return jnp.cos(ang), jnp.sin(ang)

def apply_rope(x, cos, sin):
    xf = x.astype(jnp.float32).reshape(*x.shape[:-1], HEAD_DIM // 2, 2)
    x1, x2 = xf[..., 0], xf[..., 1]
    c = cos[None, :, None, :]
    s = sin[None, :, None, :]
    return jnp.stack([x1 * c - x2 * s, x1 * s + x2 * c], axis=-1).reshape(x.shape).astype(x.dtype)

def attend(qg, k, v):
    s = jnp.einsum('bqhgd,bkhd->bhgqk', qg, k, preferred_element_type=jnp.float32) * ATTN_SCALE
    p = jax.nn.softmax(s, axis=-1).astype(v.dtype)
    return jnp.einsum('bhgqk,bkhd->bqhgd', p, v)

def dense_attention(q, k, v):
    B, L, hq, _ = q.shape
    hkv = k.shape[2]
    out = attend(q.reshape(B, L, hkv, hq // hkv, HEAD_DIM), k, v)
    return out.reshape(B, L, hq * HEAD_DIM)

def gqa_latent(q, k, v, k_ctx, v_ctx):
    B, S = q.shape[:2]
    g = GQA_HEADS // GQA_KV_HEADS
    k_all = jnp.concatenate([k, k_ctx], axis=1)
    v_all = jnp.concatenate([v, v_ctx], axis=1)
    nb = S // Q_BLOCK
    qb = q.reshape(B, nb, Q_BLOCK, GQA_KV_HEADS, g, HEAD_DIM).transpose(1, 0, 2, 3, 4, 5)
    out = lax.map(lambda qblk: attend(qblk, k_all, v_all), qb)
    return out.transpose(1, 0, 2, 3, 4, 5).reshape(B, S, GQA_Q_WIDTH)

def neighbourhood_latent(q, k, v, k_ctx, v_ctx, rpb):
    B, S = q.shape[:2]
    rows = S // GRID_W
    wr = min(NA_WIN_ROWS, rows)
    qg = q.reshape(B, rows, GRID_W, NA_HEADS, HEAD_DIM)
    kg = k.reshape(B, rows, GRID_W, NA_HEADS, HEAD_DIM)
    vg = v.reshape(B, rows, GRID_W, NA_HEADS, HEAD_DIM)
    cols = np.arange(GRID_W)
    col_start = np.clip(cols - NA_WIN_COLS // 2, 0, GRID_W - NA_WIN_COLS)
    col_idx = col_start[:, None] + np.arange(NA_WIN_COLS)[None, :]
    col_bias_idx = col_idx - cols[:, None] + (NA_WIN_COLS - 1)
    row_starts = jnp.clip(jnp.arange(rows) - NA_WIN_ROWS // 2, 0, rows - wr)
    rpb_f = rpb.astype(jnp.float32)
    n_win = wr * NA_WIN_COLS

    def row_block(args):
        r, r0, q_row = args
        k_band = lax.dynamic_slice_in_dim(kg, r0, wr, axis=1)
        v_band = lax.dynamic_slice_in_dim(vg, r0, wr, axis=1)
        k_win = k_band[:, :, col_idx]
        v_win = v_band[:, :, col_idx]
        s_win = jnp.einsum('bqhd,bwqjhd->bhqwj', q_row, k_win,
                           preferred_element_type=jnp.float32) * ATTN_SCALE
        row_bias_idx = r0 + jnp.arange(wr) - r + (NA_WIN_ROWS - 1)
        bias = rpb_f[:, row_bias_idx][:, :, col_bias_idx]
        s_win = s_win + bias.transpose(0, 2, 1, 3)[None]
        s_ctx = jnp.einsum('bqhd,bkhd->bhqk', q_row, k_ctx,
                           preferred_element_type=jnp.float32) * ATTN_SCALE
        s = jnp.concatenate([s_win.reshape(B, NA_HEADS, GRID_W, n_win), s_ctx], axis=-1)
        p = jax.nn.softmax(s, axis=-1).astype(v.dtype)
        p_win = p[..., :n_win].reshape(B, NA_HEADS, GRID_W, wr, NA_WIN_COLS)
        p_ctx = p[..., n_win:]
        return (jnp.einsum('bhqwj,bwqjhd->bqhd', p_win, v_win)
                + jnp.einsum('bhqk,bkhd->bqhd', p_ctx, v_ctx))

    out = lax.map(row_block, (jnp.arange(rows), row_starts, qg.transpose(1, 0, 2, 3, 4)))
    return out.transpose(1, 0, 2, 3, 4).reshape(B, S, NA_WIDTH)

def fourier_mix(u):
    B, L = u.shape[:2]
    ug = u.astype(jnp.float32).reshape(B, L, FOURIER_GROUPS, FOURIER_GROUP_DIM)
    y = jnp.fft.fft2(ug, axes=(1, 3), norm='ortho').real
    return y.reshape(B, L, FOURIER_WIDTH).astype(u.dtype)

def conformer_conv(u, conv_w, conv_b, conv_g):
    a, b = jnp.split(u, 2, axis=-1)
    z = a * jax.nn.sigmoid(b)
    z = lax.conv_general_dilated(z, conv_w[:, None, :], window_strides=(1,),
                                 padding=[(CONV_KERNEL // 2, CONV_KERNEL // 2)],
                                 dimension_numbers=('NWC', 'WIO', 'NWC'),
                                 feature_group_count=CONV_WIDTH) + conv_b
    return jax.nn.silu(rms_norm(z, conv_g))

def merge_branches(branches, gate_logits, w_branch, w_out):
    y = jnp.stack(branches, axis=-2)
    z = jnp.einsum('blnc,ncd->blnd', y, w_branch)
    g = jax.nn.sigmoid(gate_logits.reshape(*gate_logits.shape[:-1], N_BRANCHES, D_MODEL)
                       .astype(jnp.float32)).astype(z.dtype)
    return jnp.sum(g * z, axis=-2) @ w_out

def token_mixer(h, hc, w_in, q_g, k_g, rpb, conv_w, conv_b, conv_g, w_branch, w_out, cos, sin, update_ctx):
    B, S, _ = h.shape
    C = hc.shape[1]
    gq, gk, gv, nq, nk, nv, fu, cu, gl = jnp.split(h @ w_in, PROJ_SPLITS, axis=-1)
    cgq, cgk, cgv, cnq, cnk, cnv, cfu, ccu, cgl = jnp.split(hc @ w_in, PROJ_SPLITS, axis=-1)
    q = apply_rope(rms_norm(gq.reshape(B, S, GQA_HEADS, HEAD_DIM), q_g), cos, sin)
    k = apply_rope(rms_norm(gk.reshape(B, S, GQA_KV_HEADS, HEAD_DIM), k_g), cos, sin)
    v = gv.reshape(B, S, GQA_KV_HEADS, HEAD_DIM)
    kc = rms_norm(cgk.reshape(B, C, GQA_KV_HEADS, HEAD_DIM), k_g)
    vc = cgv.reshape(B, C, GQA_KV_HEADS, HEAD_DIM)
    y_gqa = gqa_latent(q, k, v, kc, vc)
    nkc = cnk.reshape(B, C, NA_HEADS, HEAD_DIM)
    nvc = cnv.reshape(B, C, NA_HEADS, HEAD_DIM)
    y_na = neighbourhood_latent(nq.reshape(B, S, NA_HEADS, HEAD_DIM), nk.reshape(B, S, NA_HEADS, HEAD_DIM),
                                nv.reshape(B, S, NA_HEADS, HEAD_DIM), nkc, nvc, rpb)
    y_fn = fourier_mix(fu)
    y_cv = conformer_conv(cu, conv_w, conv_b, conv_g)
    out = merge_branches((y_gqa, y_na, y_fn, y_cv), gl, w_branch, w_out)
    if not update_ctx:
        return out, None
    qc = rms_norm(cgq.reshape(B, C, GQA_HEADS, HEAD_DIM), q_g)
    yc_gqa = dense_attention(qc, kc, vc)
    yc_na = dense_attention(cnq.reshape(B, C, NA_HEADS, HEAD_DIM), nkc, nvc)
    yc_fn = fourier_mix(cfu)
    yc_cv = conformer_conv(ccu, conv_w, conv_b, conv_g)
    out_c = merge_branches((yc_gqa, yc_na, yc_fn, yc_cv), cgl, w_branch, w_out)
    return out, out_c

def moe(h, w_router, router_bias, w_gu, w_down):
    lead = h.shape[:-1]
    t = h.reshape(-1, D_MODEL)
    scores = jax.nn.sigmoid((t @ w_router).astype(jnp.float32))
    sel = scores + router_bias.astype(jnp.float32)
    group_score = lax.top_k(sel.reshape(-1, N_EXPERT_GROUPS, EXPERTS_PER_GROUP), TOP_K)[0].sum(-1)
    g_idx = jnp.argmax(group_score, axis=-1)
    in_group = (jnp.arange(N_EXPERTS) // EXPERTS_PER_GROUP)[None, :] == g_idx[:, None]
    _, top_idx = lax.top_k(jnp.where(in_group, sel, -jnp.inf), TOP_K)
    w = jnp.take_along_axis(scores, top_idx, axis=-1)
    w = w / jnp.sum(w, axis=-1, keepdims=True)
    gate = jnp.sum(jax.nn.one_hot(top_idx, N_EXPERTS, dtype=jnp.float32) * w[..., None], axis=1).astype(t.dtype)
    out = jnp.zeros_like(t)
    for e in range(N_EXPERTS):
        a, b = jnp.split(t @ w_gu[e], 2, axis=-1)
        out = out + gate[:, e:e + 1] * ((jax.nn.silu(a) * b) @ w_down[e])
    return out.reshape(*lead, D_MODEL)

def first_inputs(seed: int = 0) -> dict:
    key = jax.random.key(seed)
    ks = jax.random.split(key, 22)
    D = D_MODEL

    def nrm(k, shape, std):
        return jax.random.normal(k, shape, jnp.float32) * std

    return {
        "x": nrm(ks[0], (BATCH, SEQ, D), 1.0),
        "c": nrm(ks[1], (BATCH, D), 1.0),
        "ctx": nrm(ks[2], (BATCH, CTX_LEN, D), 1.0),
        "c_ctx": nrm(ks[3], (D,), 1.0),
        "w_mod": nrm(ks[4], (DEPTH, D, 6 * D), 0.5 * D ** -0.5),
        "b_mod": nrm(ks[5], (DEPTH, 6 * D), 0.02),
        "norm1_g": 1.0 + nrm(ks[6], (DEPTH, D), 0.02),
        "norm2_g": 1.0 + nrm(ks[7], (DEPTH, D), 0.02),
        "w_in": nrm(ks[8], (DEPTH, D, IN_WIDTH), D ** -0.5),
        "q_norm_g": 1.0 + nrm(ks[9], (DEPTH, HEAD_DIM), 0.02),
        "k_norm_g": 1.0 + nrm(ks[10], (DEPTH, HEAD_DIM), 0.02),
        "na_rpb": nrm(ks[11], (DEPTH, NA_HEADS, 2 * NA_WIN_ROWS - 1, 2 * NA_WIN_COLS - 1), 0.02),
        "conv_w": nrm(ks[12], (DEPTH, CONV_KERNEL, CONV_WIDTH), CONV_KERNEL ** -0.5),
        "conv_b": nrm(ks[13], (DEPTH, CONV_WIDTH), 0.01),
        "conv_norm_g": 1.0 + nrm(ks[14], (DEPTH, CONV_WIDTH), 0.02),
        "w_branch": nrm(ks[15], (DEPTH, N_BRANCHES, MIX_WIDTH, D), MIX_WIDTH ** -0.5),
        "w_out": nrm(ks[16], (DEPTH, D, D), D ** -0.5),
        "w_router": nrm(ks[17], (D, N_EXPERTS), D ** -0.5),
        "router_bias": nrm(ks[18], (N_EXPERTS,), 0.01),
        "w_expert_gu": nrm(ks[19], (DEPTH, N_EXPERTS, D, 2 * EXPERT_FF), D ** -0.5),
        "w_expert_down": nrm(ks[20], (DEPTH, N_EXPERTS, EXPERT_FF, D), EXPERT_FF ** -0.5),
        "final_norm_g": 1.0 + nrm(ks[21], (D,), 0.02),
    }

def first_block(x, c, ctx, c_ctx, w_mod, b_mod, norm1_g, norm2_g, w_in, q_norm_g, k_norm_g, na_rpb,
              conv_w, conv_b, conv_norm_g, w_branch, w_out, w_router, router_bias,
              w_expert_gu, w_expert_down, final_norm_g):
    S = x.shape[1]
    cos, sin = axial_rope(S)
    xc = ctx
    for l in range(DEPTH):
        update_ctx = l < DEPTH - 1
        m = jax.nn.silu(c) @ w_mod[l] + b_mod[l]
        sh1, sc1, g1, sh2, sc2, g2 = [t[:, None, :] for t in jnp.split(m, 6, axis=-1)]
        mc = jax.nn.silu(c_ctx) @ w_mod[l] + b_mod[l]
        csh1, csc1, cg1, csh2, csc2, cg2 = jnp.split(mc, 6, axis=-1)
        h = rms_norm(x, norm1_g[l]) * (1.0 + sc1) + sh1
        hc = rms_norm(xc, norm1_g[l]) * (1.0 + csc1) + csh1
        y, yc = token_mixer(h, hc, w_in[l], q_norm_g[l], k_norm_g[l], na_rpb[l], conv_w[l], conv_b[l],
                            conv_norm_g[l], w_branch[l], w_out[l], cos, sin, update_ctx)
        x = x + g1 * y
        h2 = rms_norm(x, norm2_g[l]) * (1.0 + sc2) + sh2
        if update_ctx:
            xc = xc + cg1 * yc
            h2c = rms_norm(xc, norm2_g[l]) * (1.0 + csc2) + csh2
            z = moe(jnp.concatenate([h2, h2c], axis=1), w_router, router_bias, w_expert_gu[l], w_expert_down[l])
            x = x + g2 * z[:, :S]
            xc = xc + cg2 * z[:, S:]
        else:
            x = x + g2 * moe(h2, w_router, router_bias, w_expert_gu[l], w_expert_down[l])
    return rms_norm(x, final_norm_g)


DEPTH_2 = 2

N_HEADS = D_MODEL // HEAD_DIM
N_A = max(1, DEPTH_2 // 2)
N_B = DEPTH_2 - N_A
DECAY_LORA = 64
AAA_LORA = 64
MV_LORA = 32
GATE_LORA = 160
N_GROUPS = 4
EXP_PER_GROUP = 8
N_EXPERTS_2 = N_GROUPS * EXP_PER_GROUP
D_EXPERT = 512
EXPERT_BLOCK = 128
DEEPNORM_ALPHA = (2 * DEPTH_2) ** 0.25
DEEPNORM_BETA = (8 * DEPTH_2) ** -0.25
LN_EPS = 1e-5
GN_EPS = 64e-5
QK_EPS = 1e-6


def layer_norm(x, g, b, eps=LN_EPS):
    xf = x.astype(jnp.float32)
    mu = xf.mean(-1, keepdims=True)
    var = jnp.square(xf - mu).mean(-1, keepdims=True)
    return ((xf - mu) * lax.rsqrt(var + eps)).astype(x.dtype) * g + b

def head_rms(t, g, eps=QK_EPS):
    tf = t.astype(jnp.float32)
    return (tf * lax.rsqrt(jnp.mean(tf * tf, -1, keepdims=True) + eps)).astype(t.dtype) * g

def wkv7_scan(r, w, k, v, a, b):
    B, S, H, N = r.shape

    def step(state, inp):
        r_t, w_t, k_t, v_t, a_t, b_t = inp
        sa = jnp.einsum('bhij,bhj->bhi', state, a_t)
        state = (state * w_t[:, :, None, :] + sa[..., None] * b_t[:, :, None, :]
                 + v_t[..., None] * k_t[:, :, None, :])
        return state, jnp.einsum('bhij,bhj->bhi', state, r_t)

    tm = lambda t: jnp.moveaxis(t, 1, 0)
    state0 = jnp.zeros((B, H, N, N), jnp.float32)
    _, y = lax.scan(step, state0, (tm(r), tm(w), tm(k), tm(v), tm(a), tm(b)))
    return jnp.moveaxis(y, 0, 1)

def rwkv7_time_mix(h, v_first, mu, w_rkv, w0, w1, w2, a0, a1, a2, g1, g2,
                   k_k, k_a, r_k, gn_g, gn_b, w_o, v_mix):
    B, S, D = h.shape
    f32 = jnp.float32
    xx = jnp.pad(h, ((0, 0), (1, 0), (0, 0)))[:, :-1] - h
    xr, xw, xk, xv, xa, xg = [h + xx * mu[i] for i in range(6)]
    r, k, v = jnp.einsum('nbsd,nde->nbse', jnp.stack([xr, xk, xv]), w_rkv)
    w_log = -jnp.exp((-jax.nn.softplus(-(w0 + jnp.tanh(xw @ w1) @ w2)) - 0.5).astype(f32))
    if v_mix is None:
        v_first = v
    else:
        v0, v1, v2 = v_mix
        v = v + (v_first - v) * jax.nn.sigmoid(v0 + (xv @ v1) @ v2)
    a = jax.nn.sigmoid(a0 + (xa @ a1) @ a2)
    g = jax.nn.sigmoid(xg @ g1) @ g2
    heads = lambda t: t.reshape(B, S, N_HEADS, HEAD_DIM).astype(f32)
    kk = heads(k * k_k)
    kk = kk / jnp.maximum(jnp.sqrt(jnp.sum(kk * kk, -1, keepdims=True)), 1e-12)
    k = k * (1 + (a - 1) * k_a)
    rh, kh, vh, ah = heads(r), heads(k), heads(v), heads(a)
    y = wkv7_scan(rh, jnp.exp(heads(w_log)), kh, vh, -kk, kk * ah)
    ym = y.mean(-1, keepdims=True)
    yv = jnp.square(y - ym).mean(-1, keepdims=True)
    y = ((y - ym) * lax.rsqrt(yv + GN_EPS)).reshape(B, S, D).astype(h.dtype) * gn_g + gn_b
    bonus = (jnp.sum(rh * kh * r_k, -1, keepdims=True) * vh).reshape(B, S, D).astype(h.dtype)
    return ((y + bonus) * g) @ w_o, v_first

def shared_kv(x, cs, ada_w, ada_b, w_kvf, b_f, k_norm):
    B, S, D = x.shape
    shift, scale = jnp.split(cs @ ada_w + ada_b, 2, axis=-1)
    hk = x * (1 + scale[:, None]) + shift[:, None]
    kvf = hk @ w_kvf
    k = head_rms(kvf[..., :D].reshape(B, S, N_HEADS, HEAD_DIM), k_norm)
    v = kvf[..., D:2 * D].reshape(B, S, N_HEADS, HEAD_DIM)
    log_f = jax.nn.log_sigmoid((kvf[..., 2 * D:] + b_f).astype(jnp.float32))
    fcum = jnp.cumsum(log_f, axis=1)
    return (k.transpose(0, 2, 1, 3), v.transpose(0, 2, 1, 3), fcum.transpose(0, 2, 1))

def forgetting_attention(q, k, v, fcum):
    S = q.shape[2]
    scale = HEAD_DIM ** -0.5
    outs = []
    for i in range(S // Q_BLOCK):
        lo, hi = i * Q_BLOCK, (i + 1) * Q_BLOCK
        logits = (jnp.einsum('bhqd,bhkd->bhqk', q[:, :, lo:hi], k[:, :, :hi]).astype(jnp.float32) * scale
                  + (fcum[:, :, lo:hi, None] - fcum[:, :, None, :hi]))
        causal = (lo + jnp.arange(Q_BLOCK))[:, None] >= jnp.arange(hi)[None, :]
        logits = jnp.where(causal, logits, -jnp.inf)
        p = jax.nn.softmax(logits, axis=-1).astype(v.dtype)
        outs.append(jnp.einsum('bhqk,bhkd->bhqd', p, v[:, :, :hi]))
    return jnp.concatenate(outs, axis=2)

def fox_layer(h, kv, w_qg, q_norm, w_o):
    B, S, D = h.shape
    k, v, fcum = kv
    qg = h @ w_qg
    q = head_rms(qg[..., :D].reshape(B, S, N_HEADS, HEAD_DIM), q_norm).transpose(0, 2, 1, 3)
    o = forgetting_attention(q, k, v, fcum).transpose(0, 2, 1, 3).reshape(B, S, D)
    return (o * jax.nn.sigmoid(qg[..., D:])) @ w_o

def grouped_experts(xf, expert_idx, gates, w_gate, w_up, w_down):
    T, D = xf.shape
    A = T * TOP_K
    n_blocks = -(-(A + N_EXPERTS_2 * EXPERT_BLOCK) // EXPERT_BLOCK)
    n_slots = n_blocks * EXPERT_BLOCK
    flat_e = expert_idx.reshape(A)
    order = jnp.argsort(flat_e)
    sorted_e = flat_e[order]
    counts = jnp.bincount(flat_e, length=N_EXPERTS_2)
    padded = (counts + EXPERT_BLOCK - 1) // EXPERT_BLOCK * EXPERT_BLOCK
    pad_end = jnp.cumsum(padded)
    pad_start = pad_end - padded
    start = jnp.cumsum(counts) - counts
    dest_sorted = pad_start[sorted_e] + (jnp.arange(A) - start[sorted_e])
    dest = jnp.zeros((A,), jnp.int32).at[order].set(dest_sorted.astype(jnp.int32))
    slot_tok = jnp.zeros((n_slots,), jnp.int32).at[dest].set(jnp.arange(A, dtype=jnp.int32) // TOP_K)
    block_exp = jnp.minimum(jnp.searchsorted(pad_end, jnp.arange(n_blocks) * EXPERT_BLOCK, side='right'),
                            N_EXPERTS_2 - 1)
    xs = xf[slot_tok].reshape(n_blocks, EXPERT_BLOCK, D)

    def one_block(args):
        xb, e = args
        hb = jax.nn.silu(xb @ w_gate[e]) * (xb @ w_up[e])
        return hb @ w_down[e]

    ys = lax.map(one_block, (xs, block_exp)).reshape(n_slots, D)
    y_assign = ys[dest].reshape(T, TOP_K, D)
    return jnp.einsum('tk,tkd->td', gates, y_assign)

def hier_moe(h, w_grp, b_grp, w_exp, b_exp, w_gate, w_up, w_down):
    B, S, D = h.shape
    T = B * S
    hf = h.reshape(T, D)
    p_grp = jax.nn.softmax((hf @ w_grp).astype(jnp.float32) + b_grp, axis=-1)
    g_sel = jnp.argmax(p_grp, axis=-1)
    p_g = jnp.take_along_axis(p_grp, g_sel[:, None], axis=-1)
    e_logits = ((hf @ w_exp).astype(jnp.float32) + b_exp).reshape(T, N_GROUPS, EXP_PER_GROUP)
    e_logits = jnp.take_along_axis(e_logits, g_sel[:, None, None], axis=1)[:, 0]
    top_p, top_i = lax.top_k(jax.nn.softmax(e_logits, axis=-1), TOP_K)
    gates = (p_g * top_p / jnp.sum(top_p, -1, keepdims=True)).astype(h.dtype)
    expert_idx = (g_sel[:, None] * EXP_PER_GROUP + top_i).astype(jnp.int32)
    return grouped_experts(hf, expert_idx, gates, w_gate, w_up, w_down).reshape(B, S, D)

def second_inputs(seed: int = 0) -> dict:
    key = jax.random.key(seed)
    ks = iter(jax.random.split(key, 64))
    nrm = lambda shape, s: jax.random.normal(next(ks), shape, jnp.float32) * s
    uni = lambda shape, lo, hi: jax.random.uniform(next(ks), shape, jnp.float32, lo, hi)
    D, H, N = D_MODEL, N_HEADS, HEAD_DIM
    s_in = D ** -0.5
    beta = DEEPNORM_BETA
    nv = N_A - 1
    return {
        'x': nrm((BATCH, SEQ, D), 1.0),
        'c': nrm((BATCH, D), 1.0),
        'ada_w': nrm((DEPTH_2, D, 6 * D), 0.1 * s_in),
        'ada_b': nrm((DEPTH_2, 6 * D), 0.01),
        'ln_g': 1.0 + nrm((DEPTH_2, 2, D), 0.02),
        'ln_b': nrm((DEPTH_2, 2, D), 0.02),
        'rw_mu': uni((N_A, 6, D), 0.0, 1.0),
        'rw_rkv': nrm((N_A, 3, D, D), s_in) * jnp.array([1.0, 1.0, beta], jnp.float32)[None, :, None, None],
        'rw_w0': uni((N_A, D), -6.0, -1.0),
        'rw_w1': nrm((N_A, D, DECAY_LORA), s_in),
        'rw_w2': nrm((N_A, DECAY_LORA, D), 0.1 * DECAY_LORA ** -0.5),
        'rw_a0': nrm((N_A, D), 0.1),
        'rw_a1': nrm((N_A, D, AAA_LORA), s_in),
        'rw_a2': nrm((N_A, AAA_LORA, D), 0.1 * AAA_LORA ** -0.5),
        'rw_g1': nrm((N_A, D, GATE_LORA), s_in),
        'rw_g2': nrm((N_A, GATE_LORA, D), GATE_LORA ** -0.5),
        'rw_kk': 0.85 + nrm((N_A, D), 0.02),
        'rw_ka': 1.0 + nrm((N_A, D), 0.02),
        'rw_rk': nrm((N_A, H, N), 0.1),
        'rw_gn_g': 1.0 + nrm((N_A, D), 0.02),
        'rw_gn_b': nrm((N_A, D), 0.02),
        'rw_wo': nrm((N_A, D, D), s_in * beta),
        'rw_v0': 1.0 + nrm((nv, D), 0.1),
        'rw_v1': nrm((nv, D, MV_LORA), s_in),
        'rw_v2': nrm((nv, MV_LORA, D), 0.1 * MV_LORA ** -0.5),
        'kv_ada_w': nrm((D, 2 * D), 0.1 * s_in),
        'kv_ada_b': nrm((2 * D,), 0.01),
        'kv_w': jnp.concatenate([nrm((D, D), s_in), nrm((D, D), s_in * beta), nrm((D, H), s_in)], axis=1),
        'kv_fb': uni((H,), 0.0, 5.0),
        'kv_knorm': 1.0 + nrm((N,), 0.02),
        'fx_wqg': nrm((N_B, D, 2 * D), s_in),
        'fx_qnorm': 1.0 + nrm((N_B, N), 0.02),
        'fx_wo': nrm((N_B, D, D), s_in * beta),
        'moe_wgrp': nrm((DEPTH_2, D, N_GROUPS), s_in),
        'moe_bgrp': nrm((DEPTH_2, N_GROUPS), 0.01),
        'moe_wexp': nrm((DEPTH_2, D, N_EXPERTS_2), s_in),
        'moe_bexp': nrm((DEPTH_2, N_EXPERTS_2), 0.01),
        'moe_wgate': nrm((DEPTH_2, N_EXPERTS_2, D, D_EXPERT), s_in),
        'moe_wup': nrm((DEPTH_2, N_EXPERTS_2, D, D_EXPERT), s_in),
        'moe_wdown': nrm((DEPTH_2, N_EXPERTS_2, D_EXPERT, D), D_EXPERT ** -0.5 * beta),
    }

def second_block(x, c, ada_w, ada_b, ln_g, ln_b, rw_mu, rw_rkv, rw_w0, rw_w1, rw_w2, rw_a0, rw_a1, rw_a2,
              rw_g1, rw_g2, rw_kk, rw_ka, rw_rk, rw_gn_g, rw_gn_b, rw_wo, rw_v0, rw_v1, rw_v2,
              kv_ada_w, kv_ada_b, kv_w, kv_fb, kv_knorm, fx_wqg, fx_qnorm, fx_wo,
              moe_wgrp, moe_bgrp, moe_wexp, moe_bexp, moe_wgate, moe_wup, moe_wdown):
    cs = jax.nn.silu(c)
    kv = None
    v_first = None
    for l in range(DEPTH_2):
        mod = cs @ ada_w[l] + ada_b[l]
        sh_m, sc_m, gt_m, sh_f, sc_f, gt_f = [m[:, None, :] for m in jnp.split(mod, 6, axis=-1)]
        h = x * (1 + sc_m) + sh_m
        if l < N_A:
            v_mix = None if l == 0 else (rw_v0[l - 1], rw_v1[l - 1], rw_v2[l - 1])
            y, v_first = rwkv7_time_mix(h, v_first, rw_mu[l], rw_rkv[l], rw_w0[l], rw_w1[l], rw_w2[l],
                                        rw_a0[l], rw_a1[l], rw_a2[l], rw_g1[l], rw_g2[l], rw_kk[l],
                                        rw_ka[l], rw_rk[l], rw_gn_g[l], rw_gn_b[l], rw_wo[l], v_mix)
        else:
            j = l - N_A
            y = fox_layer(h, kv, fx_wqg[j], fx_qnorm[j], fx_wo[j])
        x = layer_norm(DEEPNORM_ALPHA * x + (1 + gt_m) * y, ln_g[l, 0], ln_b[l, 0])
        h = x * (1 + sc_f) + sh_f
        y = hier_moe(h, moe_wgrp[l], moe_bgrp[l], moe_wexp[l], moe_bexp[l],
                     moe_wgate[l], moe_wup[l], moe_wdown[l])
        x = layer_norm(DEEPNORM_ALPHA * x + (1 + gt_f) * y, ln_g[l, 1], ln_b[l, 1])
        if l == N_A - 1:
            kv = shared_kv(x, cs, kv_ada_w, kv_ada_b, kv_w, kv_fb, kv_knorm)
    return x


def setup_inputs(seed=0):
    out = dict(first_inputs(seed))
    for name, value in second_inputs(seed + 1).items():
        if name != "x":
            out[name + "_2"] = value
    return out


def reference(
    x, c, ctx, c_ctx, w_mod, b_mod, norm1_g, norm2_g, w_in, q_norm_g, k_norm_g, na_rpb, conv_w,
    conv_b, conv_norm_g, w_branch, w_out, w_router, router_bias, w_expert_gu, w_expert_down,
    final_norm_g, c_2, ada_w_2, ada_b_2, ln_g_2, ln_b_2, rw_mu_2, rw_rkv_2, rw_w0_2, rw_w1_2,
    rw_w2_2, rw_a0_2, rw_a1_2, rw_a2_2, rw_g1_2, rw_g2_2, rw_kk_2, rw_ka_2, rw_rk_2, rw_gn_g_2,
    rw_gn_b_2, rw_wo_2, rw_v0_2, rw_v1_2, rw_v2_2, kv_ada_w_2, kv_ada_b_2, kv_w_2, kv_fb_2,
    kv_knorm_2, fx_wqg_2, fx_qnorm_2, fx_wo_2, moe_wgrp_2, moe_bgrp_2, moe_wexp_2, moe_bexp_2,
    moe_wgate_2, moe_wup_2, moe_wdown_2,
):
    x = first_block(
        x, c, ctx, c_ctx, w_mod, b_mod, norm1_g, norm2_g, w_in, q_norm_g, k_norm_g, na_rpb,
        conv_w, conv_b, conv_norm_g, w_branch, w_out, w_router, router_bias, w_expert_gu,
        w_expert_down, final_norm_g,
    )
    return second_block(
        x, c_2, ada_w_2, ada_b_2, ln_g_2, ln_b_2, rw_mu_2, rw_rkv_2, rw_w0_2, rw_w1_2, rw_w2_2,
        rw_a0_2, rw_a1_2, rw_a2_2, rw_g1_2, rw_g2_2, rw_kk_2, rw_ka_2, rw_rk_2, rw_gn_g_2,
        rw_gn_b_2, rw_wo_2, rw_v0_2, rw_v1_2, rw_v2_2, kv_ada_w_2, kv_ada_b_2, kv_w_2, kv_fb_2,
        kv_knorm_2, fx_wqg_2, fx_qnorm_2, fx_wo_2, moe_wgrp_2, moe_bgrp_2, moe_wexp_2,
        moe_bexp_2, moe_wgate_2, moe_wup_2, moe_wdown_2,
    )


_drawn_inputs = setup_inputs


def setup_inputs(seed=0):
    import zlib

    import numpy as np

    out = dict(_drawn_inputs(seed))
    spreads = {}
    factors = {'norm1_g': 4.086,
     'q_norm_g': 4.741,
     'k_norm_g': 8.0,
     'na_rpb': 8.0,
     'conv_b': 4.76,
     'conv_norm_g': 6.525,
     'ada_b_2': 3.993,
     'rw_w1_2': 8.0,
     'rw_w2_2': 8.0,
     'rw_a0_2': 5.172,
     'rw_a1_2': 5.127,
     'rw_a2_2': 4.966,
     'rw_kk_2': 8.0,
     'rw_ka_2': 8.0,
     'rw_gn_g_2': 7.905,
     'rw_gn_b_2': 6.078,
     'kv_ada_w_2': 7.07,
     'kv_ada_b_2': 8.0,
     'kv_knorm_2': 33.1,
     'fx_qnorm_2': 33.011,
     'moe_bgrp_2': 7.682,
     'moe_bexp_2': 5.97}
    for name, (base, spread) in spreads.items():
        noise = np.random.default_rng([zlib.crc32(name.encode()), seed]).standard_normal(out[name].shape)
        drawn = base * np.exp(spread * noise) if base else spread * noise
        out[name] = __import__('jax').numpy.asarray(drawn.astype(out[name].dtype))
    for name, factor in factors.items():
        out[name] = (out[name] * factor).astype(out[name].dtype)
    return out
```

```python
from contextlib import ExitStack

import numpy as np

import concourse.bass as bass
from concourse import mybir

F32 = mybir.dt.float32
ALU = mybir.AluOpType
ACT = mybir.ActivationFunctionType
AX = mybir.AxisListType

P = 128
D = 1024
T = 256
TT = T // P
KT = D // P
HD = 64
BIG = 1e30
CH = 32
NCH = T // CH
CAP = 64
N_HEADS = D // HD
GRID_W = 64
ALPHA = 4.0 ** 0.25

CONST = {}
_at = 0
for _name, _width in (("ident", 128), ("cos", 64), ("sin", 64), ("window", 64), ("reverse", 128), ("before", 128), ("slot", 128), ("causal", 128), ("tri", 64), ("restart", 256),
                      ("halves", 128), ("half2", 2), ("first4", 4), ("first32", 32),
                      ("cs_group", 256), ("cos_seq", 512), ("sin_seq", 512)):
    CONST[_name] = (_at, _width)
    _at += _width
CONST_WIDTH = _at
KEPT_WIDTH = CONST["cs_group"][0]


def shape_constants():
    c = np.zeros((P, CONST_WIDTH), np.float32)

    def put(name, a):
        at, width = CONST[name]
        c[:, at:at + width] = np.asarray(a, np.float32).reshape(P, width)

    p = np.arange(P)
    put("ident", np.eye(P))
    t = np.arange(T)
    inv = (np.float32(10000.0) ** (-np.arange(16, dtype=np.float32) / np.float32(16))).astype(np.float32)
    row, col = (t // GRID_W).astype(np.float32), (t % GRID_W).astype(np.float32)
    ang = np.concatenate([row[:, None] * inv, col[:, None] * inv], axis=1).astype(np.float32)
    rows = lambda a: a.reshape(TT, P, -1).transpose(1, 0, 2)
    put("cos", rows(np.cos(ang)))
    put("sin", rows(np.sin(ang)))
    ag = 2 * np.pi * ((p[:, None] * p[None, :]) % P) / P
    put("cs_group", np.concatenate([np.cos(ag), np.sin(ag)], axis=1))
    al = 2 * np.pi * ((t[:, None] * t[None, :]) % T) / T
    norm = 1.0 / np.sqrt(T * P)
    put("cos_seq", rows(np.cos(al) * norm))
    put("sin_seq", rows(-np.sin(al) * norm))
    w = np.arange(GRID_W)
    start = np.clip(w - 8, 0, GRID_W - 16)
    inside = (w[None, :] >= start[:, None]) & (w[None, :] < start[:, None] + 16)
    put("window", np.tile(np.where(inside, 0.0, -BIG)[::-1], (2, 1)))
    put("reverse", np.kron(np.eye(2), np.eye(GRID_W)[::-1]))
    put("causal", np.where(p[None, :] <= p[:, None], 0.0, -BIG))
    s, u = np.arange(P) % CH, np.arange(CH)
    put("tri", np.concatenate([s[:, None] < u[None, :], s[:, None] <= u[None, :]], axis=1))
    put("restart", np.tile((t % CH != 0).astype(np.float32), (P, 1)))
    put("halves", (p[:, None] // HD) == (p[None, :] // HD))
    put("half2", (p[:, None] // HD) == np.arange(2)[None, :])
    put("before", p[:, None] < p[None, :])
    put("slot", np.tile(p % CAP, (P, 1)))
    put("first4", np.tile(4.0 - np.arange(4), (P, 1)))
    put("first32", np.tile(32.0 - np.arange(32), (P, 1)))
    return c


class Buffer:

    def __init__(self, t):
        self.t = t
        self.readers = []

    def free(self):
        said, self.readers = self.readers, []
        return said


class Ring:

    def __init__(self, tensors):
        self.buffers = [Buffer(t) for t in tensors]
        self.n = 0

    def next(self):
        b = self.buffers[self.n % len(self.buffers)]
        self.n += 1
        return b


class Program:

    COMPUTE = ("tensor", "vector", "scalar", "gpsimd")

    def __init__(self, nc, stack, slots):
        self.nc, self.stack = nc, stack
        self.queue = {e: [] for e in (*self.COMPUTE, "sync")}
        self.done = {e: stack.enter_context(nc.semaphore(f"{e}_done")) for e in self.COMPUTE}
        self.count = dict.fromkeys(self.COMPUTE, 0)
        self.last = {}
        self.seen = {}
        self.floor = {e: [] for e in self.queue}
        self.lanes = {e: [[stack.enter_context(nc.semaphore(f"{e}_dma{i}")), 0] for i in range(n)]
                      for e, n in (("gpsimd", 16), ("scalar", 16))}
        self.lane = dict.fromkeys(self.lanes, 0)
        self.banks = Ring([stack.enter_context(nc.psum_tensor(f"bank{i}", [P, 512], F32)) for i in range(8)])
        self.memory = stack.enter_context(nc.sbuf_tensor("weights", [P, slots, 4096], F32))
        self.slots = Ring([self.memory[:, i, :] for i in range(slots)])
        self.landed = {}
        for i, b in enumerate(self.slots.buffers):
            self.landed[b] = [stack.enter_context(nc.semaphore(f"weights{i}_landed")), 0]

    def wait(self, engine, tokens):
        for token in tokens:
            if token is None:
                continue
            sem, value = token
            key = (engine, sem.name)
            if self.seen.get(key, 0) < value:
                self.seen[key] = value
                self.queue[engine].append(("wait", sem, value))

    def put(self, engine, call, *args, after=(), signal=True, chain=True, **kw):
        self.wait(engine, self.floor[engine])
        self.floor[engine] = []
        self.wait(engine, after)
        if chain:
            self.wait(engine, [self.last.get(engine)])
        token = None
        if signal:
            self.count[engine] += 1
            token = (self.done[engine], self.count[engine])
            self.last[engine] = token
        self.queue[engine].append(("do", call, args, kw, (self.done[engine], 1) if signal else None))
        return token

    def V(self, call, *args, **kw):
        return self.put("vector", call, *args, **kw)

    def S(self, *args, **kw):
        return self.put("scalar", self.nc.scalar.activation, *args, **kw)

    def G(self, call, *args, **kw):
        return self.put("gpsimd", call, *args, **kw)

    def dma(self, out, in_, after=(), engine="gpsimd"):
        lane = self.lanes[engine][self.lane[engine] % len(self.lanes[engine])]
        self.lane[engine] += 1
        self.wait(engine, self.floor[engine])
        self.floor[engine] = []
        self.wait(engine, after)
        if lane[1]:
            self.wait(engine, [(lane[0], lane[1])])
        lane[1] += 16
        call = self.nc.gpsimd.dma_start if engine == "gpsimd" else self.nc.scalar.dma_start
        self.queue[engine].append(("do", call, (out, in_), {}, (lane[0], 16)))
        return lane[0], lane[1]

    def transfers(self):
        return [(lane[0], lane[1]) for lanes in self.lanes.values() for lane in lanes if lane[1]]

    def barrier(self):
        tokens = list(self.last.values()) + self.transfers()
        for e in self.COMPUTE:
            self.floor[e] = list(tokens)

    def product(self, bank, out, pairs, after=(), **kw):
        after = [*bank.free(), *after]
        token = None
        for i, (lhsT, rhs) in enumerate(pairs):
            token = self.put("tensor", self.nc.tensor.matmul, out, lhsT, rhs, start=i == 0,
                             stop=i == len(pairs) - 1, after=after, chain=False,
                             signal=i == len(pairs) - 1, **kw)
            after = ()
        return token

    def turn(self, bank, out, in_, ident, after=(), signal=True):
        return self.put("tensor", self.nc.tensor.transpose, out, in_, ident,
                        after=[*bank.free(), *after], chain=False, signal=signal)

    def weights(self, src, n):
        b = self.slots.next()
        kt = src.shape[0] // P
        view = b.t[:, 0:kt * n].rearrange("p (k n) -> p k n", n=n)
        self.wait("sync", b.free())
        landed = self.landed[b]
        landed[1] += 16
        self.queue["sync"].append(("do", self.nc.sync.dma_start,
                                   (view, src.rearrange("(k p) n -> p k n", p=P)), {}, (landed[0], 16)))
        return b, view, (landed[0], landed[1])

    def weight_pair(self, srcs):
        i = self.slots.n % len(self.slots.buffers)
        got = [self.weights(w, 512) for w in srcs]
        return [g[0] for g in got], self.memory[:, i:i + 2, :].rearrange("p w (k n) -> p k w n", n=512), \
            [g[2] for g in got]

    def align(self, n):
        while self.slots.n % n:
            self.slots.n += 1

    def branch(self, flag, body):
        engines = ("tensor", "vector", "scalar", "sync")
        for e in engines:
            self.wait(e, self.floor[e])
            self.floor[e] = []
        outer = {e: self.queue[e] for e in engines}
        seen, counts = dict(self.seen), dict(self.count)
        landed = {b: l[1] for b, l in self.landed.items()}
        for e in engines:
            self.queue[e] = []
        body()
        for e in engines:
            inner, skipped = self.queue[e], []
            if e == "sync":
                for b, l in self.landed.items():
                    if l[1] > landed[b]:
                        if landed[b]:
                            skipped.append(("wait", l[0], landed[b]))
                        skipped.append(("inc", l[0], l[1] - landed[b]))
            elif self.count[e] > counts[e]:
                skipped += [("wait", self.done[e], counts[e]), ("inc", self.done[e], self.count[e] - counts[e])]
            self.queue[e] = outer[e]
            self.queue[e].append(("branch", flag, inner, skipped))
        self.seen = seen

    def emit(self, block):
        def run(eng, queue):
            for step in queue:
                if step[0] == "wait":
                    eng.wait_ge(step[1], step[2])
                elif step[0] == "inc":
                    eng.sem_inc(step[1], step[2])
                elif step[0] == "branch":
                    for taken in (False, True):
                        flag = eng.value_load(step[1], min_val=0, max_val=1)
                        with eng.If(flag != 0) if taken else eng.If(flag == 0):
                            run(eng, step[2] if taken else step[3])
                else:
                    _, call, args, kw, signal = step
                    ins = call(*args, **kw)
                    if signal:
                        ins.then_inc(*signal)

        @block.sync
        def _(eng):
            run(eng, self.queue["sync"])

        @block.gpsimd
        def _(eng):
            run(eng, self.queue["gpsimd"])

        @block.scalar
        def _(eng):
            run(eng, self.queue["scalar"])

        @block.tensor
        def _(eng):
            run(eng, self.queue["tensor"])

        @block.vector
        def _(eng):
            run(eng, self.queue["vector"])


def pipeline(n, stages):
    for i in range(n + len(stages) - 1):
        for j, stage in enumerate(stages):
            if 0 <= i - j < n:
                stage(i - j)


class Model:

    def __init__(self, nc, stack, inputs, consts, out, debug=None):
        self.nc, self.A, self.out, self.debug = nc, inputs, out, debug or {}
        self.p = Program(nc, stack, 6)
        self.stack = stack
        self.names = 0
        v = nc.vector
        self.tt, self.ts, self.stt, self.cp = v.tensor_tensor, v.tensor_scalar, v.scalar_tensor_tensor, v.tensor_copy
        self.consts = self.sb(stack, "consts", [P, KEPT_WIDTH])
        self.all_consts = consts
        self.ones = self.sb(stack, "ones", [P, P])
        self.x = self.sb(stack, "x_rows", [P, TT, D])
        self.flags = [stack.enter_context(nc.sbuf_tensor(f"more_rounds{i}", [P, T // CAP * n], mybir.dt.int32))
                      for i, n in enumerate((32, 32, 16))]
        self.mod = nc.dram_tensor("mod_rows", (5, 6 * D), F32, kind="Internal").ap()
        self.v_dram = nc.dram_tensor("v_rows", (T, D), F32, kind="Internal").ap()
        self.y_dram = nc.dram_tensor("y_rows", (T, D), F32, kind="Internal").ap()
        self.f_dram = nc.dram_tensor("forget_rows", (2, N_HEADS, T), F32, kind="Internal").ap()
        p = self.p
        p.dma(self.consts[:, :], consts[:, 0:KEPT_WIDTH], engine="scalar")
        p.dma(self.x[:, :, :], inputs["x"][0].rearrange("(t p) d -> p t d", p=P), engine="scalar")
        p.G(nc.gpsimd.memset, self.ones[:, :], 1.0)
        p.barrier()

    def sb(self, stack, name, shape):
        self.names += 1
        return stack.enter_context(self.nc.sbuf_tensor(f"{name}_{self.names}", shape, F32))

    def ring(self, stack, name, shape, n):
        return Ring([self.sb(stack, f"{name}{i}", shape) for i in range(n)])

    def const(self, name):
        at, width = CONST[name]
        return self.consts[:, at:at + width]

    def show(self, name, ap, token=None):
        if name in self.debug:
            self.p.barrier()
            self.p.dma(self.debug[name], ap)

    def columns(self, out, vectors, after=()):
        p = self.p
        total = sum(v.shape[0] for v in vectors)
        with ExitStack() as tmp:
            tokens, at, rows = [], 0, self.sb(tmp, "vector_rows", [P, P])
            for v in vectors:
                tokens.append(p.dma(rows[at:at + v.shape[0], :], v, after=after))
                at += v.shape[0]
            b = p.banks.next()
            turned = p.turn(b, b.t[:, 0:total], rows[0:total, :], self.const("ident")[0:total, 0:total], after=tokens)
            token = p.V(self.cp, out, b.t[:, 0:total], after=[turned])
            b.readers.append(token)
            p.barrier()
        return token

    def modulation(self, conds, w, b, rows, width):
        p, nc = self.p, self.nc
        m = len(conds)
        with ExitStack() as tmp:
            cs = self.sb(tmp, "cond_silu", [P, KT, m])
            for i, c in enumerate(conds):
                ready = p.S(cs[:, :, i], c, ACT.Silu)
            bias = self.sb(tmp, "mod_bias", [m, width])
            row = self.sb(tmp, "mod_row", [m, width])
            came = p.dma(bias[:, :], b.partition_broadcast(m))
            for f in range(width // 512):
                slot, wv, landed = p.weights(w[:, f * 512:(f + 1) * 512], 512)
                bank = p.banks.next()
                got = p.product(bank, bank.t[0:m, :], [(cs[:, k, :], wv[:, k, :]) for k in range(KT)],
                                after=[ready, landed])
                slot.readers.append(got)
                last = p.V(self.tt, row[:, f * 512:(f + 1) * 512], bank.t[0:m, :],
                           bias[:, f * 512:(f + 1) * 512], ALU.add, after=[got, came])
                bank.readers.append(last)
            p.dma(self.mod[rows[0]:rows[0] + m, 0:width], row[:, :], after=[last])
            p.barrier()

    def rstd(self, sums, n, eps, tmp):
        p = self.p
        p.V(self.ts, sums, sums, 1.0 / n, eps, ALU.mult, ALU.add)
        r = p.V(self.nc.vector.reciprocal, sums, sums)
        return p.S(sums, sums, ACT.Sqrt, after=[r])

    def turned(self, rows, cols, col0=0, scale=None, shift=None, after=(), kt=KT):
        p = self.p
        token = None
        for k in range(kt):
            b = p.banks.next()
            for t in range(TT):
                got = p.turn(b, b.t[:, t * P:(t + 1) * P], rows[:, t, k * P:(k + 1) * P],
                             self.const("ident"), after=after)
            out = cols[:, k, col0:col0 + T]
            if scale is None:
                token = p.V(self.cp, out, b.t[:, 0:T], after=[got])
            else:
                token = p.V(self.ts, out, b.t[:, 0:T], scale[:, k:k + 1], shift[:, k:k + 1],
                            ALU.mult, ALU.add, after=[got])
            b.readers.append(token)
        return token

    def rms_turned(self, x, cols, col0, scale, shift):
        p = self.p
        with ExitStack() as tmp:
            xn = self.sb(tmp, "x_normed", [P, TT, D])
            ss = self.sb(tmp, "square_sums", [P, TT])
            for t in range(TT):
                a = p.S(xn[:, t, :], x[:, t, :], ACT.Square, accum_out=ss[:, t:t + 1], after=[p.last.get("vector")])
            p.wait("vector", [a])
            r = self.rstd(ss[:, :], D, 1e-6, tmp)
            for t in range(TT):
                n = p.V(self.ts, xn[:, t, :], x[:, t, :], ss[:, t:t + 1], None, ALU.mult, after=[r])
            token = self.turned(xn, cols, col0, scale, shift, after=[n])
            p.barrier()
        return token

    def to_cols(self, src, F, w, evac, n=T, col0=0, ktiles=KT, ready=()):
        p = self.p
        step = 4096 // ktiles
        for f0 in range(0, F, step):
            wide = min(step, F - f0)
            slot, wv, landed = p.weights(w[:, f0:f0 + wide], wide)
            for f in range(f0, f0 + wide, P):
                bank = p.banks.next()
                got = p.product(bank, bank.t[:, 0:n],
                                [(wv[:, k, f - f0:f - f0 + P], src[:, k, col0:col0 + n]) for k in range(ktiles)],
                                after=[landed, *ready])
                bank.readers.append(evac(f // P, bank.t[:, 0:n], got))
            slot.readers.append(got)

    def to_rows(self, src, F, w, evac, tiles=TT, ktiles=KT, ready=()):
        p = self.p
        step = 4096 // ktiles
        for f0 in range(0, F, step):
            wide = min(step, F - f0)
            slot, wv, landed = p.weights(w[:, f0:f0 + wide], wide)
            for t in range(tiles):
                for g in range(0, wide, 512):
                    n = min(512, wide - g)
                    bank = p.banks.next()
                    got = p.product(bank, bank.t[:, 0:n],
                                    [(src[:, k, t * P:(t + 1) * P], wv[:, k, g:g + n]) for k in range(ktiles)],
                                    after=[landed, *ready])
                    bank.readers.append(evac(t, f0 + g, bank.t[:, 0:n], got))
            slot.readers.append(got)

    def copier(self, dst):
        return lambda f, ps, got: self.p.V(self.cp, dst[:, f, 0:ps.shape[1]], ps, after=[got])

    def head_rms(self, t, heads, gain, tmp, factor=1.0):
        p = self.p
        sq = self.sb(tmp, "head_squares", [P, heads, HD])
        ss = self.sb(tmp, "head_sums", [P, heads])
        p.V(self.tt, sq[:, :, :], t, t, ALU.mult)
        p.V(self.nc.vector.tensor_reduce, ss[:, :], sq[:, :, :], AX.X, ALU.add)
        r = self.rstd(ss[:, :], HD, 1e-6, tmp)
        p.V(self.tt, t, t, ss[:, :].unsqueeze(2).to_broadcast([P, heads, HD]), ALU.mult, after=[r])
        return p.V(self.tt, t, t, gain.unsqueeze(1).to_broadcast([P, heads, HD]), ALU.mult)

    def attention(self, items, scale):
        p, nc, v = self.p, self.nc, self.nc.vector
        with ExitStack() as tmp:
            probs = self.ring(tmp, "probs", [P, 512], 3)
            turned = self.ring(tmp, "probs_turned", [P, 512], 3)
            stats = self.sb(tmp, "softmax_stats", [P, len(items), 4])
            state = [dict() for _ in items]

            def score(i):
                it, st = items[i], state[i]
                bank = p.banks.next()
                after = [*bank.free(), *it["ready"]]
                pairs = [(slice(0, it["n"]), it["q"], it["keys"])] + it["extra"]
                for j, (cols, l, r) in enumerate(pairs):
                    tok = p.put("tensor", nc.tensor.matmul, bank.t[:, cols], l, r, start=j == 0,
                                stop=j == len(pairs) - 1, skip_group_check=True, after=after, chain=False,
                                signal=j == len(pairs) - 1)
                    after = ()
                p.V(v.reduce_max, stats[:, i, 0:1], bank.t[:, 0:it["n"]], AX.X, after=[tok])
                st["max"] = p.V(self.ts, stats[:, i, 1:2], stats[:, i, 0:1], -scale, None, ALU.mult)
                st["bank"] = bank
                b = probs.next()
                st["exp"] = p.S(b.t[:, 0:it["n"]], bank.t[:, 0:it["n"]], ACT.Exp, bias=stats[:, i, 1:2],
                                scale=scale, accum_out=stats[:, i, 2:3], after=[st["max"], *b.free()])
                bank.readers.append(st["exp"])
                st["probs"] = b

            def turn(i):
                it, st = items[i], state[i]
                bank, b = p.banks.next(), st["probs"]
                for k in range(it["n"] // P):
                    tok = p.turn(bank, bank.t[:, k * P:(k + 1) * P], b.t[:, k * P:(k + 1) * P],
                                 self.const("ident"), after=[st["exp"]])
                b.readers.append(tok)
                c = turned.next()
                st["turned"] = c
                st["copied"] = p.V(self.cp, c.t[:, 0:it["n"]], bank.t[:, 0:it["n"]], after=[tok, *c.free()])
                bank.readers.append(st["copied"])

            def mix(i):
                it, st = items[i], state[i]
                bank, c = p.banks.next(), st["turned"]
                tok = p.product(bank, bank.t[:, 0:HD],
                                [(c.t[:, k * P:(k + 1) * P], it["values"](k)) for k in range(it["n"] // P)],
                                after=[st["copied"]])
                c.readers.append(tok)
                p.V(v.reciprocal, stats[:, i, 3:4], stats[:, i, 2:3], after=[st["exp"]])
                done = p.V(self.ts, it["out"], bank.t[:, 0:HD], stats[:, i, 3:4], None, ALU.mult, after=[tok])
                bank.readers.append(done)

            pipeline(len(items), [score, turn, mix])
            p.barrier()

    def first_of_max(self, onehot, vals, m, order, tmpv):
        p, v = self.p, self.nc.vector
        shape = list(vals.shape)
        wide = lambda a: a.unsqueeze(len(shape) - 1).to_broadcast(shape)
        p.V(v.tensor_reduce, m, vals, AX.X, ALU.max)
        p.V(self.tt, tmpv, vals, wide(m), ALU.is_ge)
        p.V(self.tt, tmpv, tmpv, order, ALU.mult)
        p.V(v.tensor_reduce, m, tmpv, AX.X, ALU.max)
        return p.V(self.tt, onehot, tmpv, wide(m), ALU.is_equal)

    def modulated_rows(self, x, h, scale, shift, gain=None):
        p = self.p
        with ExitStack() as tmp:
            a, b = self.sb(tmp, "scale_rows", [P, D]), self.sb(tmp, "shift_rows", [P, D])
            came = [p.dma(a[:, :], scale.partition_broadcast(P)), p.dma(b[:, :], shift.partition_broadcast(P))]
            p.wait("vector", came)
            p.V(self.ts, a[:, :], a[:, :], 1.0, None, ALU.add)
            if gain is not None:
                g = self.sb(tmp, "gain_rows", [P, D])
                p.V(self.tt, a[:, :], a[:, :], g[:, :], ALU.mult, after=[p.dma(g[:, :], gain.partition_broadcast(P))])
            for t in range(TT):
                p.V(self.tt, h[:, t, :], x[:, t, :], a[:, :], ALU.mult)
                p.V(self.tt, h[:, t, :], h[:, t, :], b[:, :], ALU.add)
            p.barrier()

    def experts(self, rows, chosen, gate, out, n, tiles):
        p, nc, v = self.p, self.nc, self.nc.vector
        rounds = T // CAP
        with ExitStack() as tmp:
            pos = self.sb(tmp, "slot_of_token", [P, rounds, TT, n])
            flagf = self.sb(tmp, "more_rounds", [P, rounds * n])
            flags = self.flags.pop()
            bank = p.banks.next()
            ready = [p.last["vector"]]
            before, ones = self.const("before"), self.ones[:, :]
            p.product(bank, bank.t[:, 0:n], [(before, chosen[:, 0, :])], after=ready)
            p.product(bank, bank.t[:, n:2 * n], [(before, chosen[:, 1, :]), (ones, chosen[:, 0, :])])
            got = p.product(bank, bank.t[:, 2 * n:3 * n], [(ones, chosen[:, 0, :]), (ones, chosen[:, 1, :])])
            p.V(self.ts, pos[:, 0, :, :], chosen[:, :, :], -1e4, 1e4, ALU.mult, ALU.add)
            p.V(self.tt, pos[:, 0, :, :], pos[:, 0, :, :], bank.t[:, 0:2 * n].rearrange("p (t n) -> p t n", t=TT),
                ALU.add, after=[got])
            for r in range(1, rounds):
                p.V(self.ts, pos[:, r, :, :], pos[:, 0, :, :], -float(CAP * r), None, ALU.add)
                bank.readers.append(p.V(self.ts, flagf[:, r * n:(r + 1) * n], bank.t[:, 2 * n:3 * n], float(CAP * r),
                                        None, ALU.is_gt))
            p.V(v.memset, flagf[:, 0:n], 0.0)
            p.V(v.tensor_reduce, flagf[:, 0:1], flagf[:, n:2 * n], AX.X, ALU.max)
            flagged = p.V(self.cp, flags[:, :], flagf[:, :])
            all_banks = p.banks
            sums, p.banks = all_banks.buffers[0:4], Ring([])
            p.banks.buffers = all_banks.buffers[4:8]
            sel = self.ring(tmp, "chooser", [P, TT, CAP], 2)
            selg = self.ring(tmp, "gated_chooser", [P, TT, P], 3)
            xe = self.ring(tmp, "expert_in", [P, KT, CAP], 2)
            act = self.ring(tmp, "silu", [P, 256], 2)
            hid = self.ring(tmp, "hidden", [P, 256], 2)
            cols = self.ring(tmp, "hidden_cols", [P, 512], 3)
            ys = self.ring(tmp, "expert_out", [P, 512], 2)

            def round_stages(jobs, first):
                st = [dict() for _ in jobs]

                def load(i):
                    if jobs[i][1] <= 1:
                        wa, wb, wd = tiles(jobs[i][0])
                        slots, both, landed = p.weight_pair([wa, wb])
                        self.held = dict(slots=slots, both=both, landed=landed, down=p.weights(wd, D))
                    st[i]["w"] = self.held

                def gather(i):
                    e, r = jobs[i]
                    s, g = sel.next(), selg.next()
                    free = s.free() + g.free()
                    for t in range(TT):
                        at = pos[:, r, t, e:e + 1]
                        p.V(self.ts, g.t[:, t, :], self.const("slot"), at, gate[:, t, e:e + 1], ALU.is_equal, ALU.mult,
                            after=free, chain=t == 0)
                        chose = p.V(self.ts, s.t[:, t, :], self.const("slot")[:, 0:CAP], at, None, ALU.is_equal, chain=False)
                    bank, x = p.banks.next(), xe.next()
                    for k in range(KT):
                        got = p.product(bank, bank.t[:, k * CAP:(k + 1) * CAP],
                                        [(rows[:, t, k * P:(k + 1) * P], s.t[:, t, :]) for t in range(TT)], after=[chose])
                    s.readers.append(got)
                    copied = p.V(self.cp, x.t[:, :, :].rearrange("p k s -> p (k s)"), bank.t[:, :], after=[got, *x.free()])
                    bank.readers.append(copied)
                    st[i].update(x=x, copied=copied, g=g, chose=chose)

                def up(i):
                    j, bank = st[i], p.banks.next()
                    w, after = j["w"], [*bank.free(), j["copied"], *j["w"]["landed"]]
                    for k in range(KT):
                        for half in range(2):
                            out = bank.t[CAP * half:CAP * half + CAP, :].rearrange("p (w n) -> p w n", w=2)
                            got = p.put("tensor", nc.tensor.matmul, out, j["x"].t[:, k, :],
                                        w["both"][:, k, :, half * 256:half * 256 + 256], start=k == 0, stop=k == KT - 1,
                                        tile_position=(0, CAP * half), after=after, chain=False, signal=k == KT - 1 and half)
                            after = ()
                    for slot in w["slots"]:
                        slot.readers.append(got)
                    j["x"].readers.append(got)
                    a, h = act.next(), hid.next()
                    s = p.S(a.t[:, :], bank.t[:, 0:256], ACT.Silu, after=[got, *a.free()])
                    j["h_done"] = p.V(self.tt, h.t[:, :], a.t[:, :], bank.t[:, 256:512], ALU.mult, after=[s, *h.free()])
                    a.readers.append(j["h_done"])
                    bank.readers.append(j["h_done"])
                    j["h"] = h

                def turn(i):
                    j, bank, c = st[i], p.banks.next(), cols.next()
                    for b in range(2):
                        p.turn(bank, bank.t[:, b * P:(b + 1) * P], j["h"].t[:, b * P:(b + 1) * P], self.const("ident"),
                               after=[j["h_done"]], signal=False)
                    for t in range(TT):
                        got = p.turn(bank, bank.t[:, 256 + t * P:256 + (t + 1) * P], j["g"].t[:, t, :],
                                     self.const("ident"), after=[j["chose"]])
                    j["h"].readers.append(got)
                    j["g"].readers.append(got)
                    j["c_done"] = p.S(c.t[:, :], bank.t[:, :], ACT.Copy, after=[got, *c.free()])
                    bank.readers.append(j["c_done"])
                    j["c"] = c

                def down(i):
                    j, bank = st[i], p.banks.next()
                    slot, wd, landed = j["w"]["down"]
                    after = [*bank.free(), j["c_done"], landed]
                    for f in range(4):
                        half, b = f // 2, f % 2
                        for c in range(2):
                            got = p.put("tensor", nc.tensor.matmul, bank.t[CAP * c:CAP * c + CAP, :],
                                        j["c"].t[:, b * P + half * CAP:b * P + half * CAP + CAP],
                                        wd[:, f, c * 512:c * 512 + 512], start=f == 0, stop=f == 3,
                                        tile_position=(0, CAP * c), after=after, chain=False, signal=f == 3 and c)
                            after = ()
                    slot.readers.append(got)
                    y = ys.next()
                    j["y_done"] = p.S(y.t[:, :], bank.t[:, :], ACT.Copy, after=[got, *y.free()])
                    bank.readers.append(j["y_done"])
                    j["y"] = y

                def scatter(i):
                    j, start = st[i], first and i == 0
                    for t in range(TT):
                        for c in range(2):
                            side = slice(CAP * c, CAP * c + CAP)
                            b = sums[2 * t + c]
                            got = p.put("tensor", nc.tensor.matmul, b.t[:, :], j["c"].t[side, 256 + t * P:256 + (t + 1) * P],
                                        j["y"].t[side, :], start=start, stop=True, skip_group_check=True,
                                        tile_position=(CAP * c, 0), after=[*b.free(), j["y_done"]], chain=False,
                                        signal=t and c)
                    j["c"].readers.append(got)
                    j["y"].readers.append(got)
                    self.summed = got

                return load, gather, up, turn, down, scatter

            p.align(3)
            load, gather, up, turn, down, scatter = round_stages([(e, 0) for e in range(n)], True)
            for i in range(n + 3):
                for stage, lag in ((gather, 0), (turn, 2), (up, 1), (down, 2), (scatter, 3), (load, 0)):
                    if 0 <= i - lag < n:
                        stage(i - lag)

            def more(e, r):
                def body():
                    load, *stages = round_stages([(e, r)], False)
                    load(0)
                    for stage in stages:
                        stage(0)
                    if r + 1 < rounds:
                        p.branch(flags[0:1, (r + 1) * n + e:(r + 1) * n + e + 1], more(e, r + 1))
                return body

            def any_more():
                for e in range(n):
                    p.branch(flags[0:1, n + e:n + e + 1], more(e, 1))
            for engine in ("tensor", "vector", "scalar", "sync"):
                p.wait(engine, [flagged])
            p.branch(flags[0:1, 0:1], any_more)
            for t in range(TT):
                for c in range(2):
                    b = sums[2 * t + c]
                    b.readers.append(p.V(self.cp, out[:, t, c * 512:(c + 1) * 512], b.t[:, :], after=[self.summed]))
            p.banks = all_banks
            p.barrier()

    def first_block(self):
        p, nc, A, v = self.p, self.nc, self.A, self.nc.vector
        with ExitStack() as blk:
            par = self.sb(blk, "params1", [P, 48])
            N1, N2, CB, CG, C1, C2 = 0, 8, 16, 20, 24, 32
            r8 = lambda a: a.rearrange("(k p) -> k p", p=P)
            self.columns(par[:, 0:40], [r8(A["norm1_g"][0]), r8(A["norm2_g"][0]), r8(A["conv_b"][0]),
                                        r8(A["conv_norm_g"][0]), r8(A["c"][0]), r8(A["c_ctx"])])
            convw = self.sb(blk, "conv_w", [P, 31, 4])
            self.columns(convw[:, :, :].rearrange("p a b -> p (a b)"),
                         [A["conv_w"][0].rearrange("t (k p) -> (t k) p", p=P)])
            self.modulation([par[:, C1:C1 + 8], par[:, C2:C2 + 8]], A["w_mod"][0], A["b_mod"][0], [0, 1], 6 * D)
            modT = self.sb(blk, "mod_cols", [P, 64])
            self.columns(modT[:, :], [r8(self.mod[0]), r8(self.mod[1, 0:2 * D])])
            AB = self.sb(blk, "norm_scales", [P, 3, 8])
            for i, (sc, g) in enumerate(((8, N1), (56, N1), (32, N2))):
                p.V(self.stt, out=AB[:, i, :], in0=modT[:, sc:sc + 8], scalar=1.0, in1=par[:, g:g + 8],
                    op0=ALU.add, op1=ALU.mult)
            y_sum = self.sb(blk, "branch_sum_cols", [P, KT, T])
            with ExitStack() as mix:
                self.mixer(mix, par, convw, modT, AB, y_sum, CB, CG)
                p.barrier()
            with ExitStack() as tmp:
                g1 = self.sb(tmp, "gate1", [P, D])
                came = p.dma(g1[:, :], self.mod[0, 2 * D:3 * D].partition_broadcast(P))
                t1 = self.ring(tmp, "mixed", [P, 512], 2)

                def evac(t, f0, ps, got):
                    b = t1.next()
                    tok = p.V(self.tt, b.t[:, :], ps, g1[:, f0:f0 + 512], ALU.mult, after=[got, came])
                    xs = self.x[:, t, f0:f0 + 512]
                    p.V(self.tt, xs, xs, b.t[:, :], ALU.add)
                    return tok
                self.to_rows(y_sum, D, A["w_out"][0], evac)
                p.barrier()
            self.show("x_mid1", self.x[:, :, :])
            with ExitStack() as tmp:
                rows = self.sb(tmp, "h2_rows", [P, TT, D])
                acc = self.sb(tmp, "moe_sum", [P, TT, D])
                gate = self.sb(tmp, "gates", [P, TT, 16])
                chosen = self.sb(tmp, "chosen", [P, TT, 16])
                ss = self.sb(tmp, "square_sums", [P, TT])
                for t in range(TT):
                    a = p.S(rows[:, t, :], self.x[:, t, :], ACT.Square, accum_out=ss[:, t:t + 1])
                p.wait("vector", [a])
                r = self.rstd(ss[:, :], D, 1e-6, tmp)
                for t in range(TT):
                    p.V(self.ts, rows[:, t, :], self.x[:, t, :], ss[:, t:t + 1], None, ALU.mult, after=[r])
                self.modulated_rows(rows, rows, self.mod[0, 4 * D:5 * D], self.mod[0, 3 * D:4 * D], A["norm2_g"][0])
                with ExitStack() as t2:
                    h2 = self.sb(t2, "h2_cols", [P, KT, T])
                    self.turned(rows, h2)
                    self.route1(h2, gate, chosen)
                    p.barrier()
                wgu, wd = A["w_expert_gu"][0], A["w_expert_down"][0]
                self.experts(rows, chosen, gate, acc, 16, lambda e: (wgu[e][:, 0:512], wgu[e][:, 512:1024], wd[e]))
                g2 = self.sb(tmp, "gate2", [P, D])
                gf = self.sb(tmp, "final_gain", [P, D])
                came = p.dma(g2[:, :], self.mod[0, 5 * D:6 * D].partition_broadcast(P))
                came2 = p.dma(gf[:, :], A["final_norm_g"].partition_broadcast(P))
                for t in range(TT):
                    p.V(self.tt, acc[:, t, :], acc[:, t, :], g2[:, :], ALU.mult, after=[came])
                    a = p.V(self.tt, self.x[:, t, :], self.x[:, t, :], acc[:, t, :], ALU.add)
                for t in range(TT):
                    s = p.S(acc[:, t, :], self.x[:, t, :], ACT.Square, accum_out=ss[:, t:t + 1], after=[a])
                p.wait("vector", [s])
                r = self.rstd(ss[:, :], D, 1e-6, tmp)
                for t in range(TT):
                    p.V(self.stt, out=self.x[:, t, :], in0=self.x[:, t, :], scalar=ss[:, t:t + 1], in1=gf[:, :],
                        op0=ALU.mult, op1=ALU.mult, after=[r, came2])
                p.barrier()
        self.show("x_first", self.x[:, :, :])

    def mixer(self, mix, par, convw, modT, AB, y_sum, CB, CG):
        p, nc, A, v = self.p, self.nc, self.A, self.nc.vector
        w_in = A["w_in"][0]
        hT = self.sb(mix, "h_cols", [P, KT, 2 * T])
        with ExitStack() as tmp:
            ctx = self.sb(tmp, "ctx_rows", [P, TT, D])
            came = p.dma(ctx[:, :, :], A["ctx"][0].rearrange("(t p) d -> p t d", p=P), engine="scalar")
            p.wait("scalar", [came])
            p.wait("vector", [came])
            self.rms_turned(self.x, hT, 0, AB[:, 0, :], modT[:, 0:8])
            self.rms_turned(ctx, hT, T, AB[:, 1, :], modT[:, 48:56])
        self.show("hT", hT[:, :, :])
        branches = [self.sb(mix, f"branch{i}_cols", [P, 4, T]) for i in range(4)]
        with ExitStack() as tmp:
            q = self.sb(tmp, "q_rows", [P, TT, 8, HD])
            k = self.sb(tmp, "k_rows", [P, 4, 2, HD])
            val = self.sb(tmp, "v_rows", [P, 4, 2, HD])
            gains = self.sb(tmp, "head_gains", [P, 2, HD])
            p.dma(gains[:, 0, :], A["q_norm_g"][0].partition_broadcast(P))
            p.dma(gains[:, 1, :], A["k_norm_g"][0].partition_broadcast(P))
            flat = lambda a: a.rearrange("p h d -> p (h d)")
            self.to_rows(hT, 512, w_in[:, 0:512],
                         lambda t, f0, ps, got: p.V(self.cp, flat(q[:, t, :, :]), ps, after=[got]))

            def split(t, f0, ps, got):
                p.V(self.cp, flat(k[:, t, :, :]), ps[:, 0:128], after=[got])
                return p.V(self.cp, flat(val[:, t, :, :]), ps[:, 128:256])
            self.to_rows(hT, 256, w_in[:, 512:768], split, tiles=4)
            p.barrier()
            rot = self.sb(tmp, "rotated", [P, 2, 8, 32])
            for t in range(TT):
                self.head_rms(q[:, t, :, :], 8, gains[:, 0, :], tmp)
                self.rope(q[:, t, :, :], 8, t, rot)
            for t in range(4):
                self.head_rms(k[:, t, :, :], 2, gains[:, 1, :], tmp)
                if t < TT:
                    self.rope(k[:, t, :, :], 2, t, rot)
            k2 = self.sb(tmp, "k_twice", [P, 4, 2, 2, HD])
            for i in range(2):
                done = p.V(self.cp, k2[:, :, :, i, :], k[:, :, :, :])
            qT = self.sb(tmp, "q_cols", [P, 4, T])
            kT = self.sb(tmp, "k_cols", [P, 2, 2 * T])
            self.turned(q[:, :, :, :].rearrange("p t h d -> p t (h d)"), qT, kt=4, after=[done])
            k2f = k2[:, :, :, :, :].rearrange("p t h i d -> p t (h i d)")
            self.turned(k2f[:, 0:2, :], kT, 0, kt=2)
            ready = self.turned(k2f[:, 2:4, :], kT, T, kt=2)
            y = self.sb(tmp, "attention_rows", [P, TT, 512])
            items = []
            for h in range(8):
                half = slice(HD * (h % 2), HD * (h % 2) + HD)
                for t in range(TT):
                    items.append(dict(q=qT[half, h // 2, t * P:(t + 1) * P], keys=kT[half, h // 4, :], n=512,
                                      extra=[], values=lambda k, h=h: val[:, k, h // 4, :],
                                      out=y[:, t, h * HD:(h + 1) * HD], ready=[ready]))
            self.attention(items, HD ** -0.5)
            self.turned(y, branches[0], kt=4)
            p.barrier()
        self.show("y_gqa", branches[0][:, :, :])
        with ExitStack() as tmp:
            qT = self.sb(tmp, "nq_cols", [P, 4, T])
            kT = self.sb(tmp, "nk_cols", [P, 4, 2 * T])
            val = self.sb(tmp, "nv_rows", [P, 4, 8, HD])
            bias = self.sb(tmp, "window_bias", [P, TT, 8, 4, GRID_W])
            rpb = A["na_rpb"][0]
            came = []
            for t in range(TT):
                for half in range(2):
                    r = 2 * t + half
                    for h in range(8):
                        src = bass.AP(tensor=rpb.tensor, offset=rpb.offset + h * 15 * 31 + (7 - r) * 31 + 15 - (GRID_W - 1),
                                      ap=[[1, GRID_W], [31, 4], [1, GRID_W]])
                        came.append(p.dma(bias[HD * half:HD * half + HD, t, h, :, :], src))
            self.to_cols(hT, 512, w_in[:, 768:1280], self.copier(qT))
            self.to_cols(hT, 512, w_in[:, 1280:1792], self.copier(kT), n=2 * T)
            self.to_rows(hT, 512, w_in[:, 1792:2304],
                         lambda t, f0, ps, got: p.V(self.cp, val[:, t, :, :].rearrange("p h d -> p (h d)"),
                                                    ps, after=[got]), tiles=4)
            p.wait("vector", came)
            for t in range(TT):
                for h in range(8):
                    b = bias[:, t, h, :, :]
                    done = p.V(self.stt, out=b, in0=b, scalar=HD ** 0.5, op0=ALU.mult, op1=ALU.add,
                               in1=self.const("window").unsqueeze(1).to_broadcast([P, 4, GRID_W]))
            y = self.sb(tmp, "na_rows", [P, TT, 512])
            items = []
            for h in range(8):
                half = slice(HD * (h % 2), HD * (h % 2) + HD)
                for t in range(TT):
                    items.append(dict(q=qT[half, h // 2, t * P:(t + 1) * P], keys=kT[half, h // 2, :], n=512,
                                      extra=[(slice(0, T), self.const("reverse"),
                                              bias[:, t, h, :, :].rearrange("p a b -> p (a b)"))],
                                      values=lambda k, h=h: val[:, k, h, :],
                                      out=y[:, t, h * HD:(h + 1) * HD], ready=[done]))
            self.attention(items, HD ** -0.5)
            self.turned(y, branches[1], kt=4)
            p.barrier()
        self.show("y_na", branches[1][:, :, :])
        with ExitStack() as tmp:
            u = self.sb(tmp, "fourier_cols", [P, 4, T])
            spec = self.sb(tmp, "spectrum_rows", [P, TT, 4, 2, P])
            tables = self.sb(tmp, "fourier_tables", [P, CONST_WIDTH - KEPT_WIDTH])
            p.dma(tables[:, :], self.all_consts[:, KEPT_WIDTH:CONST_WIDTH])
            table = lambda n: tables[:, CONST[n][0] - KEPT_WIDTH:CONST[n][0] - KEPT_WIDTH + CONST[n][1]]
            self.to_cols(hT, 512, w_in[:, 2304:2816], self.copier(u))
            p.barrier()
            for t in range(TT):
                for g in range(4):
                    bank = p.banks.next()
                    got = p.product(bank, bank.t[:, 0:256], [(u[:, g, t * P:(t + 1) * P], table("cs_group"))])
                    done = p.V(self.cp, spec[:, t, g, :, :].rearrange("p a b -> p (a b)"), bank.t[:, 0:256], after=[got])
                    bank.readers.append(done)
            for g in range(4):
                bank = p.banks.next()
                pairs = [(spec[:, t, g, i, :], table(("cos_seq", "sin_seq")[i])[:, t * T:(t + 1) * T])
                         for t in range(TT) for i in range(2)]
                got = p.product(bank, bank.t[:, 0:T], pairs, after=[done])
                bank.readers.append(p.V(self.cp, branches[2][:, g, :], bank.t[:, 0:T], after=[got]))
            p.barrier()
        self.show("y_fn", branches[2][:, :, :])
        with ExitStack() as tmp:
            pad = 15
            a = self.sb(tmp, "glu_cols", [P, 4, T])
            z = self.sb(tmp, "padded_cols", [P, 4, T + 2 * pad])
            c = branches[3]
            p.V(v.memset, z[:, :, :], 0.0)
            self.to_cols(hT, 512, w_in[:, 2816:3328], self.copier(a))
            sg = self.ring(tmp, "sigmoid", [P, T], 2)

            def glu(f, ps, got):
                b = sg.next()
                s = p.S(b.t[:, :], ps, ACT.Sigmoid, after=[got, *b.free()])
                b.readers.append(p.V(self.tt, z[:, f, pad:pad + T], a[:, f, :], b.t[:, :], ALU.mult, after=[s]))
                return s
            self.to_cols(hT, 512, w_in[:, 3328:3840], glu)
            for i in range(31):
                for f in range(4):
                    src, w = z[:, f, i:i + T], convw[:, i, f:f + 1]
                    if i == 0:
                        p.V(self.ts, c[:, f, :], src, w, par[:, CB + f:CB + f + 1], ALU.mult, ALU.add, chain=f == 0)
                    else:
                        p.V(self.stt, out=c[:, f, :], in0=src, scalar=w, in1=c[:, f, :], op0=ALU.mult, op1=ALU.add,
                            chain=f == 0)
            sq = self.sb(tmp, "conv_squares", [P, 4, T])
            done = p.V(self.tt, sq[:, :, :], c[:, :, :], c[:, :, :], ALU.mult)
            bank = p.banks.next()
            got = p.product(bank, bank.t[:, 0:T], [(self.ones[:, :], sq[:, f, :]) for f in range(4)], after=[done])
            rs = self.sb(tmp, "conv_rstd", [P, T])
            bank.readers.append(p.V(self.cp, rs[:, :], bank.t[:, 0:T], after=[got]))
            r = self.rstd(rs[:, :], 512, 1e-6, tmp)
            p.V(self.tt, c[:, :, :], c[:, :, :], rs[:, :].unsqueeze(1).to_broadcast([P, 4, T]), ALU.mult, after=[r])
            for f in range(4):
                p.S(c[:, f, :], c[:, f, :], ACT.Silu, scale=par[:, CG + f:CG + f + 1], after=[p.last["vector"]])
            p.barrier()
        self.show("y_cv", branches[3][:, :, :])
        with ExitStack() as tmp:
            gates = self.sb(tmp, "branch_gates", [P, KT, T])
            t1 = self.ring(tmp, "gated", [P, T], 2)
            for n in range(4):
                g0 = 3840 + n * D
                self.to_cols(hT, D, w_in[:, g0:g0 + D],
                             lambda f, ps, got: p.S(gates[:, f, :], ps, ACT.Sigmoid,
                                                    after=[got, p.last["vector"]]))

                def evac(f, ps, got, n=n):
                    out = y_sum[:, f, :] if n == 0 else t1.next().t[:, :]
                    tok = p.V(self.tt, out, ps, gates[:, f, :], ALU.mult, after=[got, p.last["scalar"]])
                    if n:
                        p.V(self.tt, y_sum[:, f, :], y_sum[:, f, :], out, ALU.add)
                    return tok
                self.to_cols(branches[n], D, A["w_branch"][0, n], evac, ktiles=4)
            p.barrier()
        self.show("y_sum", y_sum[:, :, :])

    def rope(self, t, heads, tile, rot):
        p = self.p
        pairs = t.rearrange("p h (j i) -> p h j i", i=2)
        x1, x2 = pairs[:, :, :, 0], pairs[:, :, :, 1]
        cut = lambda n: self.const(n)[:, tile * 32:tile * 32 + 32].unsqueeze(1).to_broadcast([P, heads, 32])
        cos, sin = cut("cos"), cut("sin")
        with ExitStack() as tmp:
            a, b = rot[:, 0, 0:heads, :], rot[:, 1, 0:heads, :]
            rot2 = self.sb(tmp, "rope_scratch", [P, 2, 8, 32])
            c, d = rot2[:, 0, 0:heads, :], rot2[:, 1, 0:heads, :]
            p.V(self.tt, a, x1, cos, ALU.mult)
            p.V(self.tt, b, x2, sin, ALU.mult)
            p.V(self.tt, c, x1, sin, ALU.mult)
            p.V(self.tt, d, x2, cos, ALU.mult)
            p.V(self.tt, x1, a, b, ALU.subtract)
            p.V(self.tt, x2, c, d, ALU.add)

    def scores_rows(self, hT, w_aps, bias_aps, n, out, tmp):
        p = self.p
        w = self.sb(tmp, "router_w", [P, KT, n])
        bias = self.sb(tmp, "router_bias", [P, n])
        at, came = 0, [p.last["vector"]]
        for wa, ba in zip(w_aps, bias_aps):
            m = wa.shape[1]
            came.append(p.dma(w[:, :, at:at + m], wa.rearrange("(k p) n -> p k n", p=P)))
            came.append(p.dma(bias[:, at:at + m], ba.partition_broadcast(P)))
            at += m
        for t in range(TT):
            bank = p.banks.next()
            got = p.product(bank, bank.t[:, 0:n], [(hT[:, k, t * P:(t + 1) * P], w[:, k, :]) for k in range(KT)],
                            after=came)
            bank.readers.append(p.V(self.cp, out[:, t, :], bank.t[:, 0:n], after=[got, *came]))
        return bias[:, :].unsqueeze(1).to_broadcast([P, TT, n])

    def route1(self, hT, gate, chosen):
        p, v, A = self.p, self.nc.vector, self.A
        with ExitStack() as tmp:
            sb = lambda name, *s: self.sb(tmp, name, [P, TT, *s])
            sc, sel = sb("scores", 16), sb("selection", 16)
            bias = self.scores_rows(hT, [A["w_router"]], [A["router_bias"]], 16, sc, tmp)
            s = p.S(sc[:, :, :], sc[:, :, :], ACT.Sigmoid, after=[p.last["vector"]])
            p.V(self.tt, sel[:, :, :], sc[:, :, :], bias, ALU.add, after=[s])
            g4 = sel[:, :, :].rearrange("p t (g e) -> p t g e", e=4)
            gs, pair = sb("group_score", 4), sb("pair_sum", 4)
            for n, (i, j) in enumerate(((0, 1), (0, 2), (0, 3), (1, 2), (1, 3), (2, 3))):
                p.V(self.tt, (pair if n else gs)[:, :, :], g4[:, :, :, i], g4[:, :, :, j], ALU.add)
                if n:
                    p.V(self.tt, gs[:, :, :], gs[:, :, :], pair[:, :, :], ALU.max)
            m, t4, grp = sb("largest"), sb("tie4", 4), sb("group", 4)
            self.first_of_max(grp[:, :, :], gs[:, :, :], m[:, :],
                              self.const("first4").unsqueeze(1).to_broadcast([P, TT, 4]), t4[:, :, :])
            self.top2(sel, grp, 4, 4, chosen, tmp)
            p.V(self.tt, gate[:, :, :], chosen[:, :, :], sc[:, :, :], ALU.mult)
            p.V(v.tensor_reduce, m[:, :], gate[:, :, :], AX.X, ALU.add)
            p.V(v.reciprocal, m[:, :], m[:, :])
            p.V(self.tt, gate[:, :, :], gate[:, :, :], m[:, :].unsqueeze(2).to_broadcast([P, TT, 16]), ALU.mult)
            p.barrier()

    def top2(self, vals, grp, groups, size, chosen, tmp):
        p = self.p
        n = groups * size
        sb = lambda name, *s: self.sb(tmp, name, [P, TT, *s])
        m, tie, one, pen = sb("largest"), sb("tie", n), sb("first", n), sb("outside", groups)
        order = self.const("first32")[:, 0:n].unsqueeze(1).to_broadcast([P, TT, n])
        v4 = vals[:, :, :].rearrange("p t (g e) -> p t g e", e=size)
        wide = lambda a: a[:, :, :].unsqueeze(3).to_broadcast([P, TT, groups, size])
        p.V(self.ts, pen[:, :, :], grp[:, :, :], -1.0, BIG, ALU.add, ALU.mult)
        p.V(self.tt, v4, v4, wide(grp), ALU.mult)
        p.V(self.tt, v4, v4, wide(pen), ALU.add)
        second = sb("without_first", n)
        self.first_of_max(one[:, :, :], vals[:, :, :], m[:, :], order, tie[:, :, :])
        p.V(self.stt, out=second[:, :, :], in0=one[:, :, :], scalar=-3 * BIG, in1=vals[:, :, :],
            op0=ALU.mult, op1=ALU.add)
        self.first_of_max(chosen[:, :, :], second[:, :, :], m[:, :], order, tie[:, :, :])
        p.V(self.tt, chosen[:, :, :], chosen[:, :, :], one[:, :, :], ALU.add)

    def second_block(self):
        p, nc, A = self.p, self.nc, self.A
        r8 = lambda a: a.rearrange("(k p) -> k p", p=P)
        with ExitStack() as blk:
            c2 = self.sb(blk, "cond2", [P, 8])
            self.columns(c2[:, :], [r8(A["c_2"][0])])
            modT = self.sb(blk, "mod2_cols", [P, 2, 48])
            modK = self.sb(blk, "mod_kv_cols", [P, 16])
            self.modulation([c2[:, :]], A["ada_w_2"][0], A["ada_b_2"][0], [2], 6 * D)
            self.modulation([c2[:, :]], A["ada_w_2"][1], A["ada_b_2"][1], [3], 6 * D)
            self.modulation([c2[:, :]], A["kv_ada_w_2"], A["kv_ada_b_2"], [4], 2 * D)
            for l in range(2):
                self.columns(modT[:, l, :], [r8(self.mod[2 + l])])
            self.columns(modK[:, :], [r8(self.mod[4, 0:2 * D])])
            one_plus = self.sb(blk, "one_plus_scale", [P, 5, 8])
            for i, src in enumerate((modT[:, 0, 8:16], modT[:, 0, 32:40], modT[:, 1, 8:16], modT[:, 1, 32:40],
                                     modK[:, 8:16])):
                p.V(self.ts, one_plus[:, i, :], src, 1.0, None, ALU.add)
            p.barrier()
            for l in range(2):
                y = self.sb(blk, "layer_out_rows", [P, TT, D]) if l == 0 else y
                if l == 0:
                    self.rwkv(y, one_plus[:, 0, :], modT[:, 0, 0:8])
                else:
                    self.fox(y, one_plus[:, 2, :], modT[:, 1, 0:8])
                self.show(f"y_layer{l}", y[:, :, :])
                self.residual(y, l, 0)
                self.show(f"x_mid2_{l}", self.x[:, :, :])
                with ExitStack() as tmp:
                    rows = self.sb(tmp, "moe_rows", [P, TT, D])
                    gate = self.sb(tmp, "moe_gates", [P, TT, 32])
                    chosen = self.sb(tmp, "moe_chosen", [P, TT, 32])
                    self.modulated_rows(self.x, rows, self.mod[2 + l, 4 * D:5 * D], self.mod[2 + l, 3 * D:4 * D])
                    with ExitStack() as t2:
                        hT = self.sb(t2, "moe_cols", [P, KT, T])
                        self.turned(rows, hT)
                        self.route2(hT, gate, chosen, l)
                        p.barrier()
                    wg, wu, wd = (A[n][l] for n in ("moe_wgate_2", "moe_wup_2", "moe_wdown_2"))
                    self.experts(rows, chosen, gate, y, 32, lambda e: (wg[e], wu[e], wd[e]))
                self.residual(y, l, 1)
                self.show(f"x_end2_{l}", self.x[:, :, :])
                if l == 0:
                    self.kT = self.sb(blk, "fox_k_cols", [P, 8, T])
                    self.val = self.sb(blk, "fox_v_rows", [P, TT, N_HEADS, HD])
                    self.shared_kv(one_plus[:, 4, :], modK[:, 0:8])
            done = p.dma(self.out.rearrange("b (t p) d -> p (b t) d", p=P), self.x[:, :, :])
            p.wait("gpsimd", [done])

    def residual(self, y, l, which):
        p, A, v = self.p, self.A, self.nc.vector
        with ExitStack() as tmp:
            gt = self.sb(tmp, "res_gate", [P, D])
            g = self.sb(tmp, "ln_gain", [P, D])
            b = self.sb(tmp, "ln_bias", [P, D])
            at = (2 if which == 0 else 5) * D
            c = [p.dma(gt[:, :], self.mod[2 + l, at:at + D].partition_broadcast(P)),
                 p.dma(g[:, :], A["ln_g_2"][l, which].partition_broadcast(P)),
                 p.dma(b[:, :], A["ln_b_2"][l, which].partition_broadcast(P))]
            s1 = self.sb(tmp, "ln_sums", [P, TT, 2])
            p.wait("vector", c)
            for t in range(TT):
                xt, yt = self.x[:, t, :], y[:, t, :]
                p.V(self.stt, out=yt, in0=gt[:, :], scalar=1.0, in1=yt, op0=ALU.add, op1=ALU.mult)
                p.V(self.stt, out=xt, in0=xt, scalar=ALPHA, in1=yt, op0=ALU.mult, op1=ALU.add)
                p.V(v.tensor_reduce, s1[:, t, 0:1], xt, AX.X, ALU.add)
                p.V(self.ts, s1[:, t, 0:1], s1[:, t, 0:1], -1.0 / D, None, ALU.mult)
                p.V(self.ts, xt, xt, s1[:, t, 0:1], None, ALU.add)
                a = p.last["vector"]
                s = p.S(yt, xt, ACT.Square, accum_out=s1[:, t, 1:2], after=[a])
            p.wait("vector", [s])
            r = self.rstd(s1[:, :, 1], D, 1e-5, tmp)
            for t in range(TT):
                xt = self.x[:, t, :]
                p.V(self.stt, out=xt, in0=xt, scalar=s1[:, t, 1:2], in1=g[:, :], op0=ALU.mult, op1=ALU.mult, after=[r])
                p.V(self.tt, xt, xt, b[:, :], ALU.add)
            p.barrier()

    def route2(self, hT, gate, chosen, l):
        p, v, A = self.p, self.nc.vector, self.A
        with ExitStack() as tmp:
            sb = lambda name, *s: self.sb(tmp, name, [P, TT, *s])
            lg = sb("logits", 36)
            bias = self.scores_rows(hT, [A["moe_wgrp_2"][l], A["moe_wexp_2"][l]],
                                    [A["moe_bgrp_2"][l], A["moe_bexp_2"][l]], 36, lg, tmp)
            p.V(self.tt, lg[:, :, :], lg[:, :, :], bias, ALU.add)
            m, s, t4, grp, pg = sb("largest"), sb("sum"), sb("tie4", 4), sb("group", 4), sb("p_group")
            gl, el = lg[:, :, 0:4], sb("expert_logits", 32)

            def softmax(a, n):
                wide = lambda q: q[:, :].unsqueeze(2).to_broadcast([P, TT, n])
                p.V(v.tensor_reduce, m[:, :], a, AX.X, ALU.max)
                d = p.V(self.tt, a, a, wide(m), ALU.subtract)
                e = p.S(a, a, ACT.Exp, after=[d])
                p.V(v.tensor_reduce, s[:, :], a, AX.X, ALU.add, after=[e])
                p.V(v.reciprocal, s[:, :], s[:, :])
                p.V(self.tt, a, a, wide(s), ALU.mult)
            p.V(self.cp, el[:, :, :], lg[:, :, 4:36])
            softmax(gl, 4)
            self.first_of_max(grp[:, :, :], gl, m[:, :],
                              self.const("first4").unsqueeze(1).to_broadcast([P, TT, 4]), t4[:, :, :])
            p.V(v.tensor_reduce, pg[:, :], gl, AX.X, ALU.max)
            self.top2(el, grp, 4, 8, chosen, tmp)
            softmax(el[:, :, :], 32)
            p.V(self.tt, gate[:, :, :], chosen[:, :, :], el[:, :, :], ALU.mult)
            p.V(v.tensor_reduce, s[:, :], gate[:, :, :], AX.X, ALU.add)
            p.V(self.tt, gate[:, :, :], gate[:, :, :], pg[:, :].unsqueeze(2).to_broadcast([P, TT, 32]), ALU.mult)
            p.V(v.reciprocal, s[:, :], s[:, :])
            p.V(self.tt, gate[:, :, :], gate[:, :, :], s[:, :].unsqueeze(2).to_broadcast([P, TT, 32]), ALU.mult)
            p.barrier()

    def rwkv(self, y_out, scale, shift):
        p, nc, A, v = self.p, self.nc, self.A, self.nc.vector
        r8 = lambda a: a.rearrange("(k p) -> k p", p=P)
        with ExitStack() as top:
            gate = y_out
            par = self.sb(top, "params2", [P, 88])
            MU, W0, A0, KK, KA, RK = 0, 48, 56, 64, 72, 80
            self.columns(par[:, :], [A["rw_mu_2"][0].rearrange("m (k p) -> (m k) p", p=P), r8(A["rw_w0_2"][0]),
                                     r8(A["rw_a0_2"][0]), r8(A["rw_kk_2"][0]), r8(A["rw_ka_2"][0]),
                                     r8(A["rw_rk_2"][0].rearrange("h n -> (h n)"))])
            ar = self.sb(top, "a_r_cols", [P, KT, NCH, 2, CH])
            bh = self.sb(top, "b_cols", [P, KT, T])
            kh = self.sb(top, "k_cols", [P, KT, T])
            prod = self.sb(top, "bonus_cols", [P, KT, T])
            wend = self.sb(top, "chunk_decay", [P, KT, NCH])
            with ExitStack() as tmp:
                hp = self.sb(tmp, "h_padded", [P, KT, T + 1])
                xx = self.sb(tmp, "shift_diff", [P, KT, T])
                xi = self.sb(tmp, "mixed_cols", [P, KT, T])
                r_ = prod
                k_, a_, w_ = kh, bh, self.sb(tmp, "w_cols", [P, KT, T])
                p.V(v.memset, hp[:, :, 0:1], 0.0)
                self.turned(self.x, hp, 1, scale, shift)
                p.V(self.tt, xx[:, :, :], hp[:, :, 0:T], hp[:, :, 1:T + 1], ALU.subtract)

                def mixed(i):
                    for k in range(KT):
                        tok = p.V(self.stt, out=xi[:, k, :], in0=xx[:, k, :], scalar=par[:, MU + 8 * i + k:MU + 8 * i + k + 1],
                                  in1=hp[:, k, 1:T + 1], op0=ALU.mult, op1=ALU.add, after=[p.last.get("tensor")])
                    return [tok]

                def lora(i, w1, w2, r, func, evac, rows=False):
                    ready = mixed(i)
                    with ExitStack() as lo:
                        n1 = -(-r // P)
                        W1 = self.sb(lo, "lora1", [P, KT, r])
                        W2 = ar[:, 4:8, :, :, :].rearrange("p (j k) c a u -> p j (k c a u)", j=2)
                        mid = self.sb(lo, "lora_mid", [P, n1, T])
                        c1 = [p.dma(W1[:, :, :], w1.rearrange("(k p) r -> p k r", p=P))]
                        for j in range(n1):
                            m = min(P, r - j * P)
                            c1.append(p.dma(W2[0:m, j, :], w2[j * P:j * P + m, :]))
                        for j in range(n1):
                            m = min(P, r - j * P)
                            bank = p.banks.next()
                            got = p.product(bank, bank.t[0:m, 0:T], [(W1[:, k, j * P:j * P + m], xi[:, k, :])
                                                                     for k in range(KT)], after=ready + c1)
                            mt = p.S(mid[0:m, j, :], bank.t[0:m, 0:T], func, after=[got])
                            bank.readers.append(mt)
                        sizes = [min(P, r - j * P) for j in range(n1)]
                        if rows:
                            for t in range(TT):
                                for g in range(2):
                                    bank = p.banks.next()
                                    got = p.product(bank, bank.t[:, :],
                                                    [(mid[0:m, j, t * P:(t + 1) * P], W2[0:m, j, g * 512:g * 512 + 512])
                                                     for j, m in enumerate(sizes)], after=[mt])
                                    bank.readers.append(evac(t, g * 512, bank.t[:, :], got))
                        else:
                            for f in range(KT):
                                bank = p.banks.next()
                                got = p.product(bank, bank.t[:, 0:T], [(W2[0:m, j, f * P:(f + 1) * P], mid[0:m, j, :])
                                                                       for j, m in enumerate(sizes)], after=[mt])
                                bank.readers.append(evac(f, bank.t[:, 0:T], got))
                        p.barrier()
                rkv = A["rw_rkv_2"][0]
                self.to_cols(xi, D, rkv[0], self.copier(r_), ready=mixed(0))
                self.to_cols(xi, D, rkv[1], self.copier(k_), ready=mixed(2))
                if True:
                    vr = ar[:, 0:4, :, :, :].rearrange("p (t k) c a u -> p t (k c a u)", t=TT)
                    self.to_rows(xi, D, rkv[2], lambda t, f0, ps, got: p.V(self.cp, vr[:, t, f0:f0 + 512], ps, after=[got]),
                                 ready=mixed(3))
                    p.dma(self.v_dram.rearrange("(t p) d -> p t d", p=P), vr[:, :, :], after=[p.last["vector"]])
                    p.barrier()
                lora(1, A["rw_w1_2"][0], A["rw_w2_2"][0], 64, ACT.Tanh,
                     lambda f, ps, got: p.S(w_[:, f, :], ps, ACT.Sigmoid, bias=par[:, W0 + f:W0 + f + 1], after=[got]))
                lora(4, A["rw_a1_2"][0], A["rw_a2_2"][0], 64, ACT.Identity,
                     lambda f, ps, got: p.S(a_[:, f, :], ps, ACT.Sigmoid, bias=par[:, A0 + f:A0 + f + 1], after=[got]))
                lora(5, A["rw_g1_2"][0], A["rw_g2_2"][0], 160, ACT.Sigmoid,
                     lambda t, f0, ps, got: p.V(self.cp, gate[:, t, f0:f0 + 512], ps, after=[got]), rows=True)
                kk, cum = hp[:, :, 1:T + 1], xx
                bc = lambda at: par[:, at:at + 8].unsqueeze(2).to_broadcast([P, KT, T])
                p.V(self.tt, kk, k_[:, :, :], bc(KK), ALU.mult)
                sq = p.V(self.tt, xi[:, :, :], kk, kk, ALU.mult)
                for f in range(KT):
                    bank = p.banks.next()
                    got = p.product(bank, bank.t[:, 0:T], [(self.const("halves"), xi[:, f, :])], after=[sq])
                    s = p.S(cum[:, f, :], bank.t[:, 0:T], ACT.Sqrt, after=[got])
                    bank.readers.append(s)
                p.V(self.ts, xi[:, :, :], cum[:, :, :], 1e-12, None, ALU.max, after=[s])
                p.V(v.reciprocal, xi[:, :, :], xi[:, :, :])
                p.V(self.tt, kk, kk, xi[:, :, :], ALU.mult)
                p.V(self.ts, xi[:, :, :], a_[:, :, :], -1.0, None, ALU.add)
                p.V(self.tt, xi[:, :, :], xi[:, :, :], bc(KA), ALU.mult)
                p.V(self.stt, out=k_[:, :, :], in0=xi[:, :, :], scalar=1.0, in1=k_[:, :, :], op0=ALU.add, op1=ALU.mult)
                p.V(self.tt, a_[:, :, :], a_[:, :, :], kk, ALU.mult)
                wl = p.V(self.ts, w_[:, :, :], w_[:, :, :], -float(np.exp(-0.5)), None, ALU.mult)
                for f in range(KT):
                    cu = p.V(v.tensor_tensor_scan, cum[:, f, :], self.const("restart"), w_[:, f, :], 0.0,
                             ALU.mult, ALU.add)
                chunks = lambda a: a.rearrange("p k (c t) -> p k c t", t=CH)
                e1 = p.S(xi[:, :, :], cum[:, :, :], ACT.Exp, after=[cu])
                p.V(self.cp, wend[:, :, :], chunks(xi[:, :, :])[:, :, :, CH - 1], after=[e1])
                for f in range(KT):
                    p.V(self.tt, ar[:, f, :, 1, :], chunks(r_[:, :, :])[:, f, :, :], chunks(xi[:, :, :])[:, f, :, :], ALU.mult)
                p.V(self.tt, prod[:, :, :], r_[:, :, :], k_[:, :, :], ALU.mult)
                p.V(self.tt, prod[:, :, :], prod[:, :, :], bc(RK), ALU.mult)
                d = p.V(self.tt, w_[:, :, :], cum[:, :, :], w_[:, :, :], ALU.subtract)
                e2 = p.S(w_[:, :, :], w_[:, :, :], ACT.Exp, after=[d])
                for f in range(KT):
                    p.V(self.stt, out=ar[:, f, :, 0, :], in0=chunks(w_[:, :, :])[:, f, :, :], scalar=-1.0,
                        in1=chunks(kk)[:, f, :, :], op0=ALU.mult, op1=ALU.mult, after=[e2])
                e3 = p.S(xi[:, :, :], cum[:, :, :], ACT.Exp, scale=-1.0, after=[p.last["vector"]])
                p.V(self.tt, bh[:, :, :], a_[:, :, :], xi[:, :, :], ALU.mult, after=[e3])
                p.V(self.tt, kh[:, :, :], k_[:, :, :], xi[:, :, :], ALU.mult)
                p.barrier()
            for n_, ap_ in (("w_at", ar[:, :, :, 0, :]), ("w_rt", ar[:, :, :, 1, :])):
                if n_ in self.debug:
                    for f in range(8):
                        p.dma(self.debug[n_].rearrange("p k (c t) -> p k c t", t=CH)[:, f], ap_[:, f])
            self.show("w_bh", bh[:, :, :])
            self.show("w_kh", kh[:, :, :])
            p.barrier()
            yv = kh[:, :, :].rearrange("p c (h d) -> p c h d", d=HD)
            self.wkv(top, ar, bh, kh, wend, prod, yv)
            p.barrier()
            tok = []
            for q in range(4):
                dst = self.y_dram[:, q * 256:(q + 1) * 256].rearrange("(c s) f -> s c f", s=CH)
                tok.append(p.dma(dst, yv[q * CH:(q + 1) * CH, :, :, :].rearrange("s c h d -> s c (h d)")))
            yr = self.sb(top, "y_rows", [P, TT, D])
            back = p.dma(yr[:, :, :], self.y_dram.rearrange("(t p) d -> p t d", p=P), after=tok)
            m = p.V(self.tt, yr[:, :, :], yr[:, :, :], gate[:, :, :], ALU.mult, after=[back])
            yT = ar[:, :, :, :, :].rearrange("p k c a t -> p k (c a t)")
            ready = self.turned(yr, yT, after=[m])
            self.to_rows(yT, D, A["rw_wo_2"][0],
                         lambda t, f0, ps, got: p.V(self.cp, y_out[:, t, f0:f0 + 512], ps, after=[got]), ready=[ready])
            p.barrier()

    def wkv(self, top, ar, bh, kh, wend, prod, yv):
        p, nc, A, v = self.p, self.nc, self.A, self.nc.vector
        ident = self.const("ident")
        tri = self.const("tri")
        with ExitStack() as tmp:
            bar = self.sb(tmp, "b_ar", [P, NCH, 4, 2, CH])
            kar = self.sb(tmp, "k_ar", [P, NCH, 4, 2, CH])
            brow = self.sb(tmp, "b_chunk_rows", [P, NCH, 4, HD])
            krow = self.sb(tmp, "k_chunk_rows", [P, NCH, 4, HD])
            vrow = self.sb(tmp, "v_chunk_rows", [P, NCH, 4, HD])
            bonus = self.sb(tmp, "bonus", [P, NCH, 4])
            gn = self.sb(tmp, "group_norm", [P, 2, 4, HD])
            for q in range(4):
                part = slice(q * CH, (q + 1) * CH)
                p.dma(vrow[part, :, :, :].rearrange("s c h d -> s c (h d)"),
                      self.v_dram[:, q * 256:(q + 1) * 256].rearrange("(c s) f -> s c f", s=CH))
                for i, name in enumerate(("rw_gn_g_2", "rw_gn_b_2")):
                    p.dma(gn[part, i, :, :].rearrange("s h d -> s (h d)"),
                          A[name][0, q * 256:(q + 1) * 256].partition_broadcast(CH))
            for src, dst in ((bh, bar), (kh, kar)):
                for c2 in range(NCH // 2):
                    bank = p.banks.next()
                    for b, ci, hh in [(b, ci, hh) for b in range(2) for ci in range(2) for hh in range(KT)]:
                            c, h = 2 * c2 + ci, 2 * hh + b
                            order = [got] if b and not (ci or hh) else []
                            q, i, half, pair = h // 4, h % 4, slice(HD * (h % 2), HD * (h % 2) + HD), h // 2
                            col = (ci * 4 + i) * 64
                            got = p.product(bank, bank.t[q * CH:(q + 1) * CH, col:col + 64],
                                            [(src[half, pair, c * CH:(c + 1) * CH],
                                              ar[half, pair, c, :, :].rearrange("p a t -> p (a t)"))],
                                            after=order, tile_position=(HD * (h % 2), q * CH))
                    mask = tri.unsqueeze(1).to_broadcast([P, 8, 64])
                    out = dst[:, 2 * c2:2 * c2 + 2, :, :, :].rearrange("p c h a t -> p (c h) (a t)")
                    bank.readers.append(p.V(self.tt, out, bank.t[:, :].rearrange("p (g n) -> p g n", n=64), mask,
                                            ALU.mult, after=[got]))
            for src, dst in ((bh, brow), (kh, krow)):
                for c2 in range(NCH // 2):
                    bank = p.banks.next()
                    for ci in range(2):
                        c = 2 * c2 + ci
                        for pair in range(KT):
                            q = pair // 2
                            col = (ci * 4 + 2 * (pair % 2)) * HD
                            got = p.product(bank, bank.t[q * CH:(q + 1) * CH, col:col + P],
                                            [(src[:, pair, c * CH:(c + 1) * CH], ident)],
                                            tile_position=(0, q * CH))
                    out = dst[:, 2 * c2:2 * c2 + 2, :, :].rearrange("p c h d -> p (c h d)")
                    bank.readers.append(p.V(self.cp, out, bank.t[:, :], after=[got]))
            bank = p.banks.next()
            for c in range(NCH):
                for pair in range(KT):
                    q, col = pair // 2, c * 4 + 2 * (pair % 2)
                    got = p.product(bank, bank.t[q * CH:(q + 1) * CH, col:col + 2],
                                    [(prod[:, pair, c * CH:(c + 1) * CH], self.const("half2"))],
                                    tile_position=(0, q * CH))
            bank.readers.append(p.V(self.cp, bonus[:, :, :].rearrange("p c h -> p (c h)"), bank.t[:, 0:32], after=[got]))
            p.barrier()
            square = lambda a, i: a[:, 4 * i:4 * i + 4, :].rearrange("p k (a b) -> p (k a) b", b=CH)
            L, inv, flat, work, zs = square(bh, 0), square(bh, 1), square(kh, 0), square(kh, 1), square(prod, 0)
            pairs = lambda a: a.rearrange("p t n -> p (t n)")
            p.V(self.cp, flat[:, :, :], bar[:, :, :, 0, :].rearrange("p c h t -> p t (c h)"))
            p.V(v.transpose, pairs(L[:, :, :]), pairs(flat[:, :, :]))
            p.V(v.memset, inv[:, :, :], 0.0)
            p.V(v.memset, pairs(inv[:, :, :])[:, 0:CH * CH:CH + 1], 1.0)
            for t in range(1, CH):
                w = work[:, 0:t, 0:t]
                p.V(self.tt, w, inv[:, 0:t, 0:t].rearrange("p s u -> p u s"),
                    L[:, t:t + 1, 0:t].to_broadcast([P, t, t]), ALU.mult)
                p.V(v.tensor_reduce, inv[:, t, 0:t], w, AX.X, ALU.add)
            solved = p.V(v.transpose, pairs(zs[:, :, :]), pairs(inv[:, :, :]))
            state = self.sb(tmp, "state", [P, KT, HD])
            xs = self.sb(tmp, "x_chunk", [P, 4, HD])
            sa = self.sb(tmp, "sa_chunk", [P, 4, HD])
            ready = p.V(v.memset, state[:, :, :], 0.0)
            head = lambda h: (h // 4, h % 4, h % 2, h // 2)
            for c in range(NCH):
                p.barrier() if c == 0 else None
                def chunk_products(bank, parts, ready):
                    got, after = None, [*bank.free(), *ready]
                    for j, part in enumerate(parts):
                        for group in part[0]:
                            for h in group:
                                q, i, b, pair = head(h)
                                l, r = part[1](h)
                                row = HD * b if len(part[0]) == 2 else q * CH
                                got = p.put("tensor", nc.tensor.matmul, bank.t[q * CH:(q + 1) * CH, i * HD:(i + 1) * HD],
                                            l, r, start=j == 0 and h % 4 == 0, stop=j == len(parts) - 1, skip_group_check=True,
                                            tile_position=(row, q * CH), after=after, chain=False,
                                            signal=h == group[-1])
                                after = ()
                            after = [got]
                    return got
                halves = [range(b, N_HEADS, 2) for b in range(2)]
                every = [range(N_HEADS)]
                own = lambda h: (slice(HD * (h % 2), HD * (h % 2) + HD), h // 2)
                grp = lambda h: (slice(h // 4 * CH, h // 4 * CH + CH), h % 4)
                from_state = lambda n: (halves, lambda h: (ar[own(h)[0], own(h)[1], c, n, :], state[own(h)[0], own(h)[1], :]))
                from_v = lambda n: (every, lambda h: (kar[grp(h)[0], c, grp(h)[1], n, :], vrow[grp(h)[0], c, grp(h)[1], :]))
                bank = p.banks.next()
                got = chunk_products(bank, [from_state(0), from_v(0)], [ready])
                x_ready = p.V(self.cp, xs[:, :, :].rearrange("p h d -> p (h d)"), bank.t[:, 0:256], after=[got])
                bank.readers.append(x_ready)
                bank = p.banks.next()
                for h in range(N_HEADS):
                    q, i, b, pair = head(h)
                    g = slice(q * CH, (q + 1) * CH)
                    got = p.product(bank, bank.t[g, i * HD:(i + 1) * HD], [(zs[g, :, c * 4 + i], xs[g, i, :])],
                                    after=[x_ready], tile_position=(q * CH, q * CH))
                sa_ready = p.V(self.cp, sa[:, :, :].rearrange("p h d -> p (h d)"), bank.t[:, 0:256], after=[got])
                bank.readers.append(sa_ready)
                bank = p.banks.next()
                from_sa = (every, lambda h: (bar[grp(h)[0], c, grp(h)[1], 1, :], sa[grp(h)[0], grp(h)[1], :]))
                got = chunk_products(bank, [from_state(1), from_v(1), from_sa], [sa_ready])
                bank.readers.append(p.V(self.cp, yv[:, c, :, :].rearrange("p h d -> p (h d)"), bank.t[:, 0:256], after=[got]))
                if c == NCH - 1:
                    continue
                bank = p.banks.next()
                for h in range(N_HEADS):
                    q, i, b, pair = head(h)
                    g, half = slice(q * CH, (q + 1) * CH), slice(HD * b, HD * b + HD)
                    out = bank.t[half, pair * HD:(pair + 1) * HD]
                    order = [got] if q and i == 0 else []
                    got = p.product(bank, out, [(brow[g, c, i, :], sa[g, i, :]), (krow[g, c, i, :], vrow[g, c, i, :])],
                                    after=order,
                                    tile_position=(q * CH, HD * b))
                add = p.V(self.tt, state[:, :, :], state[:, :, :],
                          bank.t[:, :].rearrange("p (k d) -> p k d", d=HD), ALU.add, after=[got])
                bank.readers.append(add)
                ready = p.V(self.tt, state[:, :, :], state[:, :, :],
                            wend[:, :, c].unsqueeze(2).to_broadcast([P, KT, HD]), ALU.mult)
            self.show("w_y", yv[:, :, :, :])
            y3 = yv[:, :, :, :].rearrange("p c h d -> p (c h) d")
            s1, s2 = self.sb(tmp, "gn_mean", [P, 32]), self.sb(tmp, "gn_var", [P, 32])
            sq = brow[:, :, :, :].rearrange("p c h d -> p (c h) d")
            wide = lambda a: a.unsqueeze(2).to_broadcast([P, 32, HD])
            p.barrier()
            p.V(v.tensor_reduce, s1[:, :], y3, AX.X, ALU.add)
            p.V(self.ts, s1[:, :], s1[:, :], 1.0 / HD, None, ALU.mult)
            p.V(self.tt, y3, y3, wide(s1[:, :]), ALU.subtract)
            p.V(self.tt, sq, y3, y3, ALU.mult)
            p.V(v.tensor_reduce, s2[:, :], sq, AX.X, ALU.add)
            r = self.rstd(s2[:, :], HD, 64e-5, tmp)
            p.V(self.tt, y3, y3, wide(s2[:, :]), ALU.mult, after=[r])
            gains = lambda i: gn[:, i, :, :].unsqueeze(1).to_broadcast([P, NCH, 4, HD])
            p.V(self.tt, yv[:, :, :, :], yv[:, :, :, :], gains(0), ALU.mult)
            p.V(self.tt, yv[:, :, :, :], yv[:, :, :, :], gains(1), ALU.add)
            v3 = vrow[:, :, :, :].rearrange("p c h d -> p (c h) d")
            p.V(self.tt, sq, v3, wide(bonus[:, :, :].rearrange("p c h -> p (c h)")), ALU.mult)
            p.V(self.tt, y3, y3, sq, ALU.add)
            p.barrier()

    def shared_kv(self, scale, shift):
        p, nc, A, v = self.p, self.nc, self.A, self.nc.vector
        with ExitStack() as tmp:
            hk = self.sb(tmp, "kv_in_cols", [P, KT, T])
            k = self.sb(tmp, "fox_k_rows", [P, TT, N_HEADS, HD])
            gain = self.sb(tmp, "k_gain", [P, HD])
            wf = self.sb(tmp, "forget_w", [P, KT, N_HEADS])
            fb = self.sb(tmp, "forget_b", [N_HEADS, 1])
            w = A["kv_w_2"]
            c = [p.dma(gain[:, :], A["kv_knorm_2"].partition_broadcast(P)),
                 p.dma(wf[:, :, :], w[:, 2 * D:2 * D + N_HEADS].rearrange("(k p) n -> p k n", p=P)),
                 p.dma(fb[:, :], A["kv_fb_2"].rearrange("(n a) -> n a", a=1))]
            ready = self.turned(self.x, hk, 0, scale, shift)
            flat = lambda a: a.rearrange("p h d -> p (h d)")
            self.to_rows(hk, D, w[:, 0:D], lambda t, f0, ps, got: p.V(self.cp, flat(k[:, t, :, :])[:, f0:f0 + 512], ps, after=[got]),
                         ready=[ready])
            self.to_rows(hk, D, w[:, D:2 * D],
                         lambda t, f0, ps, got: p.V(self.cp, flat(self.val[:, t, :, :])[:, f0:f0 + 512], ps, after=[got]))
            bank = p.banks.next()
            got = p.product(bank, bank.t[0:N_HEADS, 0:T], [(wf[:, k_, :], hk[:, k_, :]) for k_ in range(KT)], after=c)
            f, e, g = (self.sb(tmp, n, [N_HEADS, T]) for n in ("forget", "forget_exp", "forget_abs"))
            bank.readers.append(p.V(self.ts, f[:, :], bank.t[0:N_HEADS, 0:T], fb[:, 0:1], None, ALU.add, after=[got, *c]))
            a = p.V(self.stt, out=g[:, :], in0=f[:, :], scalar=-1.0, in1=f[:, :], op0=ALU.mult, op1=ALU.max)
            ex = p.S(e[:, :], g[:, :], ACT.Exp, scale=-1.0, after=[a])
            a = p.V(self.ts, e[:, :], e[:, :], 1.0, None, ALU.add, after=[ex])
            ln = p.S(e[:, :], e[:, :], ACT.Ln, after=[a])
            p.V(self.stt, out=f[:, :], in0=f[:, :], scalar=0.0, in1=e[:, :], op0=ALU.min, op1=ALU.subtract, after=[ln])
            p.V(v.tensor_tensor_scan, g[:, :], self.ones[0:N_HEADS, 0:1].to_broadcast([N_HEADS, T]), f[:, :], 0.0,
                ALU.mult, ALU.add)
            n = p.V(self.ts, e[:, :], g[:, :], -1.0, None, ALU.mult)
            p.dma(self.f_dram[0], g[:, :], after=[n])
            p.dma(self.f_dram[1], e[:, :], after=[n])
            for t in range(TT):
                self.head_rms(k[:, t, :, :], N_HEADS, gain[:, :], tmp)
            self.turned(k[:, :, :, :].rearrange("p t h d -> p t (h d)"), self.kT, after=[p.last["vector"]])
            p.barrier()

    def fox(self, y_out, scale, shift):
        p, nc, A, v = self.p, self.nc, self.A, self.nc.vector
        with ExitStack() as tmp:
            hT = self.sb(tmp, "fox_in_cols", [P, KT, T])
            q = self.sb(tmp, "fox_q_rows", [P, TT, N_HEADS, HD])
            gt = self.sb(tmp, "fox_gate_rows", [P, TT, D])
            gain = self.sb(tmp, "q_gain", [P, HD])
            came = p.dma(gain[:, :], A["fx_qnorm_2"][0].partition_broadcast(P))
            fq = self.sb(tmp, "forget_q", [2, N_HEADS, T])
            fk = self.sb(tmp, "forget_k", [2, N_HEADS, T])
            p.V(v.memset, fq[:, :, :], 1.0)
            m = p.V(v.memset, fk[:, :, :], 1.0)
            p.dma(fq[0:1, :, :], self.f_dram[0:1], after=[m])
            p.dma(fk[1:2, :, :], self.f_dram[1:2], after=[m])
            ready = self.turned(self.x, hT, 0, scale, shift)
            flat = lambda a: a.rearrange("p h d -> p (h d)")
            w = A["fx_wqg_2"][0]
            self.to_rows(hT, D, w[:, 0:D], lambda t, f0, ps, got: p.V(self.cp, flat(q[:, t, :, :])[:, f0:f0 + 512], ps, after=[got]),
                         ready=[ready])
            self.to_rows(hT, D, w[:, D:2 * D],
                         lambda t, f0, ps, got: p.S(gt[:, t, f0:f0 + 512], ps, ACT.Sigmoid, after=[got]))
            with ExitStack() as t2:
                p.wait("vector", [came])
                for t in range(TT):
                    self.head_rms(q[:, t, :, :], N_HEADS, gain[:, :], t2)
                p.V(self.ts, q[:, :, :, :], q[:, :, :, :], HD ** -0.5, None, ALU.mult)
                p.barrier()
            qT = hT
            self.turned(q[:, :, :, :].rearrange("p t h d -> p t (h d)"), qT)
            p.barrier()
            y = q[:, :, :, :].rearrange("p t h d -> p t (h d)")
            items = []
            for h in range(N_HEADS):
                half = slice(HD * (h % 2), HD * (h % 2) + HD)
                for t in range(TT):
                    n = (t + 1) * P
                    items.append(dict(q=qT[half, h // 2, t * P:(t + 1) * P], keys=self.kT[half, h // 2, 0:n], n=n,
                                      extra=[(slice(0, n), fq[:, h, t * P:(t + 1) * P], fk[:, h, 0:n]),
                                             (slice(n - P, n), self.const("ident"), self.const("causal"))],
                                      values=lambda k, h=h: self.val[:, k, h, :],
                                      out=y[:, t, h * HD:(h + 1) * HD], ready=[]))
            self.attention(items, 1.0)
            for t in range(TT):
                m = p.V(self.tt, y[:, t, :], y[:, t, :], gt[:, t, :], ALU.mult)
            oT = hT
            ready = self.turned(y, oT, after=[m])
            self.to_rows(oT, D, A["fx_wo_2"][0],
                         lambda t, f0, ps, got: p.V(self.cp, y_out[:, t, f0:f0 + 512], ps, after=[got]), ready=[ready])
            p.barrier()


def two_blocks(nc, inputs, consts, out, debug=None, upto=2):
    with ExitStack() as stack:
        m = Model(nc, stack, inputs, consts, out, debug)
        m.first_block()
        if upto > 1:
            m.second_block()
        m.p.wait("gpsimd", m.p.transfers())
        m.p.emit(stack.enter_context(nc.Block()))


USED = ["x", "c", "ctx", "c_ctx", "w_mod", "b_mod", "norm1_g", "norm2_g", "w_in", "q_norm_g", "k_norm_g", "na_rpb",
        "conv_w", "conv_b", "conv_norm_g", "w_branch", "w_out", "w_router", "router_bias", "w_expert_gu",
        "w_expert_down", "final_norm_g", "c_2", "ada_w_2", "ada_b_2", "ln_g_2", "ln_b_2", "rw_mu_2", "rw_rkv_2",
        "rw_w0_2", "rw_w1_2", "rw_w2_2", "rw_a0_2", "rw_a1_2", "rw_a2_2", "rw_g1_2", "rw_g2_2", "rw_kk_2", "rw_ka_2",
        "rw_rk_2", "rw_gn_g_2", "rw_gn_b_2", "rw_wo_2", "kv_ada_w_2", "kv_ada_b_2", "kv_w_2", "kv_fb_2", "kv_knorm_2",
        "fx_wqg_2", "fx_qnorm_2", "fx_wo_2", "moe_wgrp_2", "moe_bgrp_2", "moe_wexp_2", "moe_bexp_2", "moe_wgate_2",
        "moe_wup_2", "moe_wdown_2"]


def kernel(**inputs):
    import concourse.bacc as bacc
    from concourse.bass_utils import run_bass_kernel_spmd

    nc = bacc.Bacc("TRN2", target_bir_lowering=False, num_devices=1)
    arrays, aps = {}, {}
    for name in USED:
        a = np.ascontiguousarray(inputs[name])
        arrays[f"in_{name}"] = a
        aps[name] = nc.dram_tensor(f"in_{name}", a.shape, F32, kind="ExternalInput").ap()
    arrays["in_constants"] = shape_constants()
    consts = nc.dram_tensor("in_constants", (P, CONST_WIDTH), F32, kind="ExternalInput").ap()
    out = nc.dram_tensor("out", (1, T, D), F32, kind="ExternalOutput").ap()
    two_blocks(nc, aps, consts, out)
    r = run_bass_kernel_spmd(nc, [arrays], core_ids=[0])
    return r.results[0]["out"]
```

```python
from contextlib import ExitStack

import numpy as np

import concourse.bass as bass
from concourse import mybir

F32 = mybir.dt.float32
ALU = mybir.AluOpType
ACT = mybir.ActivationFunctionType
AX = mybir.AxisListType

P = 128
D = 1024
T = 256
TT = T // P
KT = D // P
HD = 64
BIG = 1e30
CH = 32
NCH = T // CH
CAP = 64
N_HEADS = D // HD
GRID_W = 64
ALPHA = 4.0 ** 0.25

CONST = {}
_at = 0
for _name, _width in (("ident", 128), ("cos", 64), ("sin", 64), ("window", 64), ("reverse", 128), ("before", 128), ("slot", 128), ("causal", 128), ("tri", 64), ("restart", 256),
                      ("halves", 128), ("half2", 2), ("first4", 4), ("first32", 32),
                      ("cs_group", 256), ("cos_seq", 512), ("sin_seq", 512)):
    CONST[_name] = (_at, _width)
    _at += _width
CONST_WIDTH = _at
KEPT_WIDTH = CONST["cs_group"][0]


def shape_constants():
    c = np.zeros((P, CONST_WIDTH), np.float32)

    def put(name, a):
        at, width = CONST[name]
        c[:, at:at + width] = np.asarray(a, np.float32).reshape(P, width)

    p = np.arange(P)
    put("ident", np.eye(P))
    t = np.arange(T)
    inv = (np.float32(10000.0) ** (-np.arange(16, dtype=np.float32) / np.float32(16))).astype(np.float32)
    row, col = (t // GRID_W).astype(np.float32), (t % GRID_W).astype(np.float32)
    ang = np.concatenate([row[:, None] * inv, col[:, None] * inv], axis=1).astype(np.float32)
    rows = lambda a: a.reshape(TT, P, -1).transpose(1, 0, 2)
    put("cos", rows(np.cos(ang)))
    put("sin", rows(np.sin(ang)))
    ag = 2 * np.pi * ((p[:, None] * p[None, :]) % P) / P
    put("cs_group", np.concatenate([np.cos(ag), np.sin(ag)], axis=1))
    al = 2 * np.pi * ((t[:, None] * t[None, :]) % T) / T
    norm = 1.0 / np.sqrt(T * P)
    put("cos_seq", rows(np.cos(al) * norm))
    put("sin_seq", rows(-np.sin(al) * norm))
    w = np.arange(GRID_W)
    start = np.clip(w - 8, 0, GRID_W - 16)
    inside = (w[None, :] >= start[:, None]) & (w[None, :] < start[:, None] + 16)
    put("window", np.tile(np.where(inside, 0.0, -BIG)[::-1], (2, 1)))
    put("reverse", np.kron(np.eye(2), np.eye(GRID_W)[::-1]))
    put("causal", np.where(p[None, :] <= p[:, None], 0.0, -BIG))
    s, u = np.arange(P) % CH, np.arange(CH)
    put("tri", np.concatenate([s[:, None] < u[None, :], s[:, None] <= u[None, :]], axis=1))
    put("restart", np.tile((t % CH != 0).astype(np.float32), (P, 1)))
    put("halves", (p[:, None] // HD) == (p[None, :] // HD))
    put("half2", (p[:, None] // HD) == np.arange(2)[None, :])
    put("before", p[:, None] < p[None, :])
    put("slot", np.tile(p % CAP, (P, 1)))
    put("first4", np.tile(4.0 - np.arange(4), (P, 1)))
    put("first32", np.tile(32.0 - np.arange(32), (P, 1)))
    return c


class Buffer:

    def __init__(self, t):
        self.t = t
        self.readers = []

    def free(self):
        said, self.readers = self.readers, []
        return said


class Ring:

    def __init__(self, tensors):
        self.buffers = [Buffer(t) for t in tensors]
        self.n = 0

    def next(self):
        b = self.buffers[self.n % len(self.buffers)]
        self.n += 1
        return b


class Program:

    COMPUTE = ("tensor", "vector", "scalar", "gpsimd")

    def __init__(self, nc, stack, slots):
        self.nc, self.stack = nc, stack
        self.queue = {e: [] for e in (*self.COMPUTE, "sync")}
        self.done = {e: stack.enter_context(nc.semaphore(f"{e}_done")) for e in self.COMPUTE}
        self.count = dict.fromkeys(self.COMPUTE, 0)
        self.last = {}
        self.seen = {}
        self.floor = {e: [] for e in self.queue}
        self.lanes = {e: [[stack.enter_context(nc.semaphore(f"{e}_dma{i}")), 0] for i in range(n)]
                      for e, n in (("gpsimd", 16), ("scalar", 16), ("aside", 16))}
        self.lane = dict.fromkeys(self.lanes, 0)
        self.banks = Ring([stack.enter_context(nc.psum_tensor(f"bank{i}", [P, 512], F32)) for i in range(8)])
        self.memory = stack.enter_context(nc.sbuf_tensor("weights", [P, slots, 4096], F32))
        self.slots = Ring([self.memory[:, i, :] for i in range(slots)])
        self.landed = {}
        for i, b in enumerate(self.slots.buffers):
            self.landed[b] = [stack.enter_context(nc.semaphore(f"weights{i}_landed")), 0]

    def wait(self, engine, tokens):
        for token in tokens:
            if token is None:
                continue
            sem, value = token
            key = (engine, sem.name)
            if self.seen.get(key, 0) < value:
                self.seen[key] = value
                self.queue[engine].append(("wait", sem, value))

    def put(self, engine, call, *args, after=(), signal=True, chain=True, **kw):
        self.wait(engine, self.floor[engine])
        self.floor[engine] = []
        self.wait(engine, after)
        if chain:
            self.wait(engine, [self.last.get(engine)])
        token = None
        if signal:
            self.count[engine] += 1
            token = (self.done[engine], self.count[engine])
            self.last[engine] = token
        self.queue[engine].append(("do", call, args, kw, (self.done[engine], 1) if signal else None))
        return token

    def V(self, call, *args, **kw):
        return self.put("vector", call, *args, **kw)

    def S(self, *args, **kw):
        return self.put("scalar", self.nc.scalar.activation, *args, **kw)

    def G(self, call, *args, **kw):
        return self.put("gpsimd", call, *args, **kw)

    def dma(self, out, in_, after=(), engine="gpsimd", aside=False):
        lanes = "aside" if aside else engine
        lane = self.lanes[lanes][self.lane[lanes] % len(self.lanes[lanes])]
        self.lane[lanes] += 1
        self.wait(engine, self.floor[engine])
        self.floor[engine] = []
        self.wait(engine, after)
        if lane[1]:
            self.wait(engine, [(lane[0], lane[1])])
        lane[1] += 16
        call = self.nc.gpsimd.dma_start if engine == "gpsimd" else self.nc.scalar.dma_start
        self.queue[engine].append(("do", call, (out, in_), {}, (lane[0], 16)))
        return lane[0], lane[1]

    def dma_first(self, out, in_, sem):
        self.queue["sync"].append(("do", self.nc.sync.dma_start, (out, in_), {}, (sem, 16)))

    def transfers(self, aside=False):
        return [(lane[0], lane[1]) for name, lanes in self.lanes.items() for lane in lanes
                if lane[1] and (aside or name != "aside")]

    def barrier(self, aside=False):
        tokens = list(self.last.values()) + self.transfers(aside)
        for e in self.COMPUTE:
            self.floor[e] = list(tokens)

    def product(self, bank, out, pairs, after=(), **kw):
        after = [*bank.free(), *after]
        token = None
        for i, (lhsT, rhs) in enumerate(pairs):
            token = self.put("tensor", self.nc.tensor.matmul, out, lhsT, rhs, start=i == 0,
                             stop=i == len(pairs) - 1, after=after, chain=False,
                             signal=i == len(pairs) - 1, **kw)
            after = ()
        return token

    def turn(self, bank, out, in_, ident, after=(), signal=True):
        return self.put("tensor", self.nc.tensor.transpose, out, in_, ident,
                        after=[*bank.free(), *after], chain=False, signal=signal)

    def weights(self, src, n):
        b = self.slots.next()
        kt = src.shape[0] // P
        view = b.t[:, 0:kt * n].rearrange("p (k n) -> p k n", n=n)
        self.wait("sync", b.free())
        landed = self.landed[b]
        landed[1] += 16
        self.queue["sync"].append(("do", self.nc.sync.dma_start,
                                   (view, src.rearrange("(k p) n -> p k n", p=P)), {}, (landed[0], 16)))
        return b, view, (landed[0], landed[1])

    def weight_parts(self, parts):
        b = self.slots.next()
        self.wait("sync", b.free())
        landed = self.landed[b]
        for dst, src in parts(b.t):
            landed[1] += 16
            self.queue["sync"].append(("do", self.nc.sync.dma_start, (dst, src), {}, (landed[0], 16)))
        return b, (landed[0], landed[1])

    def weight_pair(self, srcs):
        i = self.slots.n % len(self.slots.buffers)
        got = [self.weights(w, 512) for w in srcs]
        return [g[0] for g in got], self.memory[:, i:i + 2, :].rearrange("p w (k n) -> p k w n", n=512), \
            [g[2] for g in got]

    def align(self, n):
        while self.slots.n % n:
            self.slots.n += 1

    def branch(self, flag, body):
        engines = ("tensor", "vector", "scalar", "sync")
        for e in engines:
            self.wait(e, self.floor[e])
            self.floor[e] = []
        outer = {e: self.queue[e] for e in engines}
        seen, counts = dict(self.seen), dict(self.count)
        landed = {b: l[1] for b, l in self.landed.items()}
        for e in engines:
            self.queue[e] = []
        body()
        for e in engines:
            inner, skipped = self.queue[e], []
            if e == "sync":
                for b, l in self.landed.items():
                    if l[1] > landed[b]:
                        if landed[b]:
                            skipped.append(("wait", l[0], landed[b]))
                        skipped.append(("inc", l[0], l[1] - landed[b]))
            elif self.count[e] > counts[e]:
                skipped += [("wait", self.done[e], counts[e]), ("inc", self.done[e], self.count[e] - counts[e])]
            self.queue[e] = outer[e]
            self.queue[e].append(("branch", flag, inner, skipped))
        self.seen = seen

    def emit(self, block):
        def run(eng, queue):
            for step in queue:
                if step[0] == "wait":
                    eng.wait_ge(step[1], step[2])
                elif step[0] == "inc":
                    eng.sem_inc(step[1], step[2])
                elif step[0] == "branch":
                    for taken in (False, True):
                        flag = eng.value_load(step[1], min_val=0, max_val=1)
                        with eng.If(flag != 0) if taken else eng.If(flag == 0):
                            run(eng, step[2] if taken else step[3])
                else:
                    _, call, args, kw, signal = step
                    ins = call(*args, **kw)
                    if signal:
                        ins.then_inc(*signal)

        @block.sync
        def _(eng):
            run(eng, self.queue["sync"])

        @block.gpsimd
        def _(eng):
            run(eng, self.queue["gpsimd"])

        @block.scalar
        def _(eng):
            run(eng, self.queue["scalar"])

        @block.tensor
        def _(eng):
            run(eng, self.queue["tensor"])

        @block.vector
        def _(eng):
            run(eng, self.queue["vector"])


def pipeline(n, stages):
    for i in range(n + len(stages) - 1):
        for j, stage in enumerate(stages):
            if 0 <= i - j < n:
                stage(i - j)


class Model:

    def __init__(self, nc, stack, inputs, consts, out):
        self.nc, self.A, self.out = nc, inputs, out
        self.p = Program(nc, stack, 6)
        self.stack = stack
        self.names = 0
        v = nc.vector
        self.tt, self.ts, self.stt, self.cp = v.tensor_tensor, v.tensor_scalar, v.scalar_tensor_tensor, v.tensor_copy
        self.consts = self.sb(stack, "consts", [P, KEPT_WIDTH])
        self.all_consts = consts
        self.ones = self.sb(stack, "ones", [P, P])
        self.x = self.sb(stack, "x_rows", [P, TT, D])
        self.flags = [stack.enter_context(nc.sbuf_tensor(f"more_rounds{i}", [P, T // CAP * n], mybir.dt.int32))
                      for i, n in enumerate((32, 32, 16))]
        self.mod = nc.dram_tensor("mod_rows", (5, 6 * D), F32, kind="Internal").ap()
        self.f_dram = nc.dram_tensor("forget_rows", (2, N_HEADS, T), F32, kind="Internal").ap()
        p = self.p
        A, r8 = inputs, lambda a: a.rearrange("(k p) -> k p", p=P)
        self.rows1 = self.sb(stack, "vector_rows_a", [P, P])
        self.rows2 = self.sb(stack, "vector_rows_b", [P, P])
        self.mod2 = self.sb(stack, "mod2_cols", [P, 112])
        self.rw_par = self.rows2[:, 0:88]
        first = stack.enter_context(nc.semaphore("first_loads"))
        at = 0
        for vec in (A["norm1_g"][0], A["norm2_g"][0], A["conv_b"][0], A["conv_norm_g"][0], A["c"][0], A["c_ctx"], A["c_2"][0]):
            n = vec.shape[0] // P
            p.dma_first(self.rows1[at:at + n, :], r8(vec), first)
            at += n
        p.dma_first(self.rows2[0:124, :], A["conv_w"][0].rearrange("t (k p) -> (t k) p", p=P), first)
        p.dma_first(self.consts[:, :], consts[:, 0:KEPT_WIDTH], first)
        p.dma_first(self.x[:, :, :], A["x"][0].rearrange("(t p) d -> p t d", p=P), first)
        p.G(nc.gpsimd.memset, self.ones[:, :], 1.0)
        p.barrier()
        for e in p.COMPUTE:
            p.floor[e].append((first, 16 * 10))

    def sb(self, stack, name, shape):
        self.names += 1
        return stack.enter_context(self.nc.sbuf_tensor(f"{name}_{self.names}", shape, F32))

    def ring(self, stack, name, shape, n):
        return Ring([self.sb(stack, f"{name}{i}", shape) for i in range(n)])

    def const(self, name):
        at, width = CONST[name]
        return self.consts[:, at:at + width]

    def columns(self, out, vectors, biases=()):
        with ExitStack() as tmp:
            rows, more = self.sb(tmp, "vector_rows", [P, P]), self.sb(tmp, "bias_rows", [P, P])
            loaded = self.column_rows(rows, vectors) + self.column_rows(more, biases)
            token = self.turned_columns(out, rows, vectors, more, biases, loaded)
            self.p.barrier()
        return token

    def column_rows(self, rows, vectors, after=()):
        at, tokens = 0, []
        for v in vectors:
            tokens.append(self.p.dma(rows[at:at + v.shape[0], :], v, after=after, aside=True))
            at += v.shape[0]
        return tokens

    def turned_columns(self, out, rows, vectors, more, biases, loaded):
        p = self.p
        total = sum(v.shape[0] for v in vectors)
        if biases:
            loaded = [p.V(self.tt, rows[0:total, :], rows[0:total, :], more[0:total, :], ALU.add, after=loaded)]
            at = 0
            for v in vectors:
                p.dma(v, rows[at:at + v.shape[0], :], after=loaded)
                at += v.shape[0]
        b = p.banks.next()
        turned = p.turn(b, b.t[:, 0:total], rows[0:total, :], self.const("ident")[0:total, 0:total], after=loaded)
        token = p.V(self.cp, out, b.t[:, 0:total], after=[turned])
        b.readers.append(token)
        return token

    def modulation_tiles(self, stack, conds, jobs, results):
        p, nc = self.p, self.nc
        cs = self.sb(stack, "cond_silu", [P, KT, 32])
        for i, c in enumerate(conds):
            left = 32 - i if i == len(conds) - 1 else 1
            ready = p.S(cs[:, :, i:i + left], c.unsqueeze(2).to_broadcast([P, KT, left]), ACT.Silu)
        def tile(w, row, f):
            result, bank = results.next(), p.banks.next()
            slot, wv, landed = p.weights(w[:, f * 512:(f + 1) * 512], 512)
            after = [*bank.free(), ready, landed]
            for k in range(KT):
                for j in range(4):
                    got = p.put("tensor", nc.tensor.matmul, bank.t[32 * j:32 * j + 32, 0:P], cs[:, k, :],
                                wv[:, k, j * P:(j + 1) * P], start=k == 0, stop=k == KT - 1, tile_position=(0, 32 * j),
                                after=after, chain=False, signal=k == KT - 1 and j == 3)
                    after = ()
            slot.readers.append(got)
            done = p.V(self.cp, result.t[:, :], bank.t[:, 0:P], after=[got, *result.free()])
            bank.readers.append(done)
            for i in range(len(conds)):
                dst = self.mod[row + i, f * 512:(f + 1) * 512].rearrange("(j n) -> j n", n=P)
                result.readers.append(p.dma(dst, result.t[i:P:32, :], after=[done], aside=True))
        return [lambda w=w, row=row, f=f: tile(w, row, f) for w, row, fs in jobs for f in fs]

    def some_late_tiles(self, n):
        for tile in self.late_tiles[:n]:
            tile()
        del self.late_tiles[:n]

    def rstd(self, sums, n, eps, tmp):
        p = self.p
        p.V(self.ts, sums, sums, 1.0 / n, eps, ALU.mult, ALU.add)
        r = p.V(self.nc.vector.reciprocal, sums, sums)
        return p.S(sums, sums, ACT.Sqrt, after=[r])

    def turned(self, rows, cols, col0=0, scale=None, shift=None, after=(), kt=KT):
        p = self.p
        token = None
        for k in range(kt):
            b = p.banks.next()
            for t in range(TT):
                got = p.turn(b, b.t[:, t * P:(t + 1) * P], rows[:, t, k * P:(k + 1) * P],
                             self.const("ident"), after=after)
            out = cols[:, k, col0:col0 + T]
            if scale is None:
                token = p.V(self.cp, out, b.t[:, 0:T], after=[got])
            else:
                token = p.V(self.ts, out, b.t[:, 0:T], scale[:, k:k + 1], shift[:, k:k + 1],
                            ALU.mult, ALU.add, after=[got])
            b.readers.append(token)
        return token

    def rms_turned(self, x, cols, col0, scale, shift):
        p = self.p
        with ExitStack() as tmp:
            xn = self.sb(tmp, "x_normed", [P, TT, D])
            ss = self.sb(tmp, "square_sums", [P, TT])
            for t in range(TT):
                a = p.S(xn[:, t, :], x[:, t, :], ACT.Square, accum_out=ss[:, t:t + 1], after=[p.last.get("vector")])
            p.wait("vector", [a])
            r = self.rstd(ss[:, :], D, 1e-6, tmp)
            for t in range(TT):
                n = p.V(self.ts, xn[:, t, :], x[:, t, :], ss[:, t:t + 1], None, ALU.mult, after=[r])
            token = self.turned(xn, cols, col0, scale, shift, after=[n])
            p.barrier()
        return token

    def to_cols(self, src, F, w, evac, n=T, col0=0, ktiles=KT, ready=()):
        p = self.p
        step = 4096 // ktiles
        for f0 in range(0, F, step):
            wide = min(step, F - f0)
            slot, wv, landed = p.weights(w[:, f0:f0 + wide], wide)
            for f in range(f0, f0 + wide, P):
                bank = p.banks.next()
                got = p.product(bank, bank.t[:, 0:n],
                                [(wv[:, k, f - f0:f - f0 + P], src[:, k, col0:col0 + n]) for k in range(ktiles)],
                                after=[landed, *ready])
                bank.readers.append(evac(f // P, bank.t[:, 0:n], got))
            slot.readers.append(got)

    def to_rows(self, src, F, w, evac, tiles=TT, ktiles=KT, ready=()):
        p = self.p
        step = 4096 // ktiles
        for f0 in range(0, F, step):
            wide = min(step, F - f0)
            slot, wv, landed = p.weights(w[:, f0:f0 + wide], wide)
            for t in range(tiles):
                for g in range(0, wide, 512):
                    n = min(512, wide - g)
                    bank = p.banks.next()
                    got = p.product(bank, bank.t[:, 0:n],
                                    [(src[:, k, t * P:(t + 1) * P], wv[:, k, g:g + n]) for k in range(ktiles)],
                                    after=[landed, *ready])
                    bank.readers.append(evac(t, f0 + g, bank.t[:, 0:n], got))
            slot.readers.append(got)

    def copier(self, dst):
        return lambda f, ps, got: self.p.V(self.cp, dst[:, f, 0:ps.shape[1]], ps, after=[got])

    def head_rms(self, t, heads, gain, tmp, factor=1.0):
        p = self.p
        sq = self.sb(tmp, "head_squares", [P, heads, HD])
        ss = self.sb(tmp, "head_sums", [P, heads])
        p.V(self.tt, sq[:, :, :], t, t, ALU.mult)
        p.V(self.nc.vector.tensor_reduce, ss[:, :], sq[:, :, :], AX.X, ALU.add)
        r = self.rstd(ss[:, :], HD, 1e-6, tmp)
        p.V(self.tt, t, t, ss[:, :].unsqueeze(2).to_broadcast([P, heads, HD]), ALU.mult, after=[r])
        return p.V(self.tt, t, t, gain.unsqueeze(1).to_broadcast([P, heads, HD]), ALU.mult)

    def attention(self, items, scale):
        p, nc, v = self.p, self.nc, self.nc.vector
        with ExitStack() as tmp:
            probs = self.ring(tmp, "probs", [P, 512], 3)
            turned = self.ring(tmp, "probs_turned", [P, 512], 3)
            stats = self.sb(tmp, "softmax_stats", [P, len(items), 4])
            state = [dict() for _ in items]

            def score(i):
                it, st = items[i], state[i]
                bank = p.banks.next()
                after = [*bank.free(), *it["ready"]]
                pairs = [(slice(0, it["n"]), it["q"], it["keys"])] + it["extra"]
                for j, (cols, l, r) in enumerate(pairs):
                    tok = p.put("tensor", nc.tensor.matmul, bank.t[:, cols], l, r, start=j == 0,
                                stop=j == len(pairs) - 1, skip_group_check=True, after=after, chain=False,
                                signal=j == len(pairs) - 1)
                    after = ()
                p.V(v.reduce_max, stats[:, i, 0:1], bank.t[:, 0:it["n"]], AX.X, after=[tok])
                st["max"] = p.V(self.ts, stats[:, i, 1:2], stats[:, i, 0:1], -scale, None, ALU.mult)
                st["bank"] = bank
                b = probs.next()
                st["exp"] = p.S(b.t[:, 0:it["n"]], bank.t[:, 0:it["n"]], ACT.Exp, bias=stats[:, i, 1:2],
                                scale=scale, accum_out=stats[:, i, 2:3], after=[st["max"], *b.free()])
                bank.readers.append(st["exp"])
                st["probs"] = b

            def turn(i):
                it, st = items[i], state[i]
                bank, b = p.banks.next(), st["probs"]
                for k in range(it["n"] // P):
                    tok = p.turn(bank, bank.t[:, k * P:(k + 1) * P], b.t[:, k * P:(k + 1) * P],
                                 self.const("ident"), after=[st["exp"]])
                b.readers.append(tok)
                c = turned.next()
                st["turned"] = c
                st["copied"] = p.V(self.cp, c.t[:, 0:it["n"]], bank.t[:, 0:it["n"]], after=[tok, *c.free()])
                bank.readers.append(st["copied"])

            def mix(i):
                it, st = items[i], state[i]
                bank, c = p.banks.next(), st["turned"]
                tok = p.product(bank, bank.t[:, 0:HD],
                                [(c.t[:, k * P:(k + 1) * P], it["values"](k)) for k in range(it["n"] // P)],
                                after=[st["copied"]])
                c.readers.append(tok)
                p.V(v.reciprocal, stats[:, i, 3:4], stats[:, i, 2:3], after=[st["exp"]])
                done = p.V(self.ts, it["out"], bank.t[:, 0:HD], stats[:, i, 3:4], None, ALU.mult, after=[tok])
                bank.readers.append(done)

            def fill(i):
                if self.spare:
                    self.spare.pop(0)()

            pipeline(len(items), [score, turn, mix, fill])
            p.barrier()

    def first_of_max(self, onehot, vals, m, order, tmpv):
        p, v = self.p, self.nc.vector
        shape = list(vals.shape)
        wide = lambda a: a.unsqueeze(len(shape) - 1).to_broadcast(shape)
        p.V(v.tensor_reduce, m, vals, AX.X, ALU.max)
        p.V(self.tt, tmpv, vals, wide(m), ALU.is_ge)
        p.V(self.tt, tmpv, tmpv, order, ALU.mult)
        p.V(v.tensor_reduce, m, tmpv, AX.X, ALU.max)
        return p.V(self.tt, onehot, tmpv, wide(m), ALU.is_equal)

    def vector_rows(self, stack, vectors):
        rows = self.sb(stack, "vectors_on_rows", [P, len(vectors), D])
        return rows, [self.p.dma(rows[:, i, :], vec.partition_broadcast(P), aside=True) for i, vec in enumerate(vectors)]

    def modulated_rows(self, x, h, ahead):
        p, (vecs, came) = self.p, ahead
        a, b = vecs[:, 0, :], vecs[:, 1, :]
        p.wait("vector", came)
        p.V(self.ts, a, a, 1.0, None, ALU.add)
        if vecs.shape[1] == 3:
            p.V(self.tt, a, a, vecs[:, 2, :], ALU.mult)
        for t in range(TT):
            p.V(self.tt, h[:, t, :], x[:, t, :], a, ALU.mult)
            done = p.V(self.tt, h[:, t, :], h[:, t, :], b, ALU.add)
        return done

    def experts(self, rows, chosen, gate, out, n, tiles):
        p, nc, v = self.p, self.nc, self.nc.vector
        rounds = T // CAP
        with ExitStack() as tmp:
            pos = self.sb(tmp, "slot_of_token", [P, rounds, TT, n])
            flagf = self.sb(tmp, "more_rounds", [P, rounds * n])
            flags = self.flags.pop()
            bank = p.banks.next()
            ready = [p.last["vector"]]
            before, ones = self.const("before"), self.ones[:, :]
            p.product(bank, bank.t[:, 0:n], [(before, chosen[:, 0, :])], after=ready)
            p.product(bank, bank.t[:, n:2 * n], [(before, chosen[:, 1, :]), (ones, chosen[:, 0, :])])
            got = p.product(bank, bank.t[:, 2 * n:3 * n], [(ones, chosen[:, 0, :]), (ones, chosen[:, 1, :])])
            p.V(self.ts, pos[:, 0, :, :], chosen[:, :, :], -1e4, 1e4, ALU.mult, ALU.add)
            p.V(self.tt, pos[:, 0, :, :], pos[:, 0, :, :], bank.t[:, 0:2 * n].rearrange("p (t n) -> p t n", t=TT),
                ALU.add, after=[got])
            for r in range(1, rounds):
                p.V(self.ts, pos[:, r, :, :], pos[:, 0, :, :], -float(CAP * r), None, ALU.add)
                bank.readers.append(p.V(self.ts, flagf[:, r * n:(r + 1) * n], bank.t[:, 2 * n:3 * n], float(CAP * r),
                                        None, ALU.is_gt))
            p.V(v.memset, flagf[:, 0:n], 0.0)
            p.V(v.tensor_reduce, flagf[:, 0:1], flagf[:, n:2 * n], AX.X, ALU.max)
            flagged = p.V(self.cp, flags[:, :], flagf[:, :])
            all_banks = p.banks
            sums, p.banks = all_banks.buffers[0:4], Ring([])
            p.banks.buffers = all_banks.buffers[4:8]
            sel = self.ring(tmp, "chooser", [P, TT, CAP], 2)
            selg = self.ring(tmp, "gated_chooser", [P, TT, P], 3)
            xe = self.ring(tmp, "expert_in", [P, KT, CAP], 2)
            act = self.ring(tmp, "silu", [P, 256], 2)
            hid = self.ring(tmp, "hidden", [P, 256], 2)
            cols = self.ring(tmp, "hidden_cols", [P, 512], 3)
            ys = self.ring(tmp, "expert_out", [P, 512], 2)

            def round_stages(jobs, first):
                st = [dict() for _ in jobs]

                def load(i):
                    if jobs[i][1] <= 1:
                        wa, wb, wd = tiles(jobs[i][0])
                        slots, both, landed = p.weight_pair([wa, wb])
                        self.held = dict(slots=slots, both=both, landed=landed, down=p.weights(wd, D))
                    st[i]["w"] = self.held

                def gather(i):
                    e, r = jobs[i]
                    s, g = sel.next(), selg.next()
                    free = s.free() + g.free()
                    for t in range(TT):
                        at = pos[:, r, t, e:e + 1]
                        p.V(self.ts, g.t[:, t, :], self.const("slot"), at, gate[:, t, e:e + 1], ALU.is_equal, ALU.mult,
                            after=free, chain=t == 0)
                        chose = p.V(self.ts, s.t[:, t, :], self.const("slot")[:, 0:CAP], at, None, ALU.is_equal, chain=False)
                    bank, x = p.banks.next(), xe.next()
                    for k in range(KT):
                        got = p.product(bank, bank.t[:, k * CAP:(k + 1) * CAP],
                                        [(rows[:, t, k * P:(k + 1) * P], s.t[:, t, :]) for t in range(TT)], after=[chose])
                    s.readers.append(got)
                    copied = p.V(self.cp, x.t[:, :, :].rearrange("p k s -> p (k s)"), bank.t[:, :], after=[got, *x.free()])
                    bank.readers.append(copied)
                    st[i].update(x=x, copied=copied, g=g, chose=chose)

                def up(i):
                    j, bank = st[i], p.banks.next()
                    w, after = j["w"], [*bank.free(), j["copied"], *j["w"]["landed"]]
                    for k in range(KT):
                        for half in range(2):
                            out = bank.t[CAP * half:CAP * half + CAP, :].rearrange("p (w n) -> p w n", w=2)
                            got = p.put("tensor", nc.tensor.matmul, out, j["x"].t[:, k, :],
                                        w["both"][:, k, :, half * 256:half * 256 + 256], start=k == 0, stop=k == KT - 1,
                                        tile_position=(0, CAP * half), after=after, chain=False, signal=k == KT - 1 and half)
                            after = ()
                    for slot in w["slots"]:
                        slot.readers.append(got)
                    j["x"].readers.append(got)
                    a, h = act.next(), hid.next()
                    s = p.S(a.t[:, :], bank.t[:, 0:256], ACT.Silu, after=[got, *a.free()])
                    j["h_done"] = p.V(self.tt, h.t[:, :], a.t[:, :], bank.t[:, 256:512], ALU.mult, after=[s, *h.free()])
                    a.readers.append(j["h_done"])
                    bank.readers.append(j["h_done"])
                    j["h"] = h

                def turn(i):
                    j, bank, c = st[i], p.banks.next(), cols.next()
                    for b in range(2):
                        p.turn(bank, bank.t[:, b * P:(b + 1) * P], j["h"].t[:, b * P:(b + 1) * P], self.const("ident"),
                               after=[j["h_done"]], signal=False)
                    for t in range(TT):
                        got = p.turn(bank, bank.t[:, 256 + t * P:256 + (t + 1) * P], j["g"].t[:, t, :],
                                     self.const("ident"), after=[j["chose"]])
                    j["h"].readers.append(got)
                    j["g"].readers.append(got)
                    j["c_done"] = p.S(c.t[:, :], bank.t[:, :], ACT.Copy, after=[got, *c.free()])
                    bank.readers.append(j["c_done"])
                    j["c"] = c

                def down(i):
                    j, bank = st[i], p.banks.next()
                    slot, wd, landed = j["w"]["down"]
                    after = [*bank.free(), j["c_done"], landed]
                    for f in range(4):
                        half, b = f // 2, f % 2
                        for c in range(2):
                            got = p.put("tensor", nc.tensor.matmul, bank.t[CAP * c:CAP * c + CAP, :],
                                        j["c"].t[:, b * P + half * CAP:b * P + half * CAP + CAP],
                                        wd[:, f, c * 512:c * 512 + 512], start=f == 0, stop=f == 3,
                                        tile_position=(0, CAP * c), after=after, chain=False, signal=f == 3 and c)
                            after = ()
                    slot.readers.append(got)
                    y = ys.next()
                    j["y_done"] = p.S(y.t[:, :], bank.t[:, :], ACT.Copy, after=[got, *y.free()])
                    bank.readers.append(j["y_done"])
                    j["y"] = y

                def scatter(i):
                    j, start = st[i], first and i == 0
                    for t in range(TT):
                        for c in range(2):
                            side = slice(CAP * c, CAP * c + CAP)
                            b = sums[2 * t + c]
                            got = p.put("tensor", nc.tensor.matmul, b.t[:, :], j["c"].t[side, 256 + t * P:256 + (t + 1) * P],
                                        j["y"].t[side, :], start=start, stop=True, skip_group_check=True,
                                        tile_position=(CAP * c, 0), after=[*b.free(), j["y_done"]], chain=False,
                                        signal=t and c)
                    j["c"].readers.append(got)
                    j["y"].readers.append(got)
                    self.summed = got

                return load, gather, up, turn, down, scatter

            p.align(3)
            load, gather, up, turn, down, scatter = round_stages([(e, 0) for e in range(n)], True)
            for i in range(n + 3):
                for stage, lag in ((gather, 0), (turn, 2), (up, 1), (down, 2), (scatter, 3), (load, 0)):
                    if 0 <= i - lag < n:
                        stage(i - lag)

            def more(e, r):
                def body():
                    load, *stages = round_stages([(e, r)], False)
                    load(0)
                    for stage in stages:
                        stage(0)
                    if r + 1 < rounds:
                        p.branch(flags[0:1, (r + 1) * n + e:(r + 1) * n + e + 1], more(e, r + 1))
                return body

            def any_more():
                for e in range(n):
                    p.branch(flags[0:1, n + e:n + e + 1], more(e, 1))
            for engine in ("tensor", "vector", "scalar", "sync"):
                p.wait(engine, [flagged])
            p.branch(flags[0:1, 0:1], any_more)
            for t in range(TT):
                for c in range(2):
                    b = sums[2 * t + c]
                    b.readers.append(p.V(self.cp, out[:, t, c * 512:(c + 1) * 512], b.t[:, :], after=[self.summed]))
            p.banks = all_banks
            p.barrier()

    def first_block(self):
        p, nc, A, v = self.p, self.nc, self.A, self.nc.vector
        with ExitStack() as blk:
            r8 = lambda a: a.rearrange("(k p) -> k p", p=P)
            par = self.sb(blk, "params1", [P, 48])
            N1, CB, CG, C1, C2, C3 = 0, 16, 20, 24, 32, 40
            convw = self.sb(blk, "conv_w", [P, 31, 4])
            for rows, out, n in ((self.rows1, par[:, :], 48), (self.rows2, convw[:, :, :].rearrange("p a b -> p (a b)"), 124)):
                b = p.banks.next()
                got = p.turn(b, b.t[:, 0:n], rows[0:n, :], self.const("ident")[0:n, 0:n])
                b.readers.append(p.V(self.cp, out, b.t[:, 0:n], after=[got]))
            p.wait("scalar", [p.last["vector"]])
            results = self.ring(blk, "mod_result", [P, P], 3)
            first, rest = range(2 * D // 512), range(2 * D // 512, 6 * D // 512)
            tiles = self.modulation_tiles(blk, [par[:, C1:C1 + 8], par[:, C2:C2 + 8]],
                                          [(A["w_mod"][0], 0, first), (A["w_mod"][0], 0, rest)], results)
            for tile in tiles[:len(first)]:
                tile()
            p.barrier(aside=True)
            self.late_tiles = tiles[len(first):]
            every = range(6 * D // 512)
            self.spare = self.modulation_tiles(
                blk, [par[:, C3:C3 + 8]],
                [(A["ada_w_2"][0], 2, every), (A["ada_w_2"][1], 3, every), (A["kv_ada_w_2"], 4, first)], results)
            modT = self.sb(blk, "mod_cols", [P, 32])
            vectors, biases = [r8(self.mod[i, 0:2 * D]) for i in range(2)], [r8(A["b_mod"][0, 0:2 * D])] * 2
            loaded = self.column_rows(self.rows1, vectors) + self.column_rows(self.rows2, biases)
            self.some_late_tiles(3)
            self.turned_columns(modT[:, :], self.rows1, vectors, self.rows2, biases, loaded)
            AB = self.sb(blk, "norm_scales", [P, 2, 8])
            for i, at in enumerate((8, 24)):
                p.V(self.stt, out=AB[:, i, :], in0=modT[:, at:at + 8], scalar=1.0, in1=par[:, N1:N1 + 8],
                    op0=ALU.add, op1=ALU.mult)
            y_sum = self.sb(blk, "branch_sum_cols", [P, KT, T])
            router = self.router(blk, [A["w_router"]], [A["router_bias"]], 16)
            rows_of = lambda a: a.rearrange("l (k p) -> (l k) p", p=P)
            self.rows3 = self.sb(blk, "vector_rows_c", [P, P])
            self.late_mods, self.late_biases = (self.sb(blk, n, [32, P]) for n in ("late_mod_rows", "late_bias_rows"))
            self.second_vectors = (
                [rows_of(self.mod[2:4, :]), r8(self.mod[4, 0:2 * D])],
                [rows_of(A["ada_b_2"]), r8(A["kv_ada_b_2"])],
                [rows_of(A["rw_mu_2"][0]), *(r8(A[n][0]) for n in ("rw_w0_2", "rw_a0_2", "rw_kk_2", "rw_ka_2")),
                 r8(A["rw_rk_2"][0].rearrange("h n -> (h n)"))])
            with ExitStack() as mix:
                self.mixer(mix, par, convw, modT, AB, y_sum, CB, CG)
                p.barrier()
            late = blk.enter_context(ExitStack())
            norm2 = self.vector_rows(late, [self.mod[0, 4 * D:5 * D], self.mod[0, 3 * D:4 * D], A["norm2_g"][0]])
            last2 = self.vector_rows(late, [self.mod[0, 5 * D:6 * D], A["final_norm_g"]])
            with ExitStack() as tmp:
                g1 = self.sb(tmp, "gate1", [P, D])
                came = p.dma(g1[:, :], self.mod[0, 2 * D:3 * D].partition_broadcast(P))
                t1 = self.ring(tmp, "mixed", [P, 512], 2)

                def evac(t, f0, ps, got):
                    b = t1.next()
                    tok = p.V(self.tt, b.t[:, :], ps, g1[:, f0:f0 + 512], ALU.mult, after=[got, came])
                    xs = self.x[:, t, f0:f0 + 512]
                    p.V(self.tt, xs, xs, b.t[:, :], ALU.add)
                    return tok
                self.to_rows(y_sum, D, A["w_out"][0], evac)
                p.barrier()
            with ExitStack() as tmp:
                rows = self.sb(tmp, "h2_rows", [P, TT, D])
                acc = self.sb(tmp, "moe_sum", [P, TT, D])
                gate = self.sb(tmp, "gates", [P, TT, 16])
                chosen = self.sb(tmp, "chosen", [P, TT, 16])
                ss = self.sb(tmp, "square_sums", [P, TT])
                for t in range(TT):
                    a = p.S(rows[:, t, :], self.x[:, t, :], ACT.Square, accum_out=ss[:, t:t + 1])
                p.wait("vector", [a])
                r = self.rstd(ss[:, :], D, 1e-6, tmp)
                for t in range(TT):
                    p.V(self.ts, rows[:, t, :], self.x[:, t, :], ss[:, t:t + 1], None, ALU.mult, after=[r])
                made = self.modulated_rows(rows, rows, norm2)
                with ExitStack() as t2:
                    h2 = self.sb(t2, "h2_cols", [P, KT, T])
                    self.turned(rows, h2, after=[made])
                    self.route1(h2, gate, chosen, router)
                    p.barrier()
                wgu, wd = A["w_expert_gu"][0], A["w_expert_down"][0]
                self.experts(rows, chosen, gate, acc, 16, lambda e: (wgu[e][:, 0:512], wgu[e][:, 512:1024], wd[e]))
                (vecs, (came, came2)) = last2
                g2, gf = vecs[:, 0, :], vecs[:, 1, :]
                for t in range(TT):
                    p.V(self.tt, acc[:, t, :], acc[:, t, :], g2, ALU.mult, after=[came])
                    a = p.V(self.tt, self.x[:, t, :], self.x[:, t, :], acc[:, t, :], ALU.add)
                for t in range(TT):
                    s = p.S(acc[:, t, :], self.x[:, t, :], ACT.Square, accum_out=ss[:, t:t + 1], after=[a])
                p.wait("vector", [s])
                r = self.rstd(ss[:, :], D, 1e-6, tmp)
                for t in range(TT):
                    p.V(self.stt, out=self.x[:, t, :], in0=self.x[:, t, :], scalar=ss[:, t:t + 1], in1=gf,
                        op0=ALU.mult, op1=ALU.mult, after=[r, came2])
                p.barrier(aside=True)

    def mixer(self, mix, par, convw, modT, AB, y_sum, CB, CG):
        p, nc, A, v = self.p, self.nc, self.A, self.nc.vector
        w_in = A["w_in"][0]
        hT = self.sb(mix, "h_cols", [P, KT, 2 * T])
        with ExitStack() as tmp:
            ctx = self.sb(tmp, "ctx_rows", [P, TT, D])
            came = p.dma(ctx[:, :, :], A["ctx"][0].rearrange("(t p) d -> p t d", p=P), engine="scalar")
            p.wait("scalar", [came])
            p.wait("vector", [came])
            self.rms_turned(self.x, hT, 0, AB[:, 0, :], modT[:, 0:8])
            self.some_late_tiles(3)
            self.rms_turned(ctx, hT, T, AB[:, 1, :], modT[:, 16:24])
            self.some_late_tiles(8)
        branches = [self.sb(mix, f"branch{i}_cols", [P, 4, T]) for i in range(4)]
        early = ExitStack()
        came = []
        bias = self.sb(early, "window_bias", [P, TT, 8, 4, GRID_W])
        with ExitStack() as tmp:
            q = y_sum[:, 4:8, :].rearrange("p (t k) (h d) -> p t (k h) d", t=TT, d=HD)
            k = self.sb(tmp, "k_rows", [P, 4, 2, HD])
            val = self.sb(tmp, "v_rows", [P, 4, 2, HD])
            gains = self.sb(tmp, "head_gains", [P, 2, HD])
            p.dma(gains[:, 0, :], A["q_norm_g"][0].partition_broadcast(P))
            p.dma(gains[:, 1, :], A["k_norm_g"][0].partition_broadcast(P))
            rpb = A["na_rpb"][0]
            for t in range(TT):
                for half in range(2):
                    r = 2 * t + half
                    for h in range(8):
                        src = bass.AP(tensor=rpb.tensor, offset=rpb.offset + h * 15 * 31 + (7 - r) * 31 + 15 - (GRID_W - 1),
                                      ap=[[1, GRID_W], [31, 4], [1, GRID_W]])
                        came.append(p.dma(bias[HD * half:HD * half + HD, t, h, :, :], src, aside=True))
            flat = lambda a: a.rearrange("p h d -> p (h d)")
            self.to_rows(hT, 512, w_in[:, 0:512],
                         lambda t, f0, ps, got: p.V(self.cp, flat(q[:, t, :, :]), ps, after=[got]))

            def split(t, f0, ps, got):
                p.V(self.cp, flat(k[:, t, :, :]), ps[:, 0:128], after=[got])
                return p.V(self.cp, flat(val[:, t, :, :]), ps[:, 128:256])
            self.to_rows(hT, 256, w_in[:, 512:768], split, tiles=4)
            p.barrier()
            rot = self.sb(tmp, "rotated", [P, 2, 8, 32])
            for t in range(TT):
                self.head_rms(q[:, t, :, :], 8, gains[:, 0, :], tmp)
                self.rope(q[:, t, :, :], 8, t, rot)
            for t in range(4):
                self.head_rms(k[:, t, :, :], 2, gains[:, 1, :], tmp)
                if t < TT:
                    self.rope(k[:, t, :, :], 2, t, rot)
            k2 = y_sum[:, 0:4, :].rearrange("p t (h i d) -> p t h i d", h=2, d=HD)
            for i in range(2):
                done = p.V(self.cp, k2[:, :, :, i, :], k[:, :, :, :])
            qT = self.sb(tmp, "q_cols", [P, 4, T])
            kT = self.sb(tmp, "k_cols", [P, 2, 2 * T])
            self.turned(q[:, :, :, :].rearrange("p t h d -> p t (h d)"), qT, kt=4, after=[done])
            k2f = y_sum[:, 0:4, :]
            self.turned(k2f[:, 0:2, :], kT, 0, kt=2)
            ready = self.turned(k2f[:, 2:4, :], kT, T, kt=2)
            y = y_sum[:, 0:4, :].rearrange("p (t k) n -> p t (k n)", t=TT)
            items = []
            for h in range(8):
                half = slice(HD * (h % 2), HD * (h % 2) + HD)
                for t in range(TT):
                    items.append(dict(q=qT[half, h // 2, t * P:(t + 1) * P], keys=kT[half, h // 4, :], n=512,
                                      extra=[], values=lambda k, h=h: val[:, k, h // 4, :],
                                      out=y[:, t, h * HD:(h + 1) * HD], ready=[ready]))
            self.attention(items, HD ** -0.5)
            self.turned(y, branches[0], kt=4)
            p.barrier()
        with ExitStack() as tmp:
            qT = self.sb(tmp, "nq_cols", [P, 4, T])
            kT = self.sb(tmp, "nk_cols", [P, 4, 2 * T])
            val = self.sb(tmp, "nv_rows", [P, 4, 8, HD])
            self.to_cols(hT, 512, w_in[:, 768:1280], self.copier(qT))
            self.to_cols(hT, 512, w_in[:, 1280:1792], self.copier(kT), n=2 * T)
            self.to_rows(hT, 512, w_in[:, 1792:2304],
                         lambda t, f0, ps, got: p.V(self.cp, val[:, t, :, :].rearrange("p h d -> p (h d)"),
                                                    ps, after=[got]), tiles=4)
            p.wait("vector", came)
            for t in range(TT):
                for h in range(8):
                    b = bias[:, t, h, :, :]
                    done = p.V(self.stt, out=b, in0=b, scalar=HD ** 0.5, op0=ALU.mult, op1=ALU.add,
                               in1=self.const("window").unsqueeze(1).to_broadcast([P, 4, GRID_W]))
            y = y_sum[:, 0:4, :].rearrange("p (t k) n -> p t (k n)", t=TT)
            items = []
            for h in range(8):
                half = slice(HD * (h % 2), HD * (h % 2) + HD)
                for t in range(TT):
                    items.append(dict(q=qT[half, h // 2, t * P:(t + 1) * P], keys=kT[half, h // 2, :], n=512,
                                      extra=[(slice(0, T), self.const("reverse"),
                                              bias[:, t, h, :, :].rearrange("p a b -> p (a b)"))],
                                      values=lambda k, h=h: val[:, k, h, :],
                                      out=y[:, t, h * HD:(h + 1) * HD], ready=[done]))
            self.attention(items, HD ** -0.5)
            self.turned(y, branches[1], kt=4)
            p.barrier()
        early.close()
        while self.spare:
            self.spare.pop(0)()
        with ExitStack() as tmp:
            u = self.sb(tmp, "fourier_cols", [P, 4, T])
            spec = self.sb(tmp, "spectrum_rows", [P, TT, 4, 2, P])
            tables = self.sb(tmp, "fourier_tables", [P, CONST_WIDTH - KEPT_WIDTH])
            p.dma(tables[:, :], self.all_consts[:, KEPT_WIDTH:CONST_WIDTH])
            table = lambda n: tables[:, CONST[n][0] - KEPT_WIDTH:CONST[n][0] - KEPT_WIDTH + CONST[n][1]]
            stored = p.transfers(aside=True)
            late = self.mod[0, 2 * D:6 * D].rearrange("(k p) -> k p", p=P)
            self.second_loads = (self.column_rows(self.rows1, self.second_vectors[0], stored)
                                 + self.column_rows(self.rows2, self.second_vectors[1]),
                                 self.column_rows(self.rows3, self.second_vectors[2]),
                             self.column_rows(self.late_mods, [late], stored)
                             + self.column_rows(self.late_biases, [A["b_mod"][0, 2 * D:6 * D].rearrange("(k p) -> k p", p=P)]))
            self.to_cols(hT, 512, w_in[:, 2304:2816], self.copier(u))
            p.barrier()
            for t in range(TT):
                for g in range(4):
                    bank = p.banks.next()
                    got = p.product(bank, bank.t[:, 0:256], [(u[:, g, t * P:(t + 1) * P], table("cs_group"))])
                    done = p.V(self.cp, spec[:, t, g, :, :].rearrange("p a b -> p (a b)"), bank.t[:, 0:256], after=[got])
                    bank.readers.append(done)
            for g in range(4):
                bank = p.banks.next()
                pairs = [(spec[:, t, g, i, :], table(("cos_seq", "sin_seq")[i])[:, t * T:(t + 1) * T])
                         for t in range(TT) for i in range(2)]
                got = p.product(bank, bank.t[:, 0:T], pairs, after=[done])
                bank.readers.append(p.V(self.cp, branches[2][:, g, :], bank.t[:, 0:T], after=[got]))
            p.barrier()
        with ExitStack() as tmp:
            pad = 15
            a = self.sb(tmp, "glu_cols", [P, 4, T])
            z = self.sb(tmp, "padded_cols", [P, 4, T + 2 * pad])
            c = branches[3]
            p.V(v.memset, z[:, :, :], 0.0)
            self.to_cols(hT, 512, w_in[:, 2816:3328], self.copier(a))
            sg = self.ring(tmp, "sigmoid", [P, T], 2)

            def glu(f, ps, got):
                b = sg.next()
                s = p.S(b.t[:, :], ps, ACT.Sigmoid, after=[got, *b.free()])
                b.readers.append(p.V(self.tt, z[:, f, pad:pad + T], a[:, f, :], b.t[:, :], ALU.mult, after=[s]))
                return s
            self.to_cols(hT, 512, w_in[:, 3328:3840], glu)
            def tap(i, f):
                src, w = z[:, f, i:i + T], convw[:, i, f:f + 1]
                if i == 0:
                    p.V(self.ts, c[:, f, :], src, w, par[:, CB + f:CB + f + 1], ALU.mult, ALU.add)
                else:
                    p.V(self.stt, out=c[:, f, :], in0=src, scalar=w, in1=c[:, f, :], op0=ALU.mult, op1=ALU.add)
            taps = [(i, f) for i in range(31) for f in range(4)]
            gates = self.sb(tmp, "branch_gates", [P, KT, T])
            t1 = self.ring(tmp, "gated", [P, T], 2)
            gate_read = [None] * KT

            def finish_conv():
                sq = self.sb(tmp, "conv_squares", [P, 4, T])
                done = p.V(self.tt, sq[:, :, :], c[:, :, :], c[:, :, :], ALU.mult)
                bank = p.banks.next()
                got = p.product(bank, bank.t[:, 0:T], [(self.ones[:, :], sq[:, f, :]) for f in range(4)], after=[done])
                rs = self.sb(tmp, "conv_rstd", [P, T])
                bank.readers.append(p.V(self.cp, rs[:, :], bank.t[:, 0:T], after=[got]))
                r = self.rstd(rs[:, :], 512, 1e-6, tmp)
                n = p.V(self.tt, c[:, :, :], c[:, :, :], rs[:, :].unsqueeze(1).to_broadcast([P, 4, T]), ALU.mult, after=[r])
                for f in range(4):
                    last = p.S(c[:, f, :], c[:, f, :], ACT.Silu, scale=par[:, CG + f:CG + f + 1], after=[n])
                return last

            mods, biases, vectors = self.second_vectors
            self.turned_columns(self.mod2[:, :], self.rows1, mods, self.rows2, biases, self.second_loads[0])
            self.turned_columns(self.rw_par, self.rows3, vectors, None, (), self.second_loads[1])
            added = p.V(self.tt, self.late_mods[:, :], self.late_mods[:, :], self.late_biases[:, :], ALU.add,
                        after=self.second_loads[2])
            p.dma(self.mod[0, 2 * D:6 * D].rearrange("(k p) -> k p", p=P), self.late_mods[:, :], after=[added])
            for n in range(4):
                g0 = 3840 + n * D
                gate_done = [None] * KT

                def gate_evac(f, ps, got):
                    gate_done[f] = p.S(gates[:, f, :], ps, ACT.Sigmoid, after=[got, gate_read[f]])
                    return gate_done[f]
                self.to_cols(hT, D, w_in[:, g0:g0 + D], gate_evac)
                ready = []
                if n == 3:
                    ready = [finish_conv()]

                def evac(f, ps, got, n=n):
                    out = y_sum[:, f, :] if n == 0 else t1.next().t[:, :]
                    tok = p.V(self.tt, out, ps, gates[:, f, :], ALU.mult, after=[got, gate_done[f]])
                    gate_read[f] = tok
                    if n:
                        p.V(self.tt, y_sum[:, f, :], y_sum[:, f, :], out, ALU.add)
                    for _ in range(6):
                        if taps:
                            tap(*taps.pop(0))
                    return tok
                self.to_cols(branches[n], D, A["w_branch"][0, n], evac, ktiles=4, ready=ready)
            p.barrier()

    def rope(self, t, heads, tile, rot):
        p = self.p
        pairs = t.rearrange("p h (j i) -> p h j i", i=2)
        x1, x2 = pairs[:, :, :, 0], pairs[:, :, :, 1]
        cut = lambda n: self.const(n)[:, tile * 32:tile * 32 + 32].unsqueeze(1).to_broadcast([P, heads, 32])
        cos, sin = cut("cos"), cut("sin")
        with ExitStack() as tmp:
            a, b = rot[:, 0, 0:heads, :], rot[:, 1, 0:heads, :]
            rot2 = self.sb(tmp, "rope_scratch", [P, 2, 8, 32])
            c, d = rot2[:, 0, 0:heads, :], rot2[:, 1, 0:heads, :]
            p.V(self.tt, a, x1, cos, ALU.mult)
            p.V(self.tt, b, x2, sin, ALU.mult)
            p.V(self.tt, c, x1, sin, ALU.mult)
            p.V(self.tt, d, x2, cos, ALU.mult)
            p.V(self.tt, x1, a, b, ALU.subtract)
            p.V(self.tt, x2, c, d, ALU.add)

    def router(self, stack, w_aps, bias_aps, n):
        p = self.p
        w = self.sb(stack, "router_w", [P, KT, n])
        bias = self.sb(stack, "router_bias", [P, n])
        at, came = 0, []
        for wa, ba in zip(w_aps, bias_aps):
            m = wa.shape[1]
            came.append(p.dma(w[:, :, at:at + m], wa.rearrange("(k p) n -> p k n", p=P), aside=True))
            came.append(p.dma(bias[:, at:at + m], ba.partition_broadcast(P), aside=True))
            at += m
        return w, bias, came

    def scores_rows(self, hT, router, out):
        p = self.p
        w, bias, came = router
        n = w.shape[2]
        came = [*came, p.last["vector"]]
        for t in range(TT):
            bank = p.banks.next()
            got = p.product(bank, bank.t[:, 0:n], [(hT[:, k, t * P:(t + 1) * P], w[:, k, :]) for k in range(KT)],
                            after=came)
            bank.readers.append(p.V(self.cp, out[:, t, :], bank.t[:, 0:n], after=[got, *came]))
        return bias[:, :].unsqueeze(1).to_broadcast([P, TT, n])

    def route1(self, hT, gate, chosen, router):
        p, v, A = self.p, self.nc.vector, self.A
        with ExitStack() as tmp:
            sb = lambda name, *s: self.sb(tmp, name, [P, TT, *s])
            sc, sel = sb("scores", 16), sb("selection", 16)
            bias = self.scores_rows(hT, router, sc)
            s = p.S(sc[:, :, :], sc[:, :, :], ACT.Sigmoid, after=[p.last["vector"]])
            p.V(self.tt, sel[:, :, :], sc[:, :, :], bias, ALU.add, after=[s])
            g4 = sel[:, :, :].rearrange("p t (g e) -> p t g e", e=4)
            gs, pair = sb("group_score", 4), sb("pair_sum", 4)
            for n, (i, j) in enumerate(((0, 1), (0, 2), (0, 3), (1, 2), (1, 3), (2, 3))):
                p.V(self.tt, (pair if n else gs)[:, :, :], g4[:, :, :, i], g4[:, :, :, j], ALU.add)
                if n:
                    p.V(self.tt, gs[:, :, :], gs[:, :, :], pair[:, :, :], ALU.max)
            m, t4, grp = sb("largest"), sb("tie4", 4), sb("group", 4)
            self.first_of_max(grp[:, :, :], gs[:, :, :], m[:, :],
                              self.const("first4").unsqueeze(1).to_broadcast([P, TT, 4]), t4[:, :, :])
            self.top2(sel, grp, 4, 4, chosen, tmp)
            p.V(self.tt, gate[:, :, :], chosen[:, :, :], sc[:, :, :], ALU.mult)
            p.V(v.tensor_reduce, m[:, :], gate[:, :, :], AX.X, ALU.add)
            p.V(v.reciprocal, m[:, :], m[:, :])
            p.V(self.tt, gate[:, :, :], gate[:, :, :], m[:, :].unsqueeze(2).to_broadcast([P, TT, 16]), ALU.mult)
            p.barrier()

    def top2(self, vals, grp, groups, size, chosen, tmp):
        p = self.p
        n = groups * size
        sb = lambda name, *s: self.sb(tmp, name, [P, TT, *s])
        m, tie, one, pen = sb("largest"), sb("tie", n), sb("first", n), sb("outside", groups)
        order = self.const("first32")[:, 0:n].unsqueeze(1).to_broadcast([P, TT, n])
        v4 = vals[:, :, :].rearrange("p t (g e) -> p t g e", e=size)
        wide = lambda a: a[:, :, :].unsqueeze(3).to_broadcast([P, TT, groups, size])
        p.V(self.ts, pen[:, :, :], grp[:, :, :], -1.0, BIG, ALU.add, ALU.mult)
        p.V(self.tt, v4, v4, wide(grp), ALU.mult)
        p.V(self.tt, v4, v4, wide(pen), ALU.add)
        second = sb("without_first", n)
        self.first_of_max(one[:, :, :], vals[:, :, :], m[:, :], order, tie[:, :, :])
        p.V(self.stt, out=second[:, :, :], in0=one[:, :, :], scalar=-3 * BIG, in1=vals[:, :, :],
            op0=ALU.mult, op1=ALU.add)
        self.first_of_max(chosen[:, :, :], second[:, :, :], m[:, :], order, tie[:, :, :])
        p.V(self.tt, chosen[:, :, :], chosen[:, :, :], one[:, :, :], ALU.add)

    def second_block(self):
        p, nc, A = self.p, self.nc, self.A
        r8 = lambda a: a.rearrange("(k p) -> k p", p=P)
        with ExitStack() as blk:
            mod2 = self.mod2
            modT = mod2[:, 0:96].rearrange("p (l k) -> p l k", l=2)
            modK = mod2[:, 96:112]
            one_plus = self.sb(blk, "one_plus_scale", [P, 5, 8])
            for i, src in enumerate((modT[:, 0, 8:16], modT[:, 0, 32:40], modT[:, 1, 8:16], modT[:, 1, 32:40],
                                     modK[:, 8:16])):
                p.V(self.ts, one_plus[:, i, :], src, 1.0, None, ALU.add)
            p.barrier()
            y = self.sb(blk, "layer_out_rows", [P, TT, D])
            routers = [self.router(blk, [A["moe_wgrp_2"][l], A["moe_wexp_2"][l]],
                                   [A["moe_bgrp_2"][l], A["moe_bexp_2"][l]], 36) for l in range(2)]
            for l in range(2):
                if l == 0:
                    self.rwkv(y, one_plus[:, 0, :], modT[:, 0, 0:8])
                else:
                    self.fox(y, one_plus[:, 2, :], modT[:, 1, 0:8])
                with ExitStack() as tmp:
                    ahead = self.residual_rows(tmp, l, 0)
                    moe_in = self.vector_rows(tmp, [self.mod[2 + l, 4 * D:5 * D], self.mod[2 + l, 3 * D:4 * D]])
                    self.residual(y, ahead)
                    ahead = self.residual_rows(tmp, l, 1)
                    rows = self.sb(tmp, "moe_rows", [P, TT, D])
                    gate = self.sb(tmp, "moe_gates", [P, TT, 32])
                    chosen = self.sb(tmp, "moe_chosen", [P, TT, 32])
                    made = self.modulated_rows(self.x, rows, moe_in)
                    with ExitStack() as t2:
                        hT = self.sb(t2, "moe_cols", [P, KT, T])
                        self.turned(rows, hT, after=[made])
                        self.route2(hT, gate, chosen, routers[l])
                        p.barrier()
                    wg, wu, wd = (A[n][l] for n in ("moe_wgate_2", "moe_wup_2", "moe_wdown_2"))
                    self.experts(rows, chosen, gate, y, 32, lambda e: (wg[e], wu[e], wd[e]))
                    self.residual(y, ahead)
                if l == 0:
                    self.kT = self.sb(blk, "fox_k_cols", [P, 8, T])
                    self.val = self.sb(blk, "fox_v_rows", [P, TT, N_HEADS, HD])
                    self.shared_kv(one_plus[:, 4, :], modK[:, 0:8])
            done = p.dma(self.out.rearrange("b (t p) d -> p (b t) d", p=P), self.x[:, :, :])
            p.wait("gpsimd", [done])

    def residual_rows(self, stack, l, which):
        at = (2 if which == 0 else 5) * D
        return self.vector_rows(stack, [self.mod[2 + l, at:at + D], self.A["ln_g_2"][l, which], self.A["ln_b_2"][l, which]])

    def residual(self, y, ahead):
        p, v = self.p, self.nc.vector
        rows, c = ahead
        with ExitStack() as tmp:
            gt, g, b = rows[:, 0, :], rows[:, 1, :], rows[:, 2, :]
            s1 = self.sb(tmp, "ln_sums", [P, TT, 2])
            p.wait("vector", c)
            for t in range(TT):
                xt, yt = self.x[:, t, :], y[:, t, :]
                p.V(self.stt, out=yt, in0=gt, scalar=1.0, in1=yt, op0=ALU.add, op1=ALU.mult)
                p.V(self.stt, out=xt, in0=xt, scalar=ALPHA, in1=yt, op0=ALU.mult, op1=ALU.add)
                p.V(v.tensor_reduce, s1[:, t, 0:1], xt, AX.X, ALU.add)
                p.V(self.ts, s1[:, t, 0:1], s1[:, t, 0:1], -1.0 / D, None, ALU.mult)
                p.V(self.ts, xt, xt, s1[:, t, 0:1], None, ALU.add)
                a = p.last["vector"]
                s = p.S(yt, xt, ACT.Square, accum_out=s1[:, t, 1:2], after=[a])
            p.wait("vector", [s])
            r = self.rstd(s1[:, :, 1], D, 1e-5, tmp)
            for t in range(TT):
                xt = self.x[:, t, :]
                p.V(self.stt, out=xt, in0=xt, scalar=s1[:, t, 1:2], in1=g, op0=ALU.mult, op1=ALU.mult, after=[r])
                p.V(self.tt, xt, xt, b, ALU.add)
            p.barrier()

    def route2(self, hT, gate, chosen, router):
        p, v, A = self.p, self.nc.vector, self.A
        with ExitStack() as tmp:
            sb = lambda name, *s: self.sb(tmp, name, [P, TT, *s])
            lg = sb("logits", 36)
            bias = self.scores_rows(hT, router, lg)
            p.V(self.tt, lg[:, :, :], lg[:, :, :], bias, ALU.add)
            m, s, t4, grp, pg = sb("largest"), sb("sum"), sb("tie4", 4), sb("group", 4), sb("p_group")
            gl, el = lg[:, :, 0:4], sb("expert_logits", 32)

            def softmax(a, n):
                wide = lambda q: q[:, :].unsqueeze(2).to_broadcast([P, TT, n])
                p.V(v.tensor_reduce, m[:, :], a, AX.X, ALU.max)
                d = p.V(self.tt, a, a, wide(m), ALU.subtract)
                e = p.S(a, a, ACT.Exp, after=[d])
                p.V(v.tensor_reduce, s[:, :], a, AX.X, ALU.add, after=[e])
                p.V(v.reciprocal, s[:, :], s[:, :])
                p.V(self.tt, a, a, wide(s), ALU.mult)
            p.V(self.cp, el[:, :, :], lg[:, :, 4:36])
            softmax(gl, 4)
            self.first_of_max(grp[:, :, :], gl, m[:, :],
                              self.const("first4").unsqueeze(1).to_broadcast([P, TT, 4]), t4[:, :, :])
            p.V(v.tensor_reduce, pg[:, :], gl, AX.X, ALU.max)
            self.top2(el, grp, 4, 8, chosen, tmp)
            softmax(el[:, :, :], 32)
            p.V(self.tt, gate[:, :, :], chosen[:, :, :], el[:, :, :], ALU.mult)
            p.V(v.tensor_reduce, s[:, :], gate[:, :, :], AX.X, ALU.add)
            p.V(self.tt, gate[:, :, :], gate[:, :, :], pg[:, :].unsqueeze(2).to_broadcast([P, TT, 32]), ALU.mult)
            p.V(v.reciprocal, s[:, :], s[:, :])
            p.V(self.tt, gate[:, :, :], gate[:, :, :], s[:, :].unsqueeze(2).to_broadcast([P, TT, 32]), ALU.mult)
            p.barrier()

    def rwkv(self, y_out, scale, shift):
        p, nc, A, v = self.p, self.nc, self.A, self.nc.vector
        r8 = lambda a: a.rearrange("(k p) -> k p", p=P)
        with ExitStack() as top:
            gate = y_out
            par = self.rw_par
            MU, W0, A0, KK, KA, RK = 0, 48, 56, 64, 72, 80
            ar = self.sb(top, "a_r_cols", [P, KT, NCH, 2, CH])
            bh = self.sb(top, "b_cols", [P, KT, T])
            kh = self.sb(top, "k_cols", [P, KT, T])
            prod = self.sb(top, "bonus_cols", [P, KT, T])
            wend = self.sb(top, "chunk_decay", [P, KT, NCH])
            vrow = self.sb(top, "v_chunk_rows", [P, NCH, 4, HD])
            with ExitStack() as tmp:
                hp = self.sb(tmp, "h_padded", [P, KT, T + 1])
                xx = self.sb(tmp, "shift_diff", [P, KT, T])
                kk = self.sb(tmp, "kk_cols", [P, KT, T])
                r_, k_, a_, w_ = prod, kh, bh, self.sb(tmp, "w_cols", [P, KT, T])
                mids = self.ring(tmp, "lora_mid", [P, 2, T], 2)
                mixes = Ring([ar[:, 4 * i:4 * i + 4, :, :, :].rearrange("p k c a u -> p (k c a u)")
                              .rearrange("p (k t) -> p k t", t=T) for i in range(2)])
                p.V(v.memset, hp[:, :, 0:1], 0.0)
                self.turned(self.x, hp, 1, scale, shift)
                p.V(self.tt, xx[:, :, :], hp[:, :, 0:T], hp[:, :, 1:T + 1], ALU.subtract)

                def mixed(i):
                    b = mixes.next()
                    after = b.free()
                    for k in range(KT):
                        tok = p.V(self.stt, out=b.t[:, k, :], in0=xx[:, k, :], scalar=par[:, MU + 8 * i + k:MU + 8 * i + k + 1],
                                  in1=hp[:, k, 1:T + 1], op0=ALU.mult, op1=ALU.add, after=after)
                    return b, tok

                def lora_in(mix, w1, w2, r, func):
                    src, ready = mix
                    sizes = [min(P, r - at) for at in range(0, r, P)]

                    def parts(slot):
                        yield slot[:, 0:KT * r].rearrange("p (k n) -> p k n", n=r), w1.rearrange("(k p) r -> p k r", p=P)
                        for j, m in enumerate(sizes):
                            yield slot[0:m, KT * r + j * D:KT * r + (j + 1) * D], w2[j * P:j * P + m, :]
                    slot, landed = p.weight_parts(parts)
                    mid = mids.next()
                    after = [landed, ready]
                    for j, m in enumerate(sizes):
                        bank = p.banks.next()
                        got = p.product(bank, bank.t[0:m, 0:T], [(slot.t[:, k * r + j * P:k * r + j * P + m], src.t[:, k, :])
                                                                 for k in range(KT)], after=after)
                        done = p.S(mid.t[0:m, j, :], bank.t[0:m, 0:T], func, after=[got, *mid.free()])
                        bank.readers.append(done)
                    src.readers.append(got)
                    w2s = [slot.t[0:m, KT * r + j * D:KT * r + (j + 1) * D] for j, m in enumerate(sizes)]
                    return slot, mid, w2s, done, sizes

                def lora_cols(mix, w1, w2, r, func, evac):
                    slot, mid, w2s, done, sizes = lora_in(mix, w1, w2, r, func)
                    for f in range(KT):
                        bank = p.banks.next()
                        got = p.product(bank, bank.t[:, 0:T], [(w2s[j][:, f * P:(f + 1) * P], mid.t[0:m, j, :])
                                                               for j, m in enumerate(sizes)], after=[done])
                        bank.readers.append(evac(f, bank.t[:, 0:T], got))
                    slot.readers.append(got)
                    mid.readers.append(got)
                    return bank.readers[-1]

                def lora_rows(mix, w1, w2, r, func, evac):
                    slot, mid, w2s, done, sizes = lora_in(mix, w1, w2, r, func)
                    for t in range(TT):
                        for g in range(0, D, 512):
                            bank = p.banks.next()
                            got = p.product(bank, bank.t[:, :], [(mid.t[0:m, j, t * P:(t + 1) * P], w2s[j][:, g:g + 512])
                                                                 for j, m in enumerate(sizes)], after=[done])
                            bank.readers.append(evac(t, g, bank.t[:, :], got))
                    slot.readers.append(got)
                    mid.readers.append(got)

                def v_evac(t, f0, ps, got):
                    for c in range(4):
                        for j in range(2):
                            q = f0 // 256 + j
                            tok = p.V(self.cp, vrow[q * CH:(q + 1) * CH, 4 * t + c, :, :].rearrange("p h d -> p (h d)"),
                                      ps[c * CH:(c + 1) * CH, j * 256:(j + 1) * 256], after=[got])
                    return tok

                rkv = A["rw_rkv_2"][0]
                mix_r, mix_k = mixed(0), mixed(2)
                self.to_cols(mix_r[0].t, D, rkv[0], self.copier(r_), ready=[mix_r[1]])
                mix_r[0].readers.append(p.last["tensor"])
                mix_v = mixed(3)
                self.to_cols(mix_k[0].t, D, rkv[1], self.copier(k_), ready=[mix_k[1]])
                mix_k[0].readers.append(p.last["tensor"])
                mix_w = mixed(1)
                bc = lambda at: par[:, at:at + 8].unsqueeze(2).to_broadcast([P, KT, T])
                p.V(self.tt, kk[:, :, :], k_[:, :, :], bc(KK), ALU.mult)
                self.to_rows(mix_v[0].t, D, rkv[2], v_evac, ready=[mix_v[1]])
                mix_v[0].readers.append(p.last["tensor"])
                mix_a = mixed(4)
                w_done = lora_cols(mix_w, A["rw_w1_2"][0], A["rw_w2_2"][0], 64, ACT.Tanh,
                                   lambda f, ps, got: p.S(w_[:, f, :], ps, ACT.Sigmoid, bias=par[:, W0 + f:W0 + f + 1], after=[got]))
                mix_g = mixed(5)
                a_done = lora_cols(mix_a, A["rw_a1_2"][0], A["rw_a2_2"][0], 64, ACT.Identity,
                                   lambda f, ps, got: p.S(a_[:, f, :], ps, ACT.Sigmoid, bias=par[:, A0 + f:A0 + f + 1], after=[got]))
                cum, work = xx, hp[:, :, 1:T + 1]
                p.V(self.ts, w_[:, :, :], w_[:, :, :], -float(np.exp(-0.5)), None, ALU.mult, after=[w_done])
                for f in range(KT):
                    cu = p.V(v.tensor_tensor_scan, cum[:, f, :], self.const("restart"), w_[:, f, :], 0.0,
                             ALU.mult, ALU.add)
                d = p.V(self.tt, w_[:, :, :], cum[:, :, :], w_[:, :, :], ALU.subtract)
                p.V(self.ts, work, a_[:, :, :], -1.0, None, ALU.add, after=[a_done])
                p.V(self.tt, work, work, bc(KA), ALU.mult)
                k_done = p.V(self.stt, out=k_[:, :, :], in0=work, scalar=1.0, in1=k_[:, :, :], op0=ALU.add, op1=ALU.mult)
                lora_rows(mix_g, A["rw_g1_2"][0], A["rw_g2_2"][0], 160, ACT.Sigmoid,
                          lambda t, f0, ps, got: p.V(self.cp, gate[:, t, f0:f0 + 512], ps, after=[got]))
                sums = [None] * KT
                small, norms = (Ring([b.t[:, 0, :], b.t[:, 1, :]]) for b in mids.buffers)
                for ring, b in zip((small, norms), mids.buffers):
                    for half in ring.buffers:
                        half.readers = list(b.readers)

                def squares(f):
                    b, bank = small.next(), p.banks.next()
                    sq = p.V(self.tt, b.t, kk[:, f, :], kk[:, f, :], ALU.mult, after=b.free())
                    got = p.product(bank, bank.t[:, 0:T], [(self.const("halves"), b.t)], after=[sq])
                    b.readers.append(got)
                    n = norms.next()
                    sums[f] = n, p.S(n.t, bank.t[:, 0:T], ACT.Sqrt, after=[got, *n.free()])
                    bank.readers.append(sums[f][1])

                def normed(f):
                    n, root = sums[f]
                    p.V(self.ts, n.t, n.t, 1e-12, None, ALU.max, after=[root])
                    p.V(v.reciprocal, n.t, n.t)
                    n.readers.append(p.V(self.tt, kk[:, f, :], kk[:, f, :], n.t, ALU.mult))
                pipeline(KT, [squares, normed])
                chunks = lambda a: a.rearrange("p k (c t) -> p k c t", t=CH)
                e1 = p.S(work, cum[:, :, :], ACT.Exp, after=[cu, k_done])
                e2 = p.S(w_[:, :, :], w_[:, :, :], ACT.Exp, after=[d])
                e3 = p.S(cum[:, :, :], cum[:, :, :], ACT.Exp, scale=-1.0)
                p.V(self.tt, a_[:, :, :], a_[:, :, :], kk[:, :, :], ALU.mult)
                p.V(self.cp, wend[:, :, :], chunks(work)[:, :, :, CH - 1], after=[e1])
                for f in range(KT):
                    p.V(self.tt, ar[:, f, :, 1, :], chunks(r_[:, :, :])[:, f, :, :], chunks(work)[:, f, :, :], ALU.mult,
                        after=mixes.buffers[f // 4].free())
                p.V(self.tt, prod[:, :, :], r_[:, :, :], k_[:, :, :], ALU.mult)
                p.V(self.tt, prod[:, :, :], prod[:, :, :], bc(RK), ALU.mult)
                for f in range(KT):
                    p.V(self.stt, out=ar[:, f, :, 0, :], in0=chunks(w_[:, :, :])[:, f, :, :], scalar=-1.0,
                        in1=chunks(kk[:, :, :])[:, f, :, :], op0=ALU.mult, op1=ALU.mult, after=[e2])
                p.V(self.tt, bh[:, :, :], a_[:, :, :], cum[:, :, :], ALU.mult, after=[e3])
                p.V(self.tt, kh[:, :, :], k_[:, :, :], cum[:, :, :], ALU.mult)
                p.barrier()
            yv = kh[:, :, :].rearrange("p c (h d) -> p c h d", d=HD)
            self.wkv(ar, bh, kh, vrow, wend, prod, yv)
            p.barrier()
            yr = self.sb(top, "y_rows", [P, TT, D])
            moved = []
            for q in range(4):
                for c in range(4):
                    out = yr[c * CH:(c + 1) * CH, :, q * 256:(q + 1) * 256]
                    in_ = yv[q * CH:(q + 1) * CH, c:NCH:4, :, :].rearrange("s c h d -> s c (h d)")
                    moved.append(p.V(self.cp, out, in_) if c % 2 else p.S(out, in_, ACT.Copy))
            m = p.V(self.tt, yr[:, :, :], yr[:, :, :], gate[:, :, :], ALU.mult, after=moved)
            yT = ar[:, :, :, :, :].rearrange("p k c a t -> p k (c a t)")
            ready = self.turned(yr, yT, after=[m])
            self.to_rows(yT, D, A["rw_wo_2"][0],
                         lambda t, f0, ps, got: p.V(self.cp, y_out[:, t, f0:f0 + 512], ps, after=[got]), ready=[ready])
            p.barrier()

    def wkv(self, ar, bh, kh, vrow, wend, prod, yv):
        p, nc, A, v = self.p, self.nc, self.A, self.nc.vector
        ident = self.const("ident")
        tri = self.const("tri")
        with ExitStack() as tmp:
            in_turn = [4 * q + i for i in range(4) for q in range(4)]
            pairs_in_turn = [2 * q + i for i in range(2) for q in range(4)]
            bar = self.sb(tmp, "b_ar", [P, NCH, 4, 2, CH])
            kar = self.sb(tmp, "k_ar", [P, NCH, 4, 2, CH])
            brow = self.sb(tmp, "b_chunk_rows", [P, NCH, 4, HD])
            krow = self.sb(tmp, "k_chunk_rows", [P, NCH, 4, HD])
            bonus = self.sb(tmp, "bonus", [P, NCH, 4])
            gn = self.sb(tmp, "group_norm", [P, 2, 4, HD])
            for q in range(4):
                part = slice(q * CH, (q + 1) * CH)
                for i, name in enumerate(("rw_gn_g_2", "rw_gn_b_2")):
                    p.dma(gn[part, i, :, :].rearrange("s h d -> s (h d)"),
                          A[name][0, q * 256:(q + 1) * 256].partition_broadcast(CH))
            def score_products(src):
                banks = []
                for c2 in range(NCH // 2):
                    bank = p.banks.next()
                    for b, ci, hh in [(b, ci, hh) for b in range(2) for ci in range(2) for hh in pairs_in_turn]:
                            c, h = 2 * c2 + ci, 2 * hh + b
                            order = [got] if b and not (ci or hh) else []
                            q, i, half, pair = h // 4, h % 4, slice(HD * (h % 2), HD * (h % 2) + HD), h // 2
                            col = (ci * 4 + i) * 64
                            got = p.product(bank, bank.t[q * CH:(q + 1) * CH, col:col + 64],
                                            [(src[half, pair, c * CH:(c + 1) * CH],
                                              ar[half, pair, c, :, :].rearrange("p a t -> p (a t)"))],
                                            after=order, tile_position=(HD * (h % 2), q * CH))
                    banks.append((bank, got))
                return banks

            def score_copies(banks, dst):
                for c2, (bank, got) in enumerate(banks):
                    mask = tri.unsqueeze(1).to_broadcast([P, 8, 64])
                    out = dst[:, 2 * c2:2 * c2 + 2, :, :, :].rearrange("p c h a t -> p (c h) (a t)")
                    bank.readers.append(p.V(self.tt, out, bank.t[:, :].rearrange("p (g n) -> p g n", n=64), mask,
                                            ALU.mult, after=[got]))

            bank = p.banks.next()
            for c in range(NCH):
                for pair in pairs_in_turn:
                    q, col = pair // 2, c * 4 + 2 * (pair % 2)
                    got = p.product(bank, bank.t[q * CH:(q + 1) * CH, col:col + 2],
                                    [(prod[:, pair, c * CH:(c + 1) * CH], self.const("half2"))],
                                    tile_position=(0, q * CH))
            bonus_read = got
            bank.readers.append(p.V(self.cp, bonus[:, :, :].rearrange("p c h -> p (c h)"), bank.t[:, 0:32], after=[got]))
            b_scores = score_products(bh)
            score_copies(b_scores, bar)
            k_scores = score_products(kh)
            square = lambda a, i: a[:, 4 * i:4 * i + 4, :].rearrange("p k (a b) -> p (k a) b", b=CH)
            area, area2 = (a.rearrange("p c h d -> p (c h d)").rearrange("p (k t) -> p k t", t=T) for a in (brow, krow))
            L, flat, inv, zs = square(area, 0), square(area, 1), square(area2, 0), square(prod, 0)
            work = area2[:, 4:8, :].rearrange("p k t -> p (k t)")
            pairs = lambda a: a.rearrange("p t n -> p (t n)")
            p.V(self.cp, flat, bar[:, :, :, 0, :].rearrange("p c h t -> p t (c h)"))
            p.V(v.transpose, pairs(L), pairs(flat))
            p.V(v.memset, inv, 0.0)
            p.V(v.memset, pairs(inv)[:, 0:CH * CH:CH + 1], 1.0)
            BL = 8
            step = BL * (CH + 1)

            def on_diagonal(a):
                a = a.rearrange("p k t -> p (k t)")[:, 0:CH // BL * step].rearrange("p (b x) -> p b x", x=step)
                return a[:, :, 0:BL * CH].rearrange("p b (r s) -> p b r s", s=CH)[:, :, :, 0:BL]
            Ld, invd = on_diagonal(area), on_diagonal(area2)
            for t in range(1, BL):
                w = work[:, 0:CH // BL * t * t].rearrange("p (b u s) -> p b u s", u=t, s=t)
                p.V(self.tt, w, invd[:, :, 0:t, 0:t].rearrange("p b s u -> p b u s"),
                    Ld[:, :, t:t + 1, 0:t].to_broadcast([P, CH // BL, t, t]), ALU.mult)
                p.V(v.tensor_reduce, invd[:, :, t, 0:t], w, AX.X, ALU.add)

            def multiply(out, a, b, n):
                rows = min(n, KT * T // 2 // (n * n))
                for i in range(0, n, rows):
                    w = work[:, 0:rows * n * n].rearrange("p (i j k) -> p i j k", j=n, k=n)
                    p.V(self.tt, w, a[:, i:i + rows, :].unsqueeze(2).to_broadcast([P, rows, n, n]),
                        b.rearrange("p k j -> p j k").unsqueeze(1).to_broadcast([P, rows, n, n]), ALU.mult)
                    p.V(v.tensor_reduce, out[:, i:i + rows, :], w, AX.X, ALU.add)
            for n in (BL, 2 * BL):
                for at in range(0, CH, 2 * n):
                    up, low = slice(at, at + n), slice(at + n, at + 2 * n)
                    mid = flat[:, 0:n, 0:n]
                    multiply(mid, L[:, low, up], inv[:, up, up], n)
                    multiply(inv[:, low, up], inv[:, low, low], mid, n)
            solved = p.V(v.transpose, pairs(zs), pairs(inv), after=[bonus_read])
            score_copies(k_scores, kar)
            for src, dst in ((bh, brow), (kh, krow)):
                for c2 in range(NCH // 2):
                    bank = p.banks.next()
                    for ci in range(2):
                        c = 2 * c2 + ci
                        for pair in pairs_in_turn:
                            q = pair // 2
                            col = (ci * 4 + 2 * (pair % 2)) * HD
                            got = p.product(bank, bank.t[q * CH:(q + 1) * CH, col:col + P],
                                            [(src[:, pair, c * CH:(c + 1) * CH], ident)],
                                            tile_position=(0, q * CH))
                    out = dst[:, 2 * c2:2 * c2 + 2, :, :].rearrange("p c h d -> p (c h d)")
                    bank.readers.append(p.S(out, bank.t[:, :], ACT.Copy, after=[got, solved]))
            state = self.sb(tmp, "state", [P, KT, HD])
            xs = prod[:, 4, :].rearrange("p (h d) -> p h d", d=HD)
            sa = prod[:, 5, :].rearrange("p (h d) -> p h d", d=HD)
            ready = p.V(v.memset, state[:, :, :], 0.0)
            head = lambda h: (h // 4, h % 4, h % 2, h // 2)
            p.barrier()

            def add_products(bank, part, after, first=False):
                groups, operands = part
                after = [*bank.free(), *after]
                for group in groups:
                    for h in group:
                        q, i, b, pair = head(h)
                        l, r, row = operands(h)
                        got = p.put("tensor", nc.tensor.matmul, bank.t[q * CH:(q + 1) * CH, i * HD:(i + 1) * HD],
                                    l, r, start=first and h % 4 == 0, stop=False, skip_group_check=True,
                                    tile_position=(row, q * CH), after=after, chain=False, signal=h == group[-1])
                        after = ()
                    after = [got]
                return got

            def add_to_state(bank, rows, cols, after, first=False):
                for q in range(4):
                    for i in range(4):
                        h = 4 * q + i
                        g, half = slice(q * CH, (q + 1) * CH), slice(HD * (h % 2), HD * (h % 2) + HD)
                        got = p.put("tensor", nc.tensor.matmul, bank.t[half, h // 2 * HD:(h // 2 + 1) * HD],
                                    rows[g, i, :], cols[g, i, :], start=first and h < 2, stop=False,
                                    skip_group_check=True, tile_position=(q * CH, HD * (h % 2)),
                                    after=after, chain=False, signal=i == 3)
                        after = ()
                    after = [got]
                return got

            halves = [[h for h in in_turn if h % 2 == b] for b in range(2)]
            every = [in_turn]

            def from_state(c, n):
                def operands(h):
                    q, i, b, pair = head(h)
                    half = slice(HD * b, HD * b + HD)
                    return ar[half, pair, c, n, :], state[half, pair, :], HD * b
                return halves, operands

            def from_rows(scores, rows, c, n):
                def operands(h):
                    q, i, b, pair = head(h)
                    g = slice(q * CH, (q + 1) * CH)
                    return scores[g, c, i, n, :], rows[g, i, :], q * CH
                return every, operands

            stats = prod[:, 6, :].rearrange("p (c n h) -> p c n h", n=2, h=16)
            squares = prod[:, 7, :].rearrange("p (h d) -> p h d", d=HD)
            wide = lambda a: a.unsqueeze(2).to_broadcast([P, 4, HD])

            def norm(c):
                y, s1, s2 = yv[:, c, :, :], stats[:, c, 0, 0:4], stats[:, c, 1, 0:4]
                p.V(v.tensor_reduce, s1, y, AX.X, ALU.add)
                p.V(self.ts, s1, s1, 1.0 / HD, None, ALU.mult)
                p.V(self.tt, y, y, wide(s1), ALU.subtract)
                p.V(self.tt, squares, y, y, ALU.mult)
                p.V(v.tensor_reduce, s2, squares, AX.X, ALU.add)
                r = self.rstd(s2, HD, 64e-5, tmp)
                p.V(self.tt, squares, vrow[:, c, :, :], wide(bonus[:, c, :]), ALU.mult)
                p.V(self.tt, y, y, wide(s2), ALU.mult, after=[r])
                p.V(self.tt, y, y, gn[:, 0, :, :], ALU.mult)
                p.V(self.tt, y, y, gn[:, 1, :, :], ALU.add)
                p.V(self.tt, y, y, squares, ALU.add)

            flat_heads = lambda a: a.rearrange("p h d -> p (h d)")
            v_rows = lambda c: vrow[:, c, :, :]
            x_bank = p.banks.next()
            x_from_v = add_products(x_bank, from_rows(kar, v_rows(0), 0, 0), [], first=True)
            for c in range(NCH):
                last = c == NCH - 1
                got = add_products(x_bank, from_state(c, 0), [ready, x_from_v])
                x_ready = p.V(self.cp, flat_heads(xs), x_bank.t[:, 0:256], after=[got])
                x_bank.readers.append(x_ready)
                if c:
                    norm(c - 1)
                y_bank = p.banks.next()
                got = add_products(y_bank, from_rows(kar, v_rows(c), c, 1), [], first=True)
                y_got = add_products(y_bank, from_state(c, 1), [got])
                if not last:
                    s_bank = p.banks.next()
                    s_got = add_to_state(s_bank, krow[:, c, :, :], v_rows(c), s_bank.free(), first=True)
                bank = p.banks.next()
                for h in in_turn:
                    q, i, b, pair = head(h)
                    g = slice(q * CH, (q + 1) * CH)
                    got = p.product(bank, bank.t[g, i * HD:(i + 1) * HD], [(zs[g, :, c * 4 + i], xs[g, i, :])],
                                    after=[x_ready], tile_position=(q * CH, q * CH))
                sa_ready = p.V(self.cp, flat_heads(sa), bank.t[:, 0:256], after=[got])
                bank.readers.append(sa_ready)
                if not last:
                    x_bank = p.banks.next()
                    x_from_v = add_products(x_bank, from_rows(kar, v_rows(c + 1), c + 1, 0), [], first=True)
                    got = add_to_state(s_bank, brow[:, c, :, :], sa, [sa_ready, s_got])
                    add = p.V(self.tt, state[:, :, :], state[:, :, :],
                              s_bank.t[:, :].rearrange("p (k d) -> p k d", d=HD), ALU.add, after=[got])
                    s_bank.readers.append(add)
                    ready = p.V(self.tt, state[:, :, :], state[:, :, :],
                                wend[:, :, c].unsqueeze(2).to_broadcast([P, KT, HD]), ALU.mult)
                got = add_products(y_bank, from_rows(bar, sa, c, 1), [sa_ready, y_got])
                y_bank.readers.append(p.V(self.cp, flat_heads(yv[:, c, :, :]), y_bank.t[:, 0:256], after=[got]))
            norm(NCH - 1)
            p.barrier()

    def shared_kv(self, scale, shift):
        p, nc, A, v = self.p, self.nc, self.A, self.nc.vector
        with ExitStack() as tmp:
            hk = self.sb(tmp, "kv_in_cols", [P, KT, T])
            k = self.sb(tmp, "fox_k_rows", [P, TT, N_HEADS, HD])
            gain = self.sb(tmp, "k_gain", [P, HD])
            wf = self.sb(tmp, "forget_w", [P, KT, N_HEADS])
            fb = self.sb(tmp, "forget_b", [N_HEADS, 1])
            w = A["kv_w_2"]
            c = [p.dma(gain[:, :], A["kv_knorm_2"].partition_broadcast(P)),
                 p.dma(wf[:, :, :], w[:, 2 * D:2 * D + N_HEADS].rearrange("(k p) n -> p k n", p=P)),
                 p.dma(fb[:, :], A["kv_fb_2"].rearrange("(n a) -> n a", a=1))]
            ready = self.turned(self.x, hk, 0, scale, shift)
            flat = lambda a: a.rearrange("p h d -> p (h d)")
            self.to_rows(hk, D, w[:, 0:D], lambda t, f0, ps, got: p.V(self.cp, flat(k[:, t, :, :])[:, f0:f0 + 512], ps, after=[got]),
                         ready=[ready])
            self.to_rows(hk, D, w[:, D:2 * D],
                         lambda t, f0, ps, got: p.V(self.cp, flat(self.val[:, t, :, :])[:, f0:f0 + 512], ps, after=[got]))
            bank = p.banks.next()
            got = p.product(bank, bank.t[0:N_HEADS, 0:T], [(wf[:, k_, :], hk[:, k_, :]) for k_ in range(KT)], after=c)
            f, e, g = (self.sb(tmp, n, [N_HEADS, T]) for n in ("forget", "forget_exp", "forget_abs"))
            bank.readers.append(p.V(self.ts, f[:, :], bank.t[0:N_HEADS, 0:T], fb[:, 0:1], None, ALU.add, after=[got, *c]))
            a = p.V(self.stt, out=g[:, :], in0=f[:, :], scalar=-1.0, in1=f[:, :], op0=ALU.mult, op1=ALU.max)
            ex = p.S(e[:, :], g[:, :], ACT.Exp, scale=-1.0, after=[a])
            a = p.V(self.ts, e[:, :], e[:, :], 1.0, None, ALU.add, after=[ex])
            ln = p.S(e[:, :], e[:, :], ACT.Ln, after=[a])
            p.V(self.stt, out=f[:, :], in0=f[:, :], scalar=0.0, in1=e[:, :], op0=ALU.min, op1=ALU.subtract, after=[ln])
            p.V(v.tensor_tensor_scan, g[:, :], self.ones[0:N_HEADS, 0:1].to_broadcast([N_HEADS, T]), f[:, :], 0.0,
                ALU.mult, ALU.add)
            n = p.V(self.ts, e[:, :], g[:, :], -1.0, None, ALU.mult)
            p.dma(self.f_dram[0], g[:, :], after=[n])
            p.dma(self.f_dram[1], e[:, :], after=[n])
            for t in range(TT):
                self.head_rms(k[:, t, :, :], N_HEADS, gain[:, :], tmp)
            self.turned(k[:, :, :, :].rearrange("p t h d -> p t (h d)"), self.kT, after=[p.last["vector"]])
            p.barrier()

    def fox(self, y_out, scale, shift):
        p, nc, A, v = self.p, self.nc, self.A, self.nc.vector
        with ExitStack() as tmp:
            hT = self.sb(tmp, "fox_in_cols", [P, KT, T])
            q = self.sb(tmp, "fox_q_rows", [P, TT, N_HEADS, HD])
            gt = self.sb(tmp, "fox_gate_rows", [P, TT, D])
            gain = self.sb(tmp, "q_gain", [P, HD])
            came = p.dma(gain[:, :], A["fx_qnorm_2"][0].partition_broadcast(P))
            fq = self.sb(tmp, "forget_q", [2, N_HEADS, T])
            fk = self.sb(tmp, "forget_k", [2, N_HEADS, T])
            p.V(v.memset, fq[:, :, :], 1.0)
            m = p.V(v.memset, fk[:, :, :], 1.0)
            p.dma(fq[0:1, :, :], self.f_dram[0:1], after=[m])
            p.dma(fk[1:2, :, :], self.f_dram[1:2], after=[m])
            ready = self.turned(self.x, hT, 0, scale, shift)
            flat = lambda a: a.rearrange("p h d -> p (h d)")
            w = A["fx_wqg_2"][0]
            self.to_rows(hT, D, w[:, 0:D], lambda t, f0, ps, got: p.V(self.cp, flat(q[:, t, :, :])[:, f0:f0 + 512], ps, after=[got]),
                         ready=[ready])
            self.to_rows(hT, D, w[:, D:2 * D],
                         lambda t, f0, ps, got: p.S(gt[:, t, f0:f0 + 512], ps, ACT.Sigmoid, after=[got]))
            with ExitStack() as t2:
                p.wait("vector", [came])
                for t in range(TT):
                    self.head_rms(q[:, t, :, :], N_HEADS, gain[:, :], t2)
                p.V(self.ts, q[:, :, :, :], q[:, :, :, :], HD ** -0.5, None, ALU.mult)
                p.barrier()
            qT = hT
            self.turned(q[:, :, :, :].rearrange("p t h d -> p t (h d)"), qT)
            p.barrier()
            y = q[:, :, :, :].rearrange("p t h d -> p t (h d)")
            items = []
            for h in range(N_HEADS):
                half = slice(HD * (h % 2), HD * (h % 2) + HD)
                for t in range(TT):
                    n = (t + 1) * P
                    items.append(dict(q=qT[half, h // 2, t * P:(t + 1) * P], keys=self.kT[half, h // 2, 0:n], n=n,
                                      extra=[(slice(0, n), fq[:, h, t * P:(t + 1) * P], fk[:, h, 0:n]),
                                             (slice(n - P, n), self.const("ident"), self.const("causal"))],
                                      values=lambda k, h=h: self.val[:, k, h, :],
                                      out=y[:, t, h * HD:(h + 1) * HD], ready=[]))
            self.attention(items, 1.0)
            for t in range(TT):
                m = p.V(self.tt, y[:, t, :], y[:, t, :], gt[:, t, :], ALU.mult)
            oT = hT
            ready = self.turned(y, oT, after=[m])
            self.to_rows(oT, D, A["fx_wo_2"][0],
                         lambda t, f0, ps, got: p.V(self.cp, y_out[:, t, f0:f0 + 512], ps, after=[got]), ready=[ready])
            p.barrier()


def two_blocks(nc, inputs, consts, out):
    with ExitStack() as stack:
        m = Model(nc, stack, inputs, consts, out)
        m.first_block()
        m.second_block()
        m.p.wait("gpsimd", m.p.transfers(aside=True))
        m.p.emit(stack.enter_context(nc.Block()))


USED = ["x", "c", "ctx", "c_ctx", "w_mod", "b_mod", "norm1_g", "norm2_g", "w_in", "q_norm_g", "k_norm_g", "na_rpb",
        "conv_w", "conv_b", "conv_norm_g", "w_branch", "w_out", "w_router", "router_bias", "w_expert_gu",
        "w_expert_down", "final_norm_g", "c_2", "ada_w_2", "ada_b_2", "ln_g_2", "ln_b_2", "rw_mu_2", "rw_rkv_2",
        "rw_w0_2", "rw_w1_2", "rw_w2_2", "rw_a0_2", "rw_a1_2", "rw_a2_2", "rw_g1_2", "rw_g2_2", "rw_kk_2", "rw_ka_2",
        "rw_rk_2", "rw_gn_g_2", "rw_gn_b_2", "rw_wo_2", "kv_ada_w_2", "kv_ada_b_2", "kv_w_2", "kv_fb_2", "kv_knorm_2",
        "fx_wqg_2", "fx_qnorm_2", "fx_wo_2", "moe_wgrp_2", "moe_bgrp_2", "moe_wexp_2", "moe_bexp_2", "moe_wgate_2",
        "moe_wup_2", "moe_wdown_2"]


def kernel(**inputs):
    import concourse.bacc as bacc
    from concourse.bass_utils import run_bass_kernel_spmd

    nc = bacc.Bacc("TRN2", target_bir_lowering=False, num_devices=1)
    arrays, aps = {}, {}
    for name in USED:
        a = np.ascontiguousarray(inputs[name])
        arrays[f"in_{name}"] = a
        aps[name] = nc.dram_tensor(f"in_{name}", a.shape, F32, kind="ExternalInput").ap()
    arrays["in_constants"] = shape_constants()
    consts = nc.dram_tensor("in_constants", (P, CONST_WIDTH), F32, kind="ExternalInput").ap()
    out = nc.dram_tensor("out", (1, T, D), F32, kind="ExternalOutput").ap()
    two_blocks(nc, aps, consts, out)
    r = run_bass_kernel_spmd(nc, [arrays], core_ids=[0])
    return r.results[0]["out"]
```
